# Optimizing a Trainium2 kernel written in Bass

```python
import math
import jax
import jax.numpy as jnp
from jax import lax
import numpy as np

D_MODEL = 1024
BATCH = 1
SEQ = 1024
DEPTH = 1
DEC_BATCH = 8
DEC_SEQ = 8
PAST_LEN = 256
PAGE_SIZE = 128

POOL_WIDTH = D_MODEL // 4
SGU_WIDTH = D_MODEL // 4
ATT_WIDTH = D_MODEL // 2
MIX_WIDTH = POOL_WIDTH + SGU_WIDTH + ATT_WIDTH

POOL_WINDOWS = (2, 4, 8, 16)
POOL_GROUPS = len(POOL_WINDOWS)
POOL_GROUP_DIM = POOL_WIDTH // POOL_GROUPS
POOL_WMAX = max(POOL_WINDOWS)
POOL_BUF = POOL_WMAX - 1

SGU_GROUPS = 4
SGU_GROUP_DIM = SGU_WIDTH // SGU_GROUPS
SGU_CHUNK = 128

N_HEADS = 8
HEAD_DIM = ATT_WIDTH // N_HEADS
N_KV = 2
REP = N_HEADS // N_KV
N_BRANCH = 3
CMP_BLOCK = 32
CMP_HIDDEN = 2 * HEAD_DIM
SEL_BLOCK = 64
CMP_PER_SEL = SEL_BLOCK // CMP_BLOCK
N_SEL = 16
WINDOW = 512
Q_BLOCK = 128
FORCED_SCORE = 1e4

IN_WIDTH = POOL_WIDTH + 2 * SGU_WIDTH + ATT_WIDTH + N_BRANCH * 2 * N_KV * HEAD_DIM + N_HEADS * N_BRANCH

N_BUCKETS = 32
REL_MAX_DIST = 128

N_EXPERTS = 16
N_GROUPS = 4
EXPERTS_PER_GROUP = N_EXPERTS // N_GROUPS
TOP_K = 2
D_EXPERT = 512
MOE_BLOCK = 128

ALPHA = (2 * DEPTH) ** 0.25
BETA = (8 * DEPTH) ** -0.25
LN_EPS = 1e-5
NEG = -1e30

kernel_name = 'hybrid_pool_sgu_nsa_moe_decoder_step'

def layer_norm(x, g, b):
    xf = x.astype(jnp.float32)
    mu = xf.mean(-1, keepdims=True)
    var = jnp.mean(jnp.square(xf - mu), -1, keepdims=True)
    return ((xf - mu) * lax.rsqrt(var + LN_EPS) * g.astype(jnp.float32) + b.astype(jnp.float32)).astype(x.dtype)

def rel_bucket(dist):
    n = jnp.maximum(dist, 0)
    max_exact = N_BUCKETS // 2
    nf = jnp.maximum(n, 1).astype(jnp.float32)
    large = max_exact + (jnp.log(nf / max_exact) / math.log(REL_MAX_DIST / max_exact) * (N_BUCKETS - max_exact)).astype(jnp.int32)
    large = jnp.minimum(large, N_BUCKETS - 1)
    return jnp.where(n < max_exact, n, large)

def masked_softmax(s, mask):
    s = jnp.where(mask, s.astype(jnp.float32), NEG)
    p = jnp.where(mask, jnp.exp(s - s.max(-1, keepdims=True)), 0.0)
    return p / jnp.maximum(p.sum(-1, keepdims=True), 1e-30)

def split_proj(z):
    B, T = z.shape[:2]
    cuts = [POOL_WIDTH, POOL_WIDTH + SGU_WIDTH, POOL_WIDTH + 2 * SGU_WIDTH,
            POOL_WIDTH + 2 * SGU_WIDTH + ATT_WIDTH,
            POOL_WIDTH + 2 * SGU_WIDTH + ATT_WIDTH + N_BRANCH * 2 * N_KV * HEAD_DIM]
    p, u, v, q, kv, g = jnp.split(z, cuts, axis=-1)
    q = q.reshape(B, T, N_KV, REP, HEAD_DIM)
    kv = kv.reshape(B, T, N_BRANCH, 2, N_KV, HEAD_DIM)
    gates = jax.nn.sigmoid(g.astype(jnp.float32)).reshape(B, T, N_KV, REP, N_BRANCH).astype(z.dtype)
    return p, u, v, q, kv, gates

def pool_mix(p_ext, n_prev, pool_w, pool_scale):
    B, L, C = p_ext.shape
    T = L - n_prev
    pf = p_ext.astype(jnp.float32)
    cs = jnp.concatenate([jnp.zeros((B, POOL_WMAX + 1, C), jnp.float32), jnp.cumsum(pf, axis=1)], axis=1)
    hi0 = n_prev + 1 + POOL_WMAX
    row = n_prev + 1 + jnp.arange(T, dtype=jnp.int32)
    means = []
    for gi, w in enumerate(POOL_WINDOWS):
        c0, c1 = gi * POOL_GROUP_DIM, (gi + 1) * POOL_GROUP_DIM
        hi = cs[:, hi0:hi0 + T, c0:c1]
        lo = cs[:, hi0 - w:hi0 - w + T, c0:c1]
        cnt = jnp.minimum(w, row).astype(jnp.float32)
        means.append((hi - lo) / cnt[None, :, None])
    diff = jnp.concatenate(means, axis=-1) - pf[:, n_prev:]
    out = jnp.einsum('btgc,gcd->btgd', diff.reshape(B, T, POOL_GROUPS, POOL_GROUP_DIM), pool_w.astype(jnp.float32))
    return (out.reshape(B, T, POOL_WIDTH) * pool_scale.astype(jnp.float32)).astype(p_ext.dtype)

def sgu_mix(u, vn, sgu_w, sgu_b):
    B, T, _ = vn.shape
    C = min(T, SGU_CHUNK)
    n = T // C
    mask = jnp.tril(jnp.ones((C, C), bool))
    w = jnp.where(mask, sgu_w[:, :C, :C], 0.0).astype(vn.dtype)
    vc = vn.reshape(B, n, C, SGU_GROUPS, SGU_GROUP_DIM)
    mixed = jnp.einsum('gij,bnjgd->bnigd', w, vc) + sgu_b[:, :C].T[None, None, :, :, None]
    return u * mixed.reshape(B, T, SGU_WIDTH).astype(u.dtype)

def compress(raw, pe, w1, w2):
    B, S = raw.shape[:2]
    n = S // CMP_BLOCK
    x = raw.reshape(B, n, CMP_BLOCK, 2, N_KV, HEAD_DIM) + jnp.transpose(pe, (1, 0, 2))[:, :, None, :]
    x = jnp.transpose(x, (0, 1, 3, 4, 2, 5)).reshape(B, n, 2, N_KV, CMP_BLOCK * HEAD_DIM)
    hdn = jax.nn.gelu(jnp.einsum('bnsgf,sfh->bnsgh', x, w1))
    return jnp.einsum('bnsgh,shd->bnsgd', hdn, w2)

def to_sel_blocks(raw):
    B, S = raw.shape[:2]
    r = raw.reshape(B, S // SEL_BLOCK, SEL_BLOCK, 2, N_KV, HEAD_DIM)
    r = jnp.transpose(r, (3, 0, 4, 1, 2, 5))
    return r[0], r[1]

def nsa_core(q, q_pos, gates, kc, vc, ks_blk, vs_blk, kw, vw, kw_pos, rel_bias):
    B, Q = q.shape[:2]
    dt = q.dtype
    scale = HEAD_DIM ** -0.5
    tb = rel_bias.astype(jnp.float32).reshape(N_BUCKETS, N_KV, REP)
    n_cmp = kc.shape[1]
    c_end = (jnp.arange(n_cmp, dtype=jnp.int32) + 1) * CMP_BLOCK - 1
    dist_c = q_pos[:, None] - c_end[None, :]
    bias_c = jnp.transpose(tb[rel_bucket(dist_c)], (2, 3, 0, 1))
    s_c = jnp.einsum('bqgrd,bngd->bgrqn', q, kc).astype(jnp.float32) * scale + bias_c
    p_c = masked_softmax(s_c, dist_c >= 0)
    o_c = jnp.einsum('bgrqn,bngd->bqgrd', p_c.astype(dt), vc)
    n_blk = ks_blk.shape[2]
    imp = p_c.sum(axis=2).reshape(B, N_KV, Q, n_blk, CMP_PER_SEL).sum(-1)
    blk = jnp.arange(n_blk, dtype=jnp.int32)[None, :]
    cur = (q_pos // SEL_BLOCK)[:, None]
    forced = (blk == 0) | (blk == cur) | (blk == cur - 1)
    valid = blk * SEL_BLOCK <= q_pos[:, None]
    imp = jnp.where(forced, FORCED_SCORE, jnp.where(valid, imp, -1.0))
    _, sel = lax.top_k(imp, min(N_SEL, n_blk))
    b_i = jnp.arange(B)[:, None, None, None]
    g_i = jnp.arange(N_KV)[None, :, None, None]
    k_s = ks_blk[b_i, g_i, sel].reshape(B, N_KV, Q, -1, HEAD_DIM)
    v_s = vs_blk[b_i, g_i, sel].reshape(B, N_KV, Q, -1, HEAD_DIM)
    k_pos = (sel[..., None] * SEL_BLOCK + jnp.arange(SEL_BLOCK, dtype=jnp.int32)).reshape(B, N_KV, Q, -1)
    dist_s = q_pos[None, None, :, None] - k_pos
    bias_s = jnp.moveaxis(tb[rel_bucket(dist_s), g_i], -1, 2)
    s_s = jnp.einsum('bqgrd,bgqkd->bgrqk', q, k_s).astype(jnp.float32) * scale + bias_s
    p_s = masked_softmax(s_s, (dist_s >= 0)[:, :, None])
    o_s = jnp.einsum('bgrqk,bgqkd->bqgrd', p_s.astype(dt), v_s)
    dist_w = q_pos[:, None] - kw_pos[None, :]
    mask_w = (dist_w >= 0) & (dist_w < WINDOW) & (kw_pos[None, :] >= 0)
    bias_w = jnp.transpose(tb[rel_bucket(dist_w)], (2, 3, 0, 1))
    s_w = jnp.einsum('bqgrd,bkgd->bgrqk', q, kw).astype(jnp.float32) * scale + bias_w
    p_w = masked_softmax(s_w, mask_w)
    o_w = jnp.einsum('bgrqk,bkgd->bqgrd', p_w.astype(dt), vw)
    return gates[..., 0:1] * o_c + gates[..., 1:2] * o_s + gates[..., 2:3] * o_w

def nsa_prompt(q, kv, gates, lp, rel_bias):
    B, T = q.shape[:2]
    cmp_raw, sel_raw, win_raw = kv[:, :, 0], kv[:, :, 1], kv[:, :, 2]
    kvc = compress(cmp_raw, lp['cmp_pe'], lp['cmp_w1'], lp['cmp_w2'])
    kc, vc = kvc[:, :, 0], kvc[:, :, 1]
    ks_blk, vs_blk = to_sel_blocks(sel_raw)
    win_pad = jnp.pad(win_raw, ((0, 0), (WINDOW, 0), (0, 0), (0, 0), (0, 0)))

    def one_block(i):
        s = i * Q_BLOCK
        qb = lax.dynamic_slice_in_dim(q, s, Q_BLOCK, 1)
        gb = lax.dynamic_slice_in_dim(gates, s, Q_BLOCK, 1)
        wb = lax.dynamic_slice_in_dim(win_pad, s, WINDOW + Q_BLOCK, 1)
        q_pos = s + jnp.arange(Q_BLOCK, dtype=jnp.int32)
        kw_pos = s - WINDOW + jnp.arange(WINDOW + Q_BLOCK, dtype=jnp.int32)
        return nsa_core(qb, q_pos, gb, kc, vc, ks_blk, vs_blk, wb[:, :, 0], wb[:, :, 1], kw_pos, rel_bias)

    o = lax.map(one_block, jnp.arange(T // Q_BLOCK, dtype=jnp.int32))
    o = jnp.moveaxis(o, 0, 1).reshape(B, T, ATT_WIDTH)
    return o, cmp_raw, sel_raw, win_raw[:, T - min(WINDOW, T):]

def nsa_sample(q, kv, gates, cmp_past, sel_past, win_buf, past_len, lp, rel_bias):
    B, T = q.shape[:2]
    cmp_new, sel_new, win_new = kv[:, :, 0], kv[:, :, 1], kv[:, :, 2]
    s_tot = past_len + T
    s_pad = -(-s_tot // SEL_BLOCK) * SEL_BLOCK
    pad = ((0, 0), (0, s_pad - s_tot), (0, 0), (0, 0), (0, 0))
    cmp_full = jnp.pad(jnp.concatenate([cmp_past.astype(q.dtype), cmp_new], 1), pad)
    sel_full = jnp.pad(jnp.concatenate([sel_past.astype(q.dtype), sel_new], 1), pad)
    kvc = compress(cmp_full, lp['cmp_pe'], lp['cmp_w1'], lp['cmp_w2'])
    kc, vc = kvc[:, :, 0], kvc[:, :, 1]
    ks_blk, vs_blk = to_sel_blocks(sel_full)
    win_keys = jnp.concatenate([win_buf.astype(q.dtype), win_new], 1)
    n_buf = win_buf.shape[1]
    kw_pos = past_len - n_buf + jnp.arange(n_buf + T, dtype=jnp.int32)

    def one_tok(j):
        qj = lax.dynamic_slice_in_dim(q, j, 1, 1)
        gj = lax.dynamic_slice_in_dim(gates, j, 1, 1)
        q_pos = jnp.reshape(past_len + j, (1,))
        return nsa_core(qj, q_pos, gj, kc, vc, ks_blk, vs_blk, win_keys[:, :, 0], win_keys[:, :, 1], kw_pos, rel_bias)

    o = lax.map(one_tok, jnp.arange(T, dtype=jnp.int32))
    o = jnp.moveaxis(o, 0, 1).reshape(B, T, ATT_WIDTH)
    return o, cmp_new, sel_new, win_keys[:, T:]

def mix_prompt(h, lp, rel_bias):
    p, u, v, q, kv, gates = split_proj(h @ lp['w_in'])
    pool_out = pool_mix(p, 0, lp['pool_w'], lp['pool_scale'])
    vn = layer_norm(v, lp['sgu_ln_g'], lp['sgu_ln_b'])
    sgu_out = sgu_mix(u, vn, lp['sgu_w'], lp['sgu_b'])
    att_out, new_cmp, new_sel, new_win = nsa_prompt(q, kv, gates, lp, rel_bias)
    out = jnp.concatenate([pool_out, sgu_out, att_out], -1) @ lp['w_out']
    return out, (new_cmp, new_sel, new_win, p[:, p.shape[1] - POOL_BUF:])

def mix_sample(h, lp, rel_bias, cmp_past, sel_past, win_buf, pool_buf, past_len):
    p, u, v, q, kv, gates = split_proj(h @ lp['w_in'])
    p_ext = jnp.concatenate([pool_buf.astype(p.dtype), p], 1)
    pool_out = pool_mix(p_ext, pool_buf.shape[1], lp['pool_w'], lp['pool_scale'])
    vn = layer_norm(v, lp['sgu_ln_g'], lp['sgu_ln_b'])
    sgu_out = sgu_mix(u, vn, lp['sgu_w'], lp['sgu_b'])
    att_out, new_cmp, new_sel, new_win = nsa_sample(q, kv, gates, cmp_past, sel_past, win_buf, past_len, lp, rel_bias)
    out = jnp.concatenate([pool_out, sgu_out, att_out], -1) @ lp['w_out']
    return out, (new_cmp, new_sel, new_win, p_ext[:, p_ext.shape[1] - POOL_BUF:], vn)

def moe(h, router_w, router_b, w_gate, w_up, w_down):
    N, D = h.shape
    s = jax.nn.sigmoid(h.astype(jnp.float32) @ router_w.astype(jnp.float32))
    grp = (s + router_b.astype(jnp.float32)).reshape(N, N_GROUPS, EXPERTS_PER_GROUP)
    g_sel = jnp.argmax(lax.top_k(grp, 2)[0].sum(-1), axis=-1)
    in_grp = jnp.take_along_axis(grp, g_sel[:, None, None], axis=1)[:, 0]
    _, loc = lax.top_k(in_grp, TOP_K)
    e_idx = (g_sel[:, None] * EXPERTS_PER_GROUP + loc).astype(jnp.int32)
    w = jnp.take_along_axis(s, e_idx, axis=1)
    w = w / w.sum(-1, keepdims=True)
    A = N * TOP_K
    flat_e = e_idx.reshape(A)
    flat_tok = jnp.arange(A, dtype=jnp.int32) // TOP_K
    flat_w = w.reshape(A)
    order = jnp.argsort(flat_e)
    e_sorted = flat_e[order]
    counts = jnp.bincount(flat_e, length=N_EXPERTS)
    padded = (counts + MOE_BLOCK - 1) // MOE_BLOCK * MOE_BLOCK
    pad_end = jnp.cumsum(padded)
    pad_start = pad_end - padded
    start = jnp.cumsum(counts) - counts
    dest = pad_start[e_sorted] + jnp.arange(A, dtype=jnp.int32) - start[e_sorted]
    n_blocks = -(-(A + N_EXPERTS * (MOE_BLOCK - 1)) // MOE_BLOCK)
    P = n_blocks * MOE_BLOCK
    buf_tok = jnp.full((P,), N, jnp.int32).at[dest].set(flat_tok[order])
    buf_w = jnp.zeros((P,), jnp.float32).at[dest].set(flat_w[order])
    block_e = jnp.minimum(jnp.searchsorted(pad_end, jnp.arange(n_blocks) * MOE_BLOCK, side='right'), N_EXPERTS - 1)
    h_pad = jnp.concatenate([h, jnp.zeros((1, D), h.dtype)], 0)
    xb = h_pad[buf_tok].reshape(n_blocks, MOE_BLOCK, D)

    def expert_block(args):
        x_blk, e = args
        return (jax.nn.silu(x_blk @ w_gate[e]) * (x_blk @ w_up[e])) @ w_down[e]

    y = lax.map(expert_block, (xb, block_e)).reshape(P, D)
    out = jnp.zeros((N + 1, D), jnp.float32).at[buf_tok].add(y.astype(jnp.float32) * buf_w[:, None])
    return out[:N].astype(h.dtype)

def post_norm_layer(x, c, w_mod_l, b_mod_l, ln_g_l, ln_b_l, mix_fn, router_w, router_b, wg, wu, wd):
    B, T, D = x.shape
    m = (jax.nn.silu(c) @ w_mod_l + b_mod_l).reshape(B, 6, 1, D)
    sh1, sc1, g1, sh2, sc2, g2 = [m[:, i] for i in range(6)]
    mix_out, new_state = mix_fn(x * (1 + sc1) + sh1)
    x = layer_norm(ALPHA * x + (1 + g1) * mix_out, ln_g_l[0], ln_b_l[0])
    h2 = x * (1 + sc2) + sh2
    ff = moe(h2.reshape(B * T, D), router_w, router_b, wg, wu, wd).reshape(B, T, D)
    x = layer_norm(ALPHA * x + (1 + g2) * ff, ln_g_l[1], ln_b_l[1])
    return x, new_state

def setup_inputs(seed: int = 0) -> dict:
    key = jax.random.key(seed)
    k = jax.random.split(key, 32)
    f32 = jnp.float32
    n_pages = PAST_LEN // PAGE_SIZE
    n_used = DEC_BATCH * n_pages
    n_phys = n_used + max(1, n_used // 4)
    win_buf = min(WINDOW, PAST_LEN)

    def nrm(kk, shape, s=1.0):
        return s * jax.random.normal(kk, shape, f32)

    page_table = jax.random.permutation(k[0], n_phys)[:n_used].reshape(DEC_BATCH, n_pages).astype(jnp.int32)
    return {
        'x_prompt': nrm(k[1], (BATCH, SEQ, D_MODEL)),
        'x_sample': nrm(k[2], (DEC_BATCH, DEC_SEQ, D_MODEL)),
        'cache_cmp_kv': nrm(k[3], (DEPTH, n_phys, PAGE_SIZE, 2, N_KV, HEAD_DIM)),
        'cache_sel_kv': nrm(k[4], (DEPTH, n_phys, PAGE_SIZE, 2, N_KV, HEAD_DIM)),
        'state_win_kv': nrm(k[5], (DEPTH, DEC_BATCH, win_buf, 2, N_KV, HEAD_DIM)),
        'state_pool': nrm(k[6], (DEPTH, DEC_BATCH, POOL_BUF, POOL_WIDTH)),
        'page_table': page_table,
        'c_prompt': nrm(k[7], (BATCH, D_MODEL)),
        'c_sample': nrm(k[8], (DEC_BATCH, D_MODEL)),
        'w_in': nrm(k[9], (DEPTH, D_MODEL, IN_WIDTH), D_MODEL ** -0.5),
        'w_out': nrm(k[10], (DEPTH, MIX_WIDTH, D_MODEL), BETA * MIX_WIDTH ** -0.5),
        'pool_w': nrm(k[11], (DEPTH, POOL_GROUPS, POOL_GROUP_DIM, POOL_GROUP_DIM), POOL_GROUP_DIM ** -0.5),
        'pool_scale': 1.0 + nrm(k[12], (DEPTH, POOL_WIDTH), 0.1),
        'sgu_ln_g': 1.0 + nrm(k[13], (DEPTH, SGU_WIDTH), 0.1),
        'sgu_ln_b': nrm(k[14], (DEPTH, SGU_WIDTH), 0.02),
        'sgu_w': nrm(k[15], (DEPTH, SGU_GROUPS, SGU_CHUNK, SGU_CHUNK), SGU_CHUNK ** -0.5),
        'sgu_b': 1.0 + nrm(k[16], (DEPTH, SGU_GROUPS, SGU_CHUNK), 0.1),
        'cmp_pe': nrm(k[17], (DEPTH, 2, CMP_BLOCK, HEAD_DIM), 0.1),
        'cmp_w1': nrm(k[18], (DEPTH, 2, CMP_BLOCK * HEAD_DIM, CMP_HIDDEN), (CMP_BLOCK * HEAD_DIM) ** -0.5),
        'cmp_w2': nrm(k[19], (DEPTH, 2, CMP_HIDDEN, HEAD_DIM), CMP_HIDDEN ** -0.5),
        'rel_bias': nrm(k[20], (N_BUCKETS, N_HEADS), 0.5),
        'w_mod': nrm(k[21], (DEPTH, D_MODEL, 6 * D_MODEL), 0.2 * D_MODEL ** -0.5),
        'b_mod': nrm(k[22], (DEPTH, 6 * D_MODEL), 0.02),
        'ln_g': 1.0 + nrm(k[23], (DEPTH, 2, D_MODEL), 0.1),
        'ln_b': nrm(k[24], (DEPTH, 2, D_MODEL), 0.02),
        'router_w': nrm(k[25], (D_MODEL, N_EXPERTS), D_MODEL ** -0.5),
        'router_b': nrm(k[26], (N_EXPERTS,), 0.01),
        'moe_w_gate': nrm(k[27], (DEPTH, N_EXPERTS, D_MODEL, D_EXPERT), D_MODEL ** -0.5),
        'moe_w_up': nrm(k[28], (DEPTH, N_EXPERTS, D_MODEL, D_EXPERT), D_MODEL ** -0.5),
        'moe_w_down': nrm(k[29], (DEPTH, N_EXPERTS, D_EXPERT, D_MODEL), BETA * D_EXPERT ** -0.5),
    }

def reference(x_prompt, x_sample, cache_cmp_kv, cache_sel_kv, state_win_kv, state_pool, page_table,
              c_prompt, c_sample, w_in, w_out, pool_w, pool_scale, sgu_ln_g, sgu_ln_b, sgu_w, sgu_b,
              cmp_pe, cmp_w1, cmp_w2, rel_bias, w_mod, b_mod, ln_g, ln_b, router_w, router_b,
              moe_w_gate, moe_w_up, moe_w_down):
    n_dec, n_pages = page_table.shape
    past_len = n_pages * PAGE_SIZE
    xp, xs = x_prompt, x_sample
    cmp_p, cmp_s, sel_p, sel_s, win_p, win_s, pool_p, pool_s, sgu_s = [], [], [], [], [], [], [], [], []
    for l in range(DEPTH):
        lp = {'w_in': w_in[l], 'w_out': w_out[l], 'pool_w': pool_w[l], 'pool_scale': pool_scale[l],
              'sgu_ln_g': sgu_ln_g[l], 'sgu_ln_b': sgu_ln_b[l], 'sgu_w': sgu_w[l], 'sgu_b': sgu_b[l],
              'cmp_pe': cmp_pe[l], 'cmp_w1': cmp_w1[l], 'cmp_w2': cmp_w2[l]}
        xp, (nc, ns, nw, npool) = post_norm_layer(
            xp, c_prompt, w_mod[l], b_mod[l], ln_g[l], ln_b[l],
            lambda h: mix_prompt(h, lp, rel_bias),
            router_w, router_b, moe_w_gate[l], moe_w_up[l], moe_w_down[l])
        cmp_p.append(nc); sel_p.append(ns); win_p.append(nw); pool_p.append(npool)
        cmp_past = cache_cmp_kv[l][page_table].reshape(n_dec, past_len, 2, N_KV, HEAD_DIM)
        sel_past = cache_sel_kv[l][page_table].reshape(n_dec, past_len, 2, N_KV, HEAD_DIM)
        xs, (nc, ns, nw, npool, nv) = post_norm_layer(
            xs, c_sample, w_mod[l], b_mod[l], ln_g[l], ln_b[l],
            lambda h: mix_sample(h, lp, rel_bias, cmp_past, sel_past, state_win_kv[l], state_pool[l], past_len),
            router_w, router_b, moe_w_gate[l], moe_w_up[l], moe_w_down[l])
        cmp_s.append(nc); sel_s.append(ns); win_s.append(nw); pool_s.append(npool); sgu_s.append(nv)
    return (xp, xs,
            jnp.stack(cmp_p), jnp.stack(cmp_s),
            jnp.stack(sel_p), jnp.stack(sel_s),
            jnp.stack(win_p), jnp.stack(win_s),
            jnp.stack(pool_p), jnp.stack(pool_s),
            jnp.stack(sgu_s))


_drawn_inputs = setup_inputs


def setup_inputs(seed=0):
    import zlib

    import numpy as np

    out = dict(_drawn_inputs(seed))
    spreads = {}
    factors = {'sgu_ln_b': 2.937}
    for name, (base, spread) in spreads.items():
        noise = np.random.default_rng([zlib.crc32(name.encode()), seed]).standard_normal(out[name].shape)
        drawn = base * np.exp(spread * noise) if base else spread * noise
        out[name] = jnp.asarray(drawn.astype(out[name].dtype))
    for name, factor in factors.items():
        out[name] = (out[name] * factor).astype(out[name].dtype)
    return out
```

```python
import math
from contextlib import ExitStack

import numpy as np
import concourse.bass as bass
from concourse import mybir

F32, BF16, I32 = mybir.dt.float32, mybir.dt.bfloat16, mybir.dt.int32
ALU, ACT, AX = mybir.AluOpType, mybir.ActivationFunctionType, mybir.AxisListType

P = 128
D = 1024
KT = D // P
SEQ, NB, JS = 1024, 8, 8
NS = NB * JS
NP_TILES = SEQ // P
NT = NP_TILES + 1
TOK = SEQ + NS
PAST, PAGE = 256, 128
NPAGE = PAST // PAGE
PW = 256
WINDOWS = (2, 4, 8, 16)
PBUF = 15
HD, NKV, REP, NH = 64, 2, 4, 8
KVW = 2 * NKV * HD
Q0 = 3 * PW
KV0 = Q0 + NH * HD
G0 = KV0 + 3 * KVW
IN_W = G0 + 3 * NH
CB, NC_P, NC_S = 32, SEQ // 32, PAST // 32
WIN_TILES = 4
NBUCK = 32
TABW = 1152
NE, DE, MB = 16, 512, 128
ALPHA = 2.0 ** 0.25
EPS = 1e-5
NEG = -1e30
BIG = 1e30
MAX_SLOTS = (2 * TOK + NE * (MB - 1) + NE - 1) // MB
SCALE = HD ** -0.5

W_, MIX_ = 0, KT * IN_W
L_ = MIX_ + KT * TOK
QT_ = L_ + NH * D
KT_ = QT_ + 4 * TOK
VS_ = KT_ + 2 * TOK
KVR_ = VS_ + NT * 256
XH_ = KVR_ + 2 * 3 * KVW
S1_ = XH_ + 3 * D
CPH_ = S1_ + 2816
PER_ = CPH_ + 2304
END_ = PER_ + 640
ZR_ = MIX_ + 4 * TOK
WB_ = (L_, W_)
WB_LEN = 2 * KT * DE + (DE // P) * D
X1_ = L_ + WB_LEN


def tile_rows(i):
    return P if i < NP_TILES else NS


def bucket(dist):
    n = np.maximum(dist, 0)
    half = NBUCK // 2
    nf = np.maximum(n, 1).astype(np.float32)
    large = half + (np.log(nf / np.float32(half)) / np.float32(math.log(128 / half)) * np.float32(NBUCK - half)).astype(np.int32)
    return np.where(n < half, n, np.minimum(large, NBUCK - 1))


def constants():
    c = {}
    r = np.arange(P)
    ident = np.eye(P)
    c["ident"] = ident
    dist = 1023 - np.arange(TABW)
    oh = np.zeros((NBUCK + 1, TABW))
    ok = dist >= 0
    oh[bucket(dist)[ok], np.arange(TABW)[ok]] = 1
    oh[NBUCK, ~ok] = 1
    c["onehot"] = oh
    first, same, prev = (np.zeros((P, 4, P)) for _ in range(3))
    buf, new = np.zeros((P, 4, NS)), np.zeros((P, 4, NS))
    for g, w in enumerate(WINDOWS):
        for t in range(P):
            lo = t - w + 1
            for s in range(lo, t + 1):
                if s >= 0:
                    first[s, g, t] += 1 / min(w, t + 1)
                    same[s, g, t] += 1 / w
                else:
                    prev[P + s, g, t] += 1 / w
            first[t, g, t] -= 1
            same[t, g, t] -= 1
        for b in range(NB):
            for j in range(JS):
                for s in range(PBUF + j - w + 1, PBUF + j + 1):
                    if s < PBUF:
                        buf[b * PBUF + s, g, b * JS + j] += 1 / w
                    else:
                        new[b * JS + s - PBUF, g, b * JS + j] += 1 / w
                new[b * JS + j, g, b * JS + j] -= 1
    tril = (r[:, None] <= r[None, :]).astype(float)
    s = np.arange(P) % NS
    blk = np.zeros((P, NS))
    blk[:NS] = (s[:NS, None] // JS == s[None, :NS] // JS)
    rep = np.zeros((P, NS))
    rep[:JS] = np.arange(JS)[:, None] == np.arange(NS)[None, :] % JS
    c["cph1"] = np.concatenate([a.reshape(P, -1) for a in (first, same, prev, tril, buf, new, blk, rep)], 1)
    b4, rr, jj = r // 32, r % 32 // JS, r % JS
    selg = np.zeros((P, 2, P))
    for half in range(2):
        selg[(4 * half + b4) * JS + jj, half, r] = 1
    rowm = np.zeros((P, 2, NH, 3))
    for g in range(2):
        rowm[r, g, 4 * g + rr, :] = 1
    selr = np.zeros((P, 4, P))
    for q in range(4):
        selr[jj, q, r] = (rr == q)
    mine = np.zeros((P, 2, NB, JS))
    for half in range(2):
        mine[r, half, 4 * half + b4, :] = 1
    c["cph2"] = np.concatenate([a.reshape(P, -1) for a in (selg, rowm, selr, mine, (1 - mine) * NEG)], 1)
    c["cph3"] = np.where(r[None, :] <= r[:, None], NEG, 0.0)
    strict = (r[:, None] < r[None, :]).astype(float)
    cols = [strict, np.tile(NE - np.arange(NE), (P, 1)), np.tile(4 - np.arange(4), (P, 1)),
            np.tile(MB * np.arange(1, 9), (P, 1)),
            np.tile((np.arange(NE)[:, None] > np.arange(NE)[None, :]).reshape(1, -1), (P, 1)),
            np.tile(np.arange(MAX_SLOTS), (P, 1)), r[:, None] + P * np.arange(NT)[None, :]]
    c["cph4"] = np.concatenate(cols, 1)
    return {k: np.ascontiguousarray(v, np.float32) for k, v in c.items()}


CONST_SHAPES = {"ident": (P, P), "onehot": (NBUCK + 1, TABW), "cph1": (P, 12 * P + P + 4 * 2 * NS + 2 * NS),
                "cph2": (P, 2 * P + 48 + 4 * P + 4 * NS), "cph3": (P, P),
                "cph4": (P, P + NE + 4 + 8 + NE * NE + MAX_SLOTS + NT)}


class Chip:
    pass


def setup(nc, ctx, t):
    c = Chip()
    c.nc, c.t = nc, t
    c.arena = ctx.enter_context(nc.sbuf_tensor("arena", [P, END_], F32))
    c.psum = ctx.enter_context(nc.psum_tensor("psum", [P, 8 * 512], F32))
    c.sem = lambda name: ctx.enter_context(nc.semaphore(name))
    c.early = []

    def early_sem(name):
        c.early.append(nc.alloc_semaphore(name))
        return c.early[-1]

    c.early_sem = early_sem

    def view(off, *dims):
        n = 1
        for d in dims:
            n *= d
        a = c.arena[:, off:off + n]
        names = "abcd"[:len(dims)]
        if len(dims) == 1:
            return a
        lhs = " ".join(names)
        return a.rearrange(f"p ({lhs}) -> p {lhs}", **{k: d for k, d in zip(names, dims)})

    c.view = view
    c.bank = lambda b, n=512: c.psum[:, b * 512:b * 512 + n]
    c.ident = view(PER_, P)
    c.gates = view(PER_ + P, NT, 24)
    c.xw = view(PER_ + P + 216, NT, 2)
    c.misc = view(PER_ + P + 234, 270)
    c.page = ctx.enter_context(nc.sbuf_tensor("page", [1, NB * NPAGE], I32))
    c.dest_i = ctx.enter_context(nc.sbuf_tensor("dest_i", [P, NT, 2], I32))
    c.ids_i = ctx.enter_context(nc.sbuf_tensor("ids_i", [P, MAX_SLOTS + 1], I32))
    c.id_now = ctx.enter_context(nc.sbuf_tensor("id_now", [P, 1], I32))
    c.slot_e = ctx.enter_context(nc.sbuf_tensor("slot_e", [1, MAX_SLOTS], I32))
    c.start_e = ctx.enter_context(nc.sbuf_tensor("start_e", [1, NE + 1], I32))
    c.mod_d = nc.dram_tensor("mod_d", (9, 6 * D), F32).ap()
    c.tab_d = nc.dram_tensor("tab_d", (NH, P, TABW), F32).ap()
    c.h2_d = nc.dram_tensor("h2_d", (TOK, D), F32).ap()
    c.tok_d = nc.dram_tensor("tok_d", ((MAX_SLOTS + 1) * MB, 1), F32).ap()
    c.y_d = nc.dram_tensor("y_d", ((MAX_SLOTS + 1) * MB, D), F32).ap()
    c.w_in = view(W_, KT, IN_W)
    c.mix = view(MIX_, KT, TOK)
    c.bias = view(L_, NH, D)
    c.qT = view(QT_, 4, TOK)
    c.kT = view(KT_, 2, TOK)
    c.vs = view(VS_, NT, 2, 2, HD)
    c.modw = [view(L_ + 4096 * s, 4, D) for s in range(2)]
    c.mods = view(ZR_ + 1792, D)
    c.modb = view(ZR_ + 1792 + D, D)
    c.cT = view(S1_ + 2690, KT, 9)
    c.modT = c.misc[:, 0:144].rearrange("p (a b) -> p a b", a=2 * KT)
    c.modw_in = [c.sem(f"modw_in{s}") for s in range(2)]
    c.modb_in, c.mod_half_done, c.mod_vec_done = c.sem("modb_in"), c.sem("mod_half_done"), c.sem("mod_vec_done")
    c.mods_ready, c.mods_out = c.sem("mods_ready"), c.sem("mods_out")
    c.w_in_in = [c.sem(f"w_in_in{n}") for n in range(5)]
    c.x_in, c.out_done, c.cph_in, c.page_in = c.sem("x_in"), c.sem("out_done"), c.sem("cph_in"), c.sem("page_in")
    c.out_total = 0
    o = 0
    c.pool_w = view(S1_, 4, HD); o += 4 * HD
    c.pool_sc = view(S1_ + o, 2); o += 2
    c.sgu_wT = view(S1_ + o, 4, P); o += 4 * P
    c.sgu_wS = view(S1_ + o, 4, NS); o += 4 * NS
    c.sgu_b = view(S1_ + o, 4); o += 4
    c.sgu_bS = view(S1_ + o, 4); o += 4
    c.lnv_g = view(S1_ + o, PW); o += PW
    c.lnv_b = view(S1_ + o, PW); o += PW
    c.vn = [view(S1_ + o + PW * s, PW) for s in range(2)]; o += 2 * PW
    c.sgo = view(S1_ + o, PW); o += PW
    c.pbuf = view(S1_ + o, PW); o += PW
    c.st = view(S1_ + o, 24); o += 24
    assert o <= 2690 and 2690 + 72 <= 2816, o
    return c


def mod_load(c, sp, n):
    v, hh = n // 2, n % 2
    if n >= 2:
        sp.wait_ge(c.mod_half_done, n - 1)
    src = c.t["w_mod"][0].rearrange("(k p) n -> p k n", p=P)[:, 4 * hh:4 * hh + 4, v * D:(v + 1) * D]
    sp.dma_start(c.modw[n % 2], src).then_inc(c.modw_in[n % 2], 16)


def mod_products(c, pe, n):
    v, hh = n // 2, n % 2
    pe.wait_ge(c.modw_in[n % 2], 16 * (n // 2 + 1))
    if hh == 0 and v >= 1:
        pe.wait_ge(c.mods_ready, v)
    for k in range(4):
        for m in range(2):
            mm = pe.matmul(c.bank(4 + m)[0:9, :], c.cT[:, 4 * hh + k, :], c.modw[n % 2][:, k, m * 512:(m + 1) * 512],
                           start=(hh == 0 and k == 0), stop=(hh == 1 and k == 3))
    mm.then_inc(c.mod_half_done, 1)


def mod_vector(c, dve, v):
    dve.wait_ge(c.mod_half_done, 2 * v + 2)
    dve.wait_ge(c.modb_in, 16 * (v + 1))
    if v >= 1:
        dve.wait_ge(c.mods_out, 16 * v)
    one = 0.0 if v in (0, 3) else 1.0
    dve.scalar_tensor_tensor(out=c.mods[0:9, :], in0=c.psum[0:9, 2048:3072], scalar=one, in1=c.modb[0:9, :],
                             op0=ALU.add, op1=ALU.add).then_inc(c.mods_ready, 1)


def mod_bias_load(c, pool, v):
    if v >= 1:
        pool.wait_ge(c.mods_ready, v)
    src = bass.AP(tensor=c.t["b_mod"].tensor, offset=v * D, ap=[[0, 9], [1, D]])
    pool.dma_start(c.modb[0:9, :], src).then_inc(c.modb_in, 16)


def mod_store(c, pool, v):
    pool.wait_ge(c.mods_ready, v + 1)
    pool.dma_start(c.mod_d[:, v * D:(v + 1) * D], c.mods[0:9, :]).then_inc(c.mods_out, 16)


W_CHUNKS = ((0, 512), (512, 256), (KV0, 512), (KV0 + 512, 280))


def block_modulation(c):
    nc, t, sem = c.nc, c.t, c.early_sem
    c_n = c.view(XH_, D)
    onehot = c.view(QT_, TABW)
    relb = c.view(QT_ + TABW, NH)
    tab = c.view(QT_ + TABW + 8, TABW)
    sgu_n = c.view(KVR_, 4, P)
    sgb_n = c.view(KVR_ + 512, P)
    c1 = c.view(CPH_, 2304)
    trilT, blk64 = c1[:, 1536:1664], c1[:, 1664 + 512:1664 + 512 + 64]
    rep8 = c1[:, 1664 + 576:1664 + 640]
    c_in, ident_in, small_in = sem("c_in"), sem("ident_in"), sem("small_in")
    silu_done, cT_ps, cT_done = sem("silu_done"), sem("cT_ps"), sem("cT_done")
    tab_ps, tab_done, tab_out, neg_set = sem("tab_ps"), sem("tab_done"), sem("tab_out"), sem("neg_set")
    sgu_ps, sgu_done, sguS_ps, modT_ps, modT_done, sguS_done = (sem(n) for n in (
        "sgu_ps", "sgu_done", "sguS_ps", "modT_ps", "modT_done", "sguS_done"))
    c.cph1 = c1
    tok0 = c.view(XH_ + D, 64)
    tok0_set, tok0_out = sem("tok0_set"), sem("tok0_out")

    with nc.Block() as block:
        @block.sync
        def _(sp):
            sp.dma_start(c_n[0:1, :], t["c_prompt"]).then_inc(c_in, 16)
            sp.dma_start(c_n[1:9, :], t["c_sample"]).then_inc(c_in, 16)
            sp.dma_start(c.ident, t["ident"]).then_inc(ident_in, 16)
            mod_load(c, sp, 0)
            mod_load(c, sp, 1)
            for dst, src in (
                (onehot[0:NBUCK + 1, :], t["onehot"]),
                (relb[0:NBUCK, :], t["rel_bias"]),
                (c1, t["cph1"]),
                (sgu_n, t["sgu_w"][0].rearrange("g i j -> i g j")),
                (sgb_n[0:4, :], t["sgu_b"][0]),
                (c.pool_w[0:HD, :, :], t["pool_w"][0].rearrange("g c d -> c g d")),
                (c.pool_sc, bass.AP(tensor=t["pool_scale"].tensor, offset=0, ap=[[1, P], [P, 2]])),
                (c.lnv_g, bass.AP(tensor=t["sgu_ln_g"].tensor, offset=0, ap=[[0, P], [1, PW]])),
                (c.lnv_b, bass.AP(tensor=t["sgu_ln_b"].tensor, offset=0, ap=[[0, P], [1, PW]])),
                (c.pbuf[0:NB * PBUF, :], t["state_pool"][0].rearrange("b r w -> (b r) w")),
                (c.page[0:1, :], t["page_table"].rearrange("(a b) q -> a (b q)", a=1)),
            ):
                sp.dma_start(dst, src, allow_slow_non_contiguous=dst is c.pool_sc).then_inc(small_in, 16)
            mod_load(c, sp, 2)
            mod_load(c, sp, 3)
            src = t["w_in"][0].rearrange("(k p) n -> p k n", p=P)
            for n, (a, w) in enumerate(W_CHUNKS):
                sp.dma_start(c.w_in[:, :, a:a + w], src[:, :, a:a + w]).then_inc(c.w_in_in[n], 16)
            for j in range(REP):
                for g in range(NKV):
                    to, at = Q0 + P * j + HD * g, Q0 + HD * (REP * g + j)
                    sp.dma_start(c.w_in[:, :, to:to + HD], src[:, :, at:at + HD]).then_inc(c.w_in_in[4], 16)
            sp.wait_ge(tab_done, 1)
            sp.dma_start(c.tab_d, tab[0:NH, :].unsqueeze(1).to_broadcast([NH, P, TABW])).then_inc(tab_out, 16)
            sp.wait_ge(silu_done, 1)
            sp.wait_ge(cT_ps, 1)
            sp.dma_start(c.view(XH_, D)[:, :], t["x_prompt"][0, 0:P, :]).then_inc(c.x_in, 16)
            sp.wait_ge(tab_out, 16)

        @block.gpsimd
        def _(pool):
            mod_bias_load(c, pool, 0)
            pool.dma_start(t["o_pool_s"][0, :, 0:PBUF - JS, :], t["state_pool"][0, :, JS:PBUF, :]).then_inc(c.out_done, 16)
            pool.dma_start(t["o_win_s"][0, :, 0:PAST - JS].rearrange("b s a g d -> b (s a g d)"),
                           t["state_win_kv"][0, :, JS:PAST].rearrange("b s a g d -> b (s a g d)")).then_inc(c.out_done, 16)
            c.out_total += 32
            pool.wait_ge(tok0_set, 1)
            pool.dma_start(c.tok_d.rearrange("(a b) o -> a (b o)", b=64), tok0[0:66, :]).then_inc(tok0_out, 16)
            mod_store(c, pool, 0)
            mod_bias_load(c, pool, 1)
            mod_store(c, pool, 1)
            mod_bias_load(c, pool, 2)
            pool.wait_ge(tok0_out, 16)

        @block.scalar
        def _(act):
            act.wait_ge(c_in, 32)
            act.activation(c_n[0:9, :], c_n[0:9, :], ACT.Silu).then_inc(silu_done, 1)

        @block.tensor
        def _(pe):
            pe.wait_ge(ident_in, 16)
            pe.wait_ge(silu_done, 1)
            for k in range(KT):
                mm = pe.transpose(c.bank(7)[:, 9 * k:9 * k + 9], c_n[0:9, k * P:(k + 1) * P], c.ident[0:9, 0:9])
            mm.then_inc(cT_ps, 1)
            pe.wait_ge(cT_done, 1)
            mod_products(c, pe, 0)
            pe.wait_ge(small_in, 16 * 11)
            pe.wait_ge(neg_set, 1)
            for n in range(3):
                w = TABW // 3
                mm = pe.matmul(c.bank(n)[0:NH, 0:w], relb[0:NBUCK + 1, :], onehot[0:NBUCK + 1, n * w:(n + 1) * w],
                               start=True, stop=True)
            mm.then_inc(tab_ps, 1)
            for g in range(4):
                pe.transpose(c.bank(3)[:, g * P:(g + 1) * P], sgu_n[:, g, :], c.ident)
            pe.transpose(c.bank(6)[:, 200:204], sgb_n[0:4, :], c.ident[0:4, 0:4]).then_inc(sgu_ps, 1)
            mod_products(c, pe, 1)
            pe.wait_ge(sgu_done, 2)
            for g in range(4):
                pe.matmul(c.bank(7)[0:NS, g * NS:(g + 1) * NS], rep8[0:JS, :],
                          c.sgu_wT[0:JS, g, 0:JS].unsqueeze(1).to_broadcast([JS, NB, JS]), start=True, stop=True)
            pe.matmul(c.bank(7)[0:NS, 256:260], rep8[0:JS, :], c.sgu_b[0:JS, :], start=True, stop=True).then_inc(sguS_ps, 1)
            mod_products(c, pe, 2)
            mod_products(c, pe, 3)
            for v in range(2):
                pe.wait_ge(c.mods_ready, v + 1)
                for k in range(KT):
                    o = (v * KT + k) * 9
                    mm = pe.transpose(c.bank(6)[:, o:o + 9], c.mods[0:9, k * P:(k + 1) * P], c.ident[0:9, 0:9])
                mm.then_inc(modT_ps, 1)

        @block.vector
        def _(dve):
            dve.memset(relb[NBUCK:NBUCK + 1, :], NEG).then_inc(neg_set, 1)
            dve.memset(tok0[0:66, :], 0.0).then_inc(tok0_set, 1)
            dve.wait_ge(cT_ps, 1)
            dve.tensor_copy(c.cT, c.bank(7, 72).rearrange("p (k a) -> p k a", k=KT)).then_inc(cT_done, 1)
            dve.wait_ge(tab_ps, 1)
            w = TABW // 3
            dve.tensor_copy(tab[0:NH, :].rearrange("p (a b) -> p a b", a=3),
                            c.psum[0:NH, 0:1536].rearrange("p (a b) -> p a b", a=3)[:, :, 0:w]).then_inc(tab_done, 1)
            dve.wait_ge(sgu_ps, 1)
            dve.tensor_tensor(c.sgu_wT, c.bank(3).rearrange("p (g i) -> p g i", g=4),
                              trilT.unsqueeze(1).to_broadcast([P, 4, P]), ALU.mult).then_inc(sgu_done, 1)
            dve.tensor_copy(c.sgu_b, c.bank(6)[:, 200:204]).then_inc(sgu_done, 1)
            dve.wait_ge(sguS_ps, 1)
            dve.tensor_tensor(c.sgu_wS[0:NS, :, :], c.bank(7)[0:NS, 0:256].rearrange("p (g i) -> p g i", g=4),
                              blk64[0:NS, :].unsqueeze(1).to_broadcast([NS, 4, NS]), ALU.mult).then_inc(sguS_done, 1)
            dve.tensor_copy(c.sgu_bS[0:NS, :], c.bank(7)[0:NS, 256:260]).then_inc(sguS_done, 1)
            mod_vector(c, dve, 0)
            dve.wait_ge(modT_ps, 1)
            dve.tensor_copy(c.modT[:, 0:KT, :], c.bank(6)[:, 0:72].rearrange("p (a b) -> p a b", a=KT)).then_inc(modT_done, 1)
            mod_vector(c, dve, 1)
            dve.wait_ge(modT_ps, 2)
            dve.tensor_copy(c.modT[:, KT:, :], c.bank(6)[:, 72:144].rearrange("p (a b) -> p a b", a=KT)).then_inc(modT_done, 1)
            dve.wait_ge(modT_done, 2)
            dve.wait_ge(sguS_done, 2)


def block_projection(c):
    nc, t, sem = c.nc, c.t, c.early_sem
    x = c.view(XH_, D)
    hT = [c.view(XH_ + D * (1 + s), KT, P) for s in range(2)]
    zp = [c.view(ZR_ + PW * s, PW) for s in range(3)]
    zuv = [c.view(ZR_ + 3 * PW + 2 * PW * s, 2, PW) for s in range(2)]
    kv = [c.view(KVR_ + 3 * KVW * s, 3, 2, P) for s in range(2)]
    dT = c.view(ZR_ + 3840, 4, P)
    first, same, prev = (c.cph1[:, 512 * n:512 * n + 512].rearrange("p (g t) -> p g t", g=4) for n in range(3))
    pb_new = c.cph1[:, 1664 + 256:1664 + 512].rearrange("p (g t) -> p g t", g=4)
    pb_buf = c.cph1[:, 1664:1664 + 256].rearrange("p (g t) -> p g t", g=4)
    stats, mv, rstd = c.st[:, 0:6], c.st[:, 8:10], c.st[:, 12:13]
    (xT_ready, h_act, h_dve, z_ready, z_act, z_dve, q_done, q_evac, kT_ready, kT_evac, pd_ready, pd_evac, po_ready,
     po_evac, sg_ready, sgo_ready, so_ready, so_evac, vn_ready, st_ready, sqrt_done, v_copied, sg_tmp,
     link) = (sem(n) for n in (
         "xT_ready", "h_act", "h_dve", "z_ready", "z_act", "z_dve", "q_done", "q_evac", "kT_ready", "kT_evac",
         "pd_ready", "pd_evac", "po_ready", "po_evac", "sg_ready", "sgo_ready", "so_ready", "so_evac", "vn_ready",
         "st_ready", "sqrt_done", "v_copied", "sg_tmp", "vn_link"))
    kv_out = [sem(f"kv_out{s}") for s in range(2)]
    p_out, sgv_out = sem("p_out"), sem("sgv_out")
    c.bias_in = c.sem("bias_in")
    smp = NP_TILES
    n_kv_out = [0, 0]

    with nc.Block() as block:
        @block.sync
        def _(sp):
            for i in range(1, NT):
                sp.wait_ge(xT_ready, i)
                T = tile_rows(i)
                src = t["x_prompt"][0, i * P:(i + 1) * P, :] if i < smp else t["x_sample"].rearrange("b j d -> (b j) d")
                sp.dma_start(x[0:T, :], src).then_inc(c.x_in, 16)
                if i + 3 <= 11:
                    mod_load(c, sp, i + 3)
            sp.wait_ge(c.mod_half_done, 12)
            src = bass.AP(tensor=c.tab_d.tensor, offset=P - 1, ap=[[TABW - 1, P], [P * TABW, NH], [1, D]])
            sp.dma_start(c.bias, src).then_inc(c.bias_in, 16)

        @block.gpsimd
        def _(pool):
            vec = 2
            for i in range(NT):
                T, s = tile_rows(i), i % 2
                pool.wait_ge(z_act, 3 * i + 3)
                for br in range(2):
                    cp = pool.tensor_copy(c.vs[0:T, i, br, :, :].rearrange("p g d -> p (g d)"), kv[s][0:T, 1 + br, 1, :])
                cp.then_inc(v_copied, 1)
                if i < smp:
                    outs = [("o_cmp_p", 0), ("o_sel_p", 1)] + ([("o_win_p", 2)] if i >= 4 else [])
                    for name, br in outs:
                        r0 = (i - 4 if br == 2 else i) * P
                        dst = t[name][0, 0, r0:r0 + P].rearrange("s a g d -> s (a g d)")
                        pool.dma_start(dst, kv[s][:, br, :, :].rearrange("p a d -> p (a d)")).then_inc(kv_out[s], 16)
                        n_kv_out[s] += 1
                else:
                    for name, br in (("o_cmp_s", 0), ("o_sel_s", 1), ("o_win_s", 2)):
                        for b in range(NB):
                            dst = t[name][0, b, (PAST - JS if br == 2 else 0):(PAST if br == 2 else JS)]
                            pool.dma_start(dst.rearrange("s a g d -> s (a g d)"),
                                           kv[s][JS * b:JS * b + JS, br, :, :].rearrange("p a d -> p (a d)")).then_inc(kv_out[s], 16)
                            n_kv_out[s] += 1
                if i == smp - 1:
                    pool.dma_start(t["o_pool_p"][0, 0], zp[i % 3][P - PBUF:P, :]).then_inc(p_out, 16)
                if i == smp:
                    for b in range(NB):
                        pool.dma_start(t["o_pool_s"][0, b, PBUF - JS:PBUF, :], zp[i % 3][JS * b:JS * b + JS, :]).then_inc(p_out, 16)
                    pool.wait_ge(vn_ready, NT)
                    pool.dma_start(t["o_sgu_s"][0].rearrange("b j w -> (b j) w"), c.vn[i % 2][0:NS, :]).then_inc(sgv_out, 16)
                if i >= 2 and i % 2 == 0:
                    mod_store(c, pool, vec)
                    if vec < 5:
                        mod_bias_load(c, pool, vec + 1)
                    vec += 1
            pool.wait_ge(p_out, 16 * 9)
            pool.wait_ge(sgv_out, 16)
            pool.wait_ge(c.mods_out, 16 * 6)
            for s in range(2):
                pool.wait_ge(kv_out[s], 16 * n_kv_out[s])

        kv_dmas = {}
        total = [0, 0]
        for i in range(NT):
            total[i % 2] += (2 if i < 4 else 3) if i < smp else 3 * NB
            kv_dmas[i] = 16 * total[i % 2]

        @block.tensor
        def _(pe):
            def transposes(i):
                T = tile_rows(i)
                pe.wait_ge(c.x_in, 16 * (i + 1))
                if i >= 1:
                    pe.wait_ge(h_act, i)
                    pe.wait_ge(h_dve, i)
                for k in range(KT):
                    mm = pe.transpose(c.bank(k // 4)[:, (k % 4) * P:(k % 4) * P + T], x[0:T, k * P:(k + 1) * P],
                                      c.ident[0:T, 0:T])
                mm.then_inc(xT_ready, 1)

            def chunk(i, n):
                T = tile_rows(i)
                a, w = W_CHUNKS[n]
                if i == 0:
                    pe.wait_ge(c.w_in_in[n], 16)
                if n == 0:
                    if i < smp:
                        pe.wait_ge(h_act, i + 1)
                    pe.wait_ge(h_dve, i + 1)
                if n <= 1 and i >= 1:
                    pe.wait_ge(z_act, 3 * (i - 1) + 2 + n)
                if n == 2:
                    pe.wait_ge(z_act, 3 * i + 1)
                if n == 3:
                    pe.wait_ge(z_dve, i + 1)
                for k in range(KT):
                    mm = pe.matmul(c.bank(2 + n % 2)[0:T, 0:w], hT[i % 2][:, k, 0:T], c.w_in[:, k, a:a + w],
                                   start=(k == 0), stop=(k == KT - 1))
                mm.then_inc(z_ready, 1)

            def queries(i):
                T = tile_rows(i)
                if i == 0:
                    pe.wait_ge(c.w_in_in[4], 16 * 2 * REP)
                else:
                    pe.wait_ge(q_evac, i)
                for j in range(REP):
                    for k in range(KT):
                        two = c.w_in[:, k, Q0 + P * j:Q0 + P * j + P]
                        mm = pe.matmul(c.bank(6)[:, j * P:j * P + T], two, hT[i % 2][:, k, 0:T],
                                       start=(k == 0), stop=(k == KT - 1))
                mm.then_inc(q_done, 1)

            def keys(i):
                T = tile_rows(i)
                pe.wait_ge(z_act, 3 * i + 3)
                if i >= 1:
                    pe.wait_ge(so_evac, i)
                for br in range(2):
                    mm = pe.transpose(c.bank(7)[:, br * P:br * P + T], kv[i % 2][0:T, 1 + br, 0, :], c.ident[0:T, 0:T])
                mm.then_inc(kT_ready, 1)

            def pool_window(i):
                T = tile_rows(i)
                pe.wait_ge(kT_evac, i + 1)
                for g in range(4):
                    out = c.bank(7)[0:HD, g * P:g * P + T]
                    cols = slice(g * HD, (g + 1) * HD)
                    if i == 0:
                        mm = pe.matmul(out, zp[0][:, cols], first[:, g, :], start=True, stop=True)
                    elif i < smp:
                        pe.matmul(out, zp[(i - 1) % 3][:, cols], prev[:, g, :], start=True, stop=False)
                        mm = pe.matmul(out, zp[i % 3][:, cols], same[:, g, :], start=False, stop=True)
                    else:
                        n = NB * PBUF
                        pe.matmul(out, c.pbuf[0:n, cols], pb_buf[0:n, g, :], start=True, stop=False)
                        mm = pe.matmul(out, zp[i % 3][0:NS, cols], pb_new[0:NS, g, :], start=False, stop=True)
                mm.then_inc(pd_ready, 1)

            def pool_mix(i):
                T = tile_rows(i)
                pe.wait_ge(pd_evac, i + 1)
                for g in range(4):
                    lo = HD * (g % 2)
                    mm = pe.matmul(c.bank(7)[lo:lo + HD, (g // 2) * P:(g // 2) * P + T], c.pool_w[0:HD, g, :],
                                   dT[0:HD, g, 0:T], start=True, stop=True)
                mm.then_inc(po_ready, 1)

            def gating(i):
                T = tile_rows(i)
                pe.wait_ge(po_evac, i + 1)
                pe.wait_ge(vn_ready, i + 1)
                w = c.sgu_wT if i < smp else c.sgu_wS
                for g in range(4):
                    mm = pe.matmul(c.bank(7)[0:T, g * HD:(g + 1) * HD], w[0:T, g, 0:T],
                                   c.vn[i % 2][0:T, g * HD:(g + 1) * HD], start=True, stop=True)
                mm.then_inc(sg_ready, 1)

            def gating_out(i):
                T = tile_rows(i)
                pe.wait_ge(sgo_ready, i + 1)
                for m in range(2):
                    mm = pe.transpose(c.bank(7)[:, m * P:m * P + T], c.sgo[0:T, m * P:(m + 1) * P], c.ident[0:T, 0:T])
                mm.then_inc(so_ready, 1)

            transposes(0)
            for i in range(NT + 1):
                last = i - 1
                if i + 1 < NT:
                    transposes(i + 1)
                if i < NT:
                    chunk(i, 0)
                if i >= 1:
                    keys(last)
                if i < NT:
                    chunk(i, 1)
                if i >= 1:
                    pool_window(last)
                if i < NT:
                    chunk(i, 2)
                if i >= 1:
                    pool_mix(last)
                    if i < NT:
                        mod_products(c, pe, i + 3)
                    gating(last)
                if i < NT:
                    chunk(i, 3)
                if i >= 1:
                    gating_out(last)
                if i < NT:
                    queries(i)

        @block.scalar
        def _(act):
            def h_part(i):
                act.wait_ge(xT_ready, i + 1)
                if i >= 2:
                    act.wait_ge(q_done, i - 1)
                for k in range(4):
                    a = act.activation(hT[i % 2][:, k, :], c.bank(0)[:, k * P:(k + 1) * P], ACT.Identity,
                                       bias=c.modT[:, k, 0:1], scale=c.modT[:, KT + k, 0:1])
                a.then_inc(h_act, 1)

            h_part(0)
            for i in range(NT):
                T, s = tile_rows(i), i % 2
                if i + 1 < smp:
                    h_part(i + 1)
                act.wait_ge(z_ready, 4 * i + 1)
                if i >= 2:
                    act.wait_ge(pd_ready, i - 1)
                    act.wait_ge(sgo_ready, i - 1)
                act.copy(zp[i % 3][0:T, :], c.bank(2)[0:T, 0:PW])
                act.copy(zuv[s][0:T, 0, :], c.bank(2)[0:T, PW:2 * PW]).then_inc(z_act, 1)
                act.wait_ge(z_ready, 4 * i + 3)
                if i >= 2:
                    act.wait_ge(kv_out[s], kv_dmas[i - 2])
                    act.wait_ge(v_copied, i - 1)
                    act.wait_ge(kT_ready, i - 1)
                act.copy(kv[s][0:T, 0:2, :, :].rearrange("p b a d -> p (b a d)"), c.bank(2)[0:T, :]).then_inc(z_act, 1)
                act.wait_ge(z_ready, 4 * i + 4)
                act.copy(kv[s][0:T, 2, :, :].rearrange("p a d -> p (a d)"), c.bank(3)[0:T, 0:KVW])
                act.copy(c.gates[0:T, i, :], c.bank(3)[0:T, KVW:KVW + 24]).then_inc(z_act, 1)
                act.wait_ge(st_ready, i + 1)
                act.activation(rstd[0:T, :], mv[0:T, 1:2], ACT.Sqrt).then_inc(sqrt_done, 1)

        @block.vector
        def _(dve):
            links = [0]

            def linked(ins):
                links[0] += 1
                ins.then_inc(link, 1)
                dve.wait_ge(link, links[0])

            def h_part(i):
                dve.wait_ge(xT_ready, i + 1)
                if i >= 2:
                    dve.wait_ge(q_done, i - 1)
                if i < smp:
                    for k in range(4, KT):
                        a = dve.tensor_scalar(hT[i % 2][:, k, :], c.bank(1)[:, (k - 4) * P:(k - 3) * P],
                                              c.modT[:, KT + k, 0:1], c.modT[:, k, 0:1], ALU.mult, ALU.add)
                    a.then_inc(h_dve, 1)
                    return
                for k in range(KT):
                    src = c.bank(k // 4)[:, (k % 4) * P:(k % 4) * P + NS].rearrange("p (b j) -> p b j", b=NB)
                    dst = hT[i % 2][:, k, 0:NS].rearrange("p (b j) -> p b j", b=NB)
                    scale = c.modT[:, KT + k, 1:9].unsqueeze(2).to_broadcast([P, NB, JS])
                    shift = c.modT[:, k, 1:9].unsqueeze(2).to_broadcast([P, NB, JS])
                    linked(dve.tensor_tensor(dst, src, scale, ALU.mult))
                    a = dve.tensor_tensor(dst, dst, shift, ALU.add)
                a.then_inc(h_dve, 1)

            h_part(0)
            for i in range(NT + 1):
                last = i - 1
                if i + 1 < NT:
                    h_part(i + 1)
                if i >= 1:
                    T = tile_rows(last)
                    dve.wait_ge(kT_ready, i)
                    dve.tensor_copy(c.kT[:, :, last * P:last * P + T],
                                    c.bank(7, 256).rearrange("p (b t) -> p b t", b=2)[:, :, 0:T]).then_inc(kT_evac, 1)
                if i < NT:
                    Ti = tile_rows(i)
                    dve.wait_ge(z_ready, 4 * i + 2)
                    dve.tensor_copy(zuv[i % 2][0:Ti, 1, :], c.bank(3)[0:Ti, 0:PW]).then_inc(z_dve, 1)
                if i >= 1:
                    dve.wait_ge(pd_ready, i)
                    if i >= 2:
                        dve.wait_ge(po_ready, i - 1)
                    dve.tensor_copy(dT[0:HD, :, 0:T], c.bank(7)[0:HD, :].rearrange("p (g t) -> p g t", g=4)[:, :, 0:T])\
                        .then_inc(pd_evac, 1)
                    dve.wait_ge(po_ready, i)
                    for m in range(2):
                        a = dve.tensor_scalar(c.mix[:, m, last * P:last * P + T], c.bank(7)[:, m * P:m * P + T],
                                              c.pool_sc[:, m:m + 1], None, ALU.mult)
                    a.then_inc(po_evac, 1)
                    if i < NT and i % 2 == 0:
                        mod_vector(c, dve, i // 2 + 1)
                    bias = c.sgu_b if last < smp else c.sgu_bS
                    dve.wait_ge(sg_ready, i)
                    if i >= 2:
                        dve.wait_ge(so_ready, i - 1)
                    linked(dve.tensor_tensor(c.sgo[0:T, :].rearrange("p (g d) -> p g d", g=4),
                                             c.bank(7)[0:T, 0:PW].rearrange("p (g d) -> p g d", g=4),
                                             bias[0:T, :].unsqueeze(2).to_broadcast([T, 4, HD]), ALU.add))
                    dve.tensor_tensor(c.sgo[0:T, :], c.sgo[0:T, :], zuv[last % 2][0:T, 0, :], ALU.mult).then_inc(sgo_ready, 1)
                    dve.wait_ge(so_ready, i)
                    dve.tensor_copy(c.mix[:, 2:4, last * P:last * P + T],
                                    c.bank(7, 256).rearrange("p (m t) -> p m t", m=2)[:, :, 0:T]).then_inc(so_evac, 1)
                if i < NT:
                    v, vn = zuv[i % 2][0:Ti, 1, :], c.vn[i % 2][0:Ti, :]
                    dve.wait_ge(z_dve, i + 1)
                    linked(dve.bn_stats(stats[0:Ti, :], v))
                    linked(dve.bn_aggr(mv[0:Ti, :], stats[0:Ti, :]))
                    dve.tensor_scalar(mv[0:Ti, 1:2], mv[0:Ti, 1:2], EPS, None, ALU.add).then_inc(st_ready, 1)
                    dve.wait_ge(sqrt_done, i + 1)
                    linked(dve.reciprocal(rstd[0:Ti, :], rstd[0:Ti, :]))
                    linked(dve.tensor_scalar(vn, v, mv[0:Ti, 0:1], rstd[0:Ti, :], ALU.subtract, ALU.mult))
                    linked(dve.tensor_tensor(vn, vn, c.lnv_g[0:Ti, :], ALU.mult))
                    dve.tensor_tensor(vn, vn, c.lnv_b[0:Ti, :], ALU.add).then_inc(vn_ready, 1)
                    dve.wait_ge(q_done, i + 1)
                    dve.tensor_scalar(c.qT[:, :, i * P:i * P + Ti],
                                      c.bank(6).rearrange("p (j t) -> p j t", j=4)[:, :, 0:Ti], SCALE, None, ALU.mult)\
                        .then_inc(q_evac, 1)


C2_ = KVR_ + 5120
NATW_ = W_ + 12480


def block_compression(c):
    nc, t, sem = c.nc, c.t, c.early_sem
    NPAIR = (SEQ + NB * PAST) // 2
    xcT = c.view(W_, 4, NPAIR)
    w1 = c.view(W_ + 4 * NPAIR, 2, CB // 2, P)
    o = W_ + 4 * NPAIR + 2 * (CB // 2) * P
    nat = [c.view(o + 512 * s, 4, 2, HD) for s in range(3)]
    o += 3 * 512
    w2 = c.view(o, 2, HD)
    pe_n = c.view(o + P, P)
    peT = c.view(o + 2 * P, 2, CB // 2)
    hid = c.view(o + 2 * P + 32, 2, 2, NC_P + NC_S * NB)
    assert o + 2 * P + 32 + 384 <= NATW_
    nblk = NC_P + NC_S * NB
    c.kcS = c.view(C2_, nblk)
    c.kc_bd = c.view(C2_ + 96, 2, NC_P)
    c.vc_bd = c.view(C2_ + 160, 4, HD)
    c.vcS = c.view(C2_ + 416, 2, HD)
    c.nat_win = c.view(NATW_, NB * NPAGE, 256)
    cw_in, pe_in = sem("cw_in"), sem("pe_in")
    nat_in = [sem(f"nat_in{s}") for s in range(3)]
    nt_ps, nt_ev, pe_ps, pe_ev, hid_ps, hid_ev, kc_ps, kc_ev, zeroed = (sem(n) for n in (
        "nt_ps", "nt_ev", "pe_ps", "pe_ev", "hid_ps", "hid_ev", "kc_ps", "kc_ev", "zeroed"))
    c.natw_in, c.gate_done = c.sem("natw_in"), c.sem("gate_done")
    tiles = NPAIR // P
    n_dma = [0, 0, 0]
    need = []
    for n in range(tiles):
        n_dma[n % 3] += 2 if n < 4 else 4
        need.append(16 * n_dma[n % 3])

    with nc.Block() as block:
        @block.sync
        def _(sp):
            sp.dma_start(pe_n[0:32, :], t["cmp_pe"][0].rearrange("s (c q) d -> (s c) (q d)", q=2)).then_inc(pe_in, 16)
            for n in range(tiles):
                if n >= 3:
                    sp.wait_ge(nt_ps, n - 2)
                dst = nat[n % 3]
                if n < 4:
                    src = t["o_cmp_p"][0, 0, n * 256:(n + 1) * 256].rearrange("(p q) s g d -> p q (s g) d", q=2)
                    for q in range(2):
                        sp.dma_start(dst[:, :, q, :], src[:, q]).then_inc(nat_in[n % 3], 16)
                else:
                    b = n - 4
                    for pg in range(NPAGE):
                        at = b * NPAGE + pg
                        page = sp.value_load(c.page[0:1, at:at + 1], min_val=0, max_val=t["cache_cmp_kv"].shape[1] - 1)
                        src = t["cache_cmp_kv"][0, bass.ds(page, 1)].rearrange("n (p q) s g d -> p q (n s g) d", q=2)
                        for q in range(2):
                            sp.dma_start(dst[64 * pg:64 * pg + 64, :, q, :], src[:, q]).then_inc(nat_in[n % 3], 16)
                if n == 3:
                    sp.dma_start(w1, t["cmp_w1"][0].rearrange("s (c p) h -> p s c h", p=P)).then_inc(cw_in, 16)
                    sp.dma_start(w2, t["cmp_w2"][0].rearrange("s h d -> h s d")).then_inc(cw_in, 16)
            sp.dma_start(c.view(CPH_, 1072), t["cph2"]).then_inc(c.cph_in, 16)
            sp.dma_start(c.view(CPH_ + 1072, P), t["cph3"]).then_inc(c.cph_in, 16)
            sp.dma_start(c.nat_win, t["state_win_kv"][0].rearrange("b (q s) a g d -> s (b q) (a g d)", s=P)).then_inc(c.natw_in, 16)

        @block.tensor
        def _(pe):
            pe.wait_ge(pe_in, 16)
            pe.transpose(c.bank(7)[:, 0:32], pe_n[0:32, :], c.ident[0:32, 0:32]).then_inc(pe_ps, 1)
            for n in range(tiles):
                pe.wait_ge(nat_in[n % 3], need[n])
                if n >= 2:
                    pe.wait_ge(nt_ev, n - 1)
                for sg in range(4):
                    mm = pe.transpose(c.bank(n % 2)[:, sg * P:(sg + 1) * P],
                                      nat[n % 3][:, sg, :, :].rearrange("p q d -> p (q d)"), c.ident)
                mm.then_inc(nt_ps, 1)
            pe.wait_ge(nt_ev, tiles)
            pe.wait_ge(cw_in, 32)
            for s in range(2):
                for k in range(CB // 2):
                    cols = xcT[:, 2 * s:2 * s + 2, :].rearrange("p g (n c) -> p g n c", c=CB // 2)[:, :, :, k]
                    mm = pe.matmul(c.bank(2 + s)[:, 0:2 * nblk].rearrange("p (g n) -> p g n", g=2), w1[:, s, k, :], cols,
                                   start=(k == 0), stop=(k == CB // 2 - 1))
                mm.then_inc(hid_ps, 1)
            pe.wait_ge(hid_ev, 1)
            for g in range(2):
                mm = pe.matmul(c.bank(6)[HD * g:HD * g + HD, 0:nblk], w2[:, 0, :], hid[:, 0, g, :], start=True, stop=True)
            pe.wait_ge(hid_ev, 2)
            for x in range(4):
                pe.matmul(c.bank(4)[32 * x:32 * x + 32, 0:HD], hid[:, 1, x % 2, 0:NC_P], w2[:, 1, :], start=True, stop=True)
            for g in range(2):
                mm = pe.matmul(c.bank(5)[0:NB * NC_S, HD * g:HD * g + HD], hid[:, 1, g, NC_P:], w2[:, 1, :],
                               start=True, stop=True)
            mm.then_inc(kc_ps, 1)

        @block.scalar
        def _(act):
            for s in range(2):
                act.wait_ge(hid_ps, s + 1)
                act.activation(hid[:, s, :, :].rearrange("p g n -> p (g n)"), c.bank(2 + s)[:, 0:2 * nblk],
                               ACT.Gelu_apprx_tanh).then_inc(hid_ev, 1)
            act.activation(c.gates[:, 0:NP_TILES, :].rearrange("p a b -> p (a b)"),
                           c.gates[:, 0:NP_TILES, :].rearrange("p a b -> p (a b)"), ACT.Sigmoid).then_inc(c.gate_done, 1)
            act.activation(c.gates[0:NS, NP_TILES, :], c.gates[0:NS, NP_TILES, :], ACT.Sigmoid).then_inc(c.gate_done, 1)

        @block.vector
        def _(dve):
            dve.memset(c.kc_bd, 0.0)
            dve.memset(c.vc_bd, 0.0).then_inc(zeroed, 1)
            dve.wait_ge(pe_ps, 1)
            dve.tensor_copy(peT, c.bank(7)[:, 0:32].rearrange("p (s c) -> p s c", s=2)).then_inc(pe_ev, 1)
            dve.wait_ge(pe_ev, 1)
            for n in range(tiles):
                dve.wait_ge(nt_ps, n + 1)
                for s in range(2):
                    a = None
                    for g in range(2):
                        a = dve.tensor_tensor(
                            xcT[:, 2 * s + g, n * P:(n + 1) * P].rearrange("p (n c) -> p n c", c=CB // 2),
                            c.bank(n % 2)[:, (2 * s + g) * P:(2 * s + g + 1) * P].rearrange("p (n c) -> p n c", c=CB // 2),
                            peT[:, s, :].unsqueeze(1).to_broadcast([P, 8, CB // 2]), ALU.add)
                a.then_inc(nt_ev, 1)
            dve.wait_ge(kc_ps, 1)
            dve.wait_ge(zeroed, 1)
            dve.tensor_copy(c.kcS, c.bank(6)[:, 0:nblk])
            for g in range(2):
                dve.tensor_copy(c.kc_bd[HD * g:HD * g + HD, g, :], c.bank(6)[HD * g:HD * g + HD, 0:NC_P])
            for x in range(4):
                dve.tensor_copy(c.vc_bd[32 * x:32 * x + 32, x, :], c.bank(4)[32 * x:32 * x + 32, 0:HD])
            dve.tensor_copy(c.vcS[0:NB * NC_S, :, :], c.bank(5)[0:NB * NC_S, 0:P].rearrange("p (g d) -> p g d", g=2))\
                .then_inc(kc_ev, 1)
            dve.wait_ge(kc_ev, 1)


def block_decode_attention(c):
    nc, t, sem = c.nc, c.t, c.early_sem
    nat_sel = c.view(W_, NB * NPAGE, 256)
    nats = [nat_sel, c.nat_win]
    kTs = [c.view(W_ + 4096 + 2048 * s, NB, PAST) for s in range(2)]
    o = W_ + 8192
    WK = PAST + NS
    bS = c.view(o, 2, 2, WK); o += 4 * WK
    bC = c.view(o, 2, 2, NS); o += 4 * NS
    qs = c.view(o, 2, P); o += 2 * P
    acc = c.view(o, 2, 2, HD); o += 4 * HD
    acc2 = c.view(o, 2, 2, 2, HD); o += 8 * HD
    gS = c.view(o, 2, 2, 3); o += 12
    gt = c.view(o, 24); o += 24
    mx = c.view(o, 12); sm = c.view(o + 12, 12); cf = c.view(o + 24, 12); o += 36
    pbuf = [c.view(o + WK * s, WK) for s in range(2)]; o += 2 * WK
    pT = [c.view(o + 3 * P * s, 3, P) for s in range(2)]; o += 6 * P
    assert o <= NATW_, o
    selg, rowm, selr = c.view(CPH_, 2, P), c.view(CPH_ + 256, 2, 24), c.view(CPH_ + 304, 4, P)
    mine, notmine = c.view(CPH_ + 816, 2, NB, JS), c.view(CPH_ + 944, 2, NB, JS)
    nats_in = sem("nats_in")
    (kt_ps, kt_ev, bs_ps, bs_ev, g_ps, g_ev, qs_ev, s_ps, s_ev, e_ev, t_ps, t_ev, o_ps, o_ev, f_ps, f_ev, link,
     a2_ev) = (sem(n) for n in (
         "dk_ps", "dk_ev", "db_ps", "db_ev", "dg_ps", "dg_ev", "dq_ev", "ds_ps", "ds_ev", "de_ev", "dt_ps", "dt_ev",
         "do_ps", "do_ev", "df_ps", "df_ev", "d_link", "da_ev"))
    units = [(br, g, half) for br in range(3) for g in range(2) for half in range(2)]

    with nc.Block() as block:
        @block.sync
        def _(sp):
            for at in range(NB * NPAGE):
                page = sp.value_load(c.page[0:1, at:at + 1], min_val=0, max_val=t["cache_sel_kv"].shape[1] - 1)
                sp.dma_start(nat_sel[:, at, :], t["cache_sel_kv"][0, bass.ds(page, 1)].rearrange("n s a g d -> s (n a g d)"))\
                    .then_inc(nats_in, 16)

        @block.tensor
        def _(pe):
            pe.wait_ge(c.bias_in, 16)
            pe.wait_ge(c.cph_in, 32)
            for g in range(2):
                for r in range(REP):
                    pe.matmul(c.bank(6 + g)[:, 0:264], selr[0:JS, r, :], c.bias[0:JS, 4 * g + r, 640:904],
                              start=(r == 0), stop=(r == REP - 1))
                for r in range(REP):
                    mm = pe.matmul(c.bank(6 + g)[:, 272:280], selr[0:JS, r, :],
                                   c.bias[0:JS, 4 * g + r, 671:671 + 32 * 7 + 1:32], start=(r == 0), stop=(r == REP - 1))
                mm.then_inc(bs_ps, 1)
            pe.wait_ge(c.gate_done, 2)
            for half in range(2):
                mm = pe.matmul(c.bank(4)[:, 24 * half:24 * half + 24], selg[0:NS, half, :], c.gates[0:NS, NP_TILES, :],
                               start=True, stop=True)
            mm.then_inc(g_ps, 1)
            pe.wait_ge(qs_ev, 1)
            n_kt = [0]

            def keys(br):
                pe.wait_ge(nats_in if br == 1 else c.natw_in, 16 * 16 if br == 1 else 16)
                for m in range(4):
                    if n_kt[0] >= 2:
                        pe.wait_ge(kt_ev, n_kt[0] - 1)
                    for q in range(4):
                        mm = pe.transpose(c.bank(2 + n_kt[0] % 2)[:, q * P:(q + 1) * P], nats[br - 1][:, 4 * m + q, 0:P], c.ident)
                    mm.then_inc(kt_ps, 1)
                    n_kt[0] += 1

            def scores(u):
                br, g, half = units[u]
                if u >= 2:
                    pe.wait_ge(s_ev, u - 1)
                if br == 1:
                    pe.wait_ge(kt_ev, 4)
                if br == 2:
                    pe.wait_ge(kt_ev, 8)
                lo = HD * g
                q = qs[lo:lo + HD, half, :]
                if br == 0:
                    pe.matmul(c.bank(u % 2)[:, 0:NS], q, c.kcS[lo:lo + HD, NC_P:], start=True, stop=True).then_inc(s_ps, 1)
                    return
                for b4 in range(4):
                    pe.matmul(c.bank(u % 2)[32 * b4:32 * b4 + 32, 0:PAST], q[:, 32 * b4:32 * b4 + 32],
                              kTs[br - 1][lo:lo + HD, 4 * half + b4, :], start=True, stop=True)
                pe.matmul(c.bank(u % 2)[:, PAST:WK], q, c.kT[lo:lo + HD, br - 1, SEQ:], start=True, stop=True).then_inc(s_ps, 1)

            def turns(u):
                br = units[u][0]
                pe.wait_ge(e_ev, u + 1)
                if u >= 2:
                    pe.wait_ge(t_ev, u - 1)
                if u < 2:
                    pe.wait_ge(kt_ev, 8)
                for k, w in enumerate((NS,) if br == 0 else (P, P, NS)):
                    mm = pe.transpose(c.bank(2 + u % 2)[0:w, k * P:(k + 1) * P], pbuf[u % 2][:, k * P:k * P + w], c.ident)
                mm.then_inc(t_ps, 1)

            def values(u):
                br, g, half = units[u]
                pe.wait_ge(t_ev, u + 1)
                if u >= 2:
                    pe.wait_ge(o_ev, u - 1)
                elif u == 0:
                    pe.wait_ge(g_ev, 1)
                out = c.bank(4 + u % 2)[:, 0:HD]
                if br == 0:
                    pe.matmul(out, pT[u % 2][0:NS, 0, :], c.vcS[0:NS, g, :], start=True, stop=True).then_inc(o_ps, 1)
                    return
                pe.matmul(out, pT[u % 2][0:NS, 2, :], c.vs[0:NS, NP_TILES, br - 1, g, :], start=True, stop=False,
                          skip_group_check=True)
                for b4 in range(4):
                    for pg in range(NPAGE):
                        mm = pe.matmul(out[32 * b4:32 * b4 + 32, :], pT[u % 2][:, pg, 32 * b4:32 * b4 + 32],
                                       nats[br - 1][:, (4 * half + b4) * NPAGE + pg, P + HD * g:P + HD * g + HD],
                                       start=False, stop=(pg == NPAGE - 1), skip_group_check=True)
                mm.then_inc(o_ps, 1)

            keys(2)
            keys(1)
            n = len(units)
            for s in range(n + 2):
                if s < n:
                    scores(s)
                if 1 <= s <= n:
                    turns(s - 1)
                if s >= 2:
                    values(s - 2)
            for g in range(2):
                for half in range(2):
                    pe.wait_ge(a2_ev, 1)
                    pe.transpose(c.bank(6 + g)[:, half * P:(half + 1) * P],
                                 acc2[:, g, half, :, :].rearrange("p a d -> p (a d)"), c.ident).then_inc(f_ps, 1)

        @block.scalar
        def _(act):
            for u, (br, g, half) in enumerate(units):
                w = NS if br == 0 else WK
                act.wait_ge(s_ev, u + 1)
                act.activation(pbuf[u % 2][:, 0:w], pbuf[u % 2][:, 0:w], ACT.Exp, bias=mx[:, u:u + 1], scale=-1.0,
                               accum_out=sm[:, u:u + 1]).then_inc(e_ev, 1)

        @block.vector
        def _(dve):
            links = [0]

            def linked(ins):
                links[0] += 1
                ins.then_inc(link, 1)
                dve.wait_ge(link, links[0])

            for half in range(2):
                for b4 in range(4):
                    b = SEQ + (4 * half + b4) * JS
                    a = dve.tensor_copy(qs[:, half, 32 * b4:32 * b4 + 32].rearrange("p (r j) -> p r j", r=REP), c.qT[:, :, b:b + JS])
            a.then_inc(qs_ev, 1)
            dve.wait_ge(c.cph_in, 32)
            for g in range(2):
                dve.wait_ge(bs_ps, g + 1)
                for half in range(2):
                    dve.tensor_copy(bS[:, g, half, 0:PAST], c.bank(6 + g)[:, 0:PAST])
                    for dst, at in ((bS[:, g, half, PAST:], PAST), (bC[:, g, half, :], 272)):
                        dst = dst.rearrange("p (b j) -> p b j", b=NB)
                        src = c.bank(6 + g)[:, at:at + JS].unsqueeze(1).to_broadcast([P, NB, JS])
                        linked(dve.tensor_tensor(dst, src, mine[:, half], ALU.mult))
                        linked(dve.tensor_tensor(dst, dst, notmine[:, half], ALU.add))
            dve.wait_ge(g_ps, 1)
            for half in range(2):
                for g in range(2):
                    linked(dve.tensor_tensor(gt, c.bank(4)[:, 24 * half:24 * half + 24], rowm[:, g, :], ALU.mult))
                    linked(dve.tensor_reduce(gS[:, g, half, :], gt.rearrange("p (h r) -> p r h", r=3), AX.X, ALU.add))
            dve.engine_nop().then_inc(g_ev, 1)
            for n in range(8):
                dve.wait_ge(kt_ps, n + 1)
                dst = kTs[1 - n // 4][:, :, :].rearrange("p b s -> p (b s)")[:, (n % 4) * 512:(n % 4) * 512 + 512]
                dve.tensor_copy(dst, c.bank(2 + n % 2)).then_inc(kt_ev, 1)

            def soft(u):
                br, g, half = units[u]
                w = NS if br == 0 else WK
                dve.wait_ge(s_ps, u + 1)
                if u >= 2:
                    dve.wait_ge(t_ps, u - 1)
                bias = bC if br == 0 else bS
                dve.tensor_tensor_reduce(pbuf[u % 2][:, 0:w], c.bank(u % 2)[:, 0:w], bias[:, g, half, :], -1.0, 3e38,
                                         ALU.add, ALU.min, mx[:, u:u + 1]).then_inc(s_ev, 1)

            def turned(u):
                dve.wait_ge(t_ps, u + 1)
                if u >= 2:
                    dve.wait_ge(o_ps, u - 1)
                if units[u][0] == 0:
                    dve.tensor_copy(pT[u % 2][0:NS, 0, :], c.bank(2 + u % 2)[0:NS, 0:P]).then_inc(t_ev, 1)
                else:
                    dve.tensor_copy(pT[u % 2][:, 0:2, :], c.bank(2 + u % 2)[:, 0:256].rearrange("p (a b) -> p a b", a=2))
                    dve.tensor_copy(pT[u % 2][0:NS, 2, :], c.bank(2 + u % 2)[0:NS, 256:384]).then_inc(t_ev, 1)

            def gather(u):
                br, g, half = units[u]
                linked(dve.tensor_scalar(cf[:, u:u + 1], sm[:, u:u + 1], 1e-30, None, ALU.max))
                linked(dve.reciprocal(cf[:, u:u + 1], cf[:, u:u + 1]))
                linked(dve.tensor_tensor(cf[:, u:u + 1], cf[:, u:u + 1], gS[:, g, half, br:br + 1], ALU.mult))
                dve.wait_ge(o_ps, u + 1)
                o = c.bank(4 + u % 2)[:, 0:HD]
                if br == 0:
                    a = dve.tensor_scalar(acc[:, g, half, :], o, cf[:, u:u + 1], None, ALU.mult)
                else:
                    a = dve.scalar_tensor_tensor(out=acc[:, g, half, :], in0=o, scalar=cf[:, u:u + 1],
                                                 in1=acc[:, g, half, :], op0=ALU.mult, op1=ALU.add)
                a.then_inc(o_ev, 1)
                dve.wait_ge(o_ev, u + 1)

            n = len(units)
            for s in range(n + 2):
                if s < n:
                    soft(s)
                if 1 <= s <= n:
                    turned(s - 1)
                if s >= 2:
                    gather(s - 2)
            for d in range(2):
                a = dve.tensor_copy(acc2[:, :, :, d, :].rearrange("p g h d -> p (g h) d"),
                                    acc.rearrange("p g h d -> p (g h) d"))
            a.then_inc(a2_ev, 1)
            for g in range(2):
                for half in range(2):
                    dve.wait_ge(f_ps, 2 * g + half + 1)
                for r in range(REP):
                    h = REP * g + r
                    lo = HD * (h % 2)
                    src = c.bank(6 + g)[lo:lo + HD, 0:256].rearrange("p (b r j) -> p b r j", b=NB, r=REP)[:, :, r, :]
                    dve.tensor_copy(c.mix[lo:lo + HD, 4 + h // 2, SEQ:].rearrange("p (b j) -> p b j", b=NB), src).then_inc(f_ev, 1)
            dve.wait_ge(f_ev, 8)


def retire_early_semaphores(c):
    c.nc.clear_and_free_semaphores(c.early)
    c.nc.all_engine_barrier()


def block_prompt_attention(c):
    nc, t, sem = c.nc, c.t, c.sem
    NU = 16 * NP_TILES
    c.w_out = c.view(W_, KT, D)
    pb = [c.view(KVR_ + D * s, D) for s in range(3)]
    pT = [c.view(KVR_ + D * (3 + s), KT, P) for s in range(2)]
    o = C2_ + 544
    oa = c.view(o, NH, HD)
    pc, pcT, tmp = c.view(o + 512, NH, NC_P), c.view(o + 768, 2, P), c.view(o + 1024, NH, HD)
    o += 1536
    mx, sm, cf = c.view(o, 3), c.view(o + 4, 16), c.view(o + 20, NH)
    cm, cs = c.view(o + 28, NH), c.view(o + 36, NH)
    assert o + 44 <= C2_ + 2304
    edge_f = c.view(CPH_ + 1072, P)
    edge = c.view(CPH_ + 1200, HD).bitcast(BF16)
    ident_b = c.view(CPH_ + 1264, HD).bitcast(BF16)
    (s_ps, s_ev, e_ev, t_ps, t_dve, t_act, v_ps, o_ev, cs_ps, cs_ev, ce_ev, cn_ev, co_ps, co_ev, edge_set,
     link, zero_set) = (sem(n) for n in ("ps_ps", "ps_ev", "pexp_ev", "pt_ps", "pt_dve", "pt_act", "pv_ps", "po_ev", "cs_ps", "cs_ev",
                               "ce_ev", "cn_ev", "co_ps", "co_ev", "edge_set", "p_link", "pc_zero"))
    c.w_out_in = sem("w_out_in")

    def unit(s):
        i, br, slot = s // 16, s % 16 // 8, s % 8
        k0 = max(0, i - WIN_TILES) if br else 0
        return i, br, slot // 2, slot % 2, k0, i + 1 - k0

    turns, number = [], {}
    for s in range(NU + 3):
        if 0 <= s - 2 < NU:
            turns.append(("unit", s - 2))
        if s < NU and s % 16 == 6 and s >= 16:
            turns.append(("result", s // 16 - 1))
        if s < NU and s % 16 == 8:
            turns.append(("compressed", s // 16))
    turns.append(("result", NP_TILES - 1))
    for n, what in enumerate(turns):
        number[what] = n

    def by_act(what):
        return what[0] == "unit" and unit(what[1])[5] > 4

    act_before = [sum(by_act(w) for w in turns[:n]) for n in range(len(turns) + 1)]

    with nc.Block() as block:
        @block.sync
        def _(sp):
            sp.dma_start(c.w_out, t["w_out"][0].rearrange("(k p) n -> p k n", p=P)).then_inc(c.w_out_in, 16)

        @block.tensor
        def _(pe):
            def bank_free(what):
                n = number[what]
                if n:
                    pe.wait_ge(t_dve, n)
                    if act_before[n]:
                        pe.wait_ge(t_act, act_before[n])

            def scores(s):
                i, br, j, g, k0, nk = unit(s)
                if s >= 2:
                    pe.wait_ge(s_ev, s - 1)
                lo, base = HD * g, (s % 2) * 1024
                edge_here = br == 1 and i >= WIN_TILES
                for c0 in range(0, nk * P, 512):
                    w = min(512, nk * P - c0)
                    masked = edge_here and c0 == 0
                    mm = pe.matmul(c.psum[:, base + c0:base + c0 + w], c.qT[lo:lo + HD, j, i * P:(i + 1) * P],
                                   c.kT[lo:lo + HD, br, k0 * P + c0:k0 * P + c0 + w], start=True, stop=not masked)
                    if masked:
                        if s == 16 * WIN_TILES + 8:
                            pe.wait_ge(edge_set, 2)
                        mm = pe.matmul(c.psum[:, base:base + P], ident_b, edge, start=False, stop=True)
                mm.then_inc(s_ps, 1)

            def turn(s):
                nk = unit(s)[5]
                pe.wait_ge(e_ev, s + 1)
                bank_free(("unit", s))
                for k in range(nk):
                    mm = pe.transpose(c.psum[:, 2048 + k * P:2048 + (k + 1) * P], pb[s % 3][:, k * P:(k + 1) * P], c.ident)
                mm.then_inc(t_ps, 1)

            def values(s):
                i, br, j, g, k0, nk = unit(s)
                pe.wait_ge(t_dve, number["unit", s] + 1)
                if nk > 4:
                    pe.wait_ge(t_act, act_before[number["unit", s] + 1])
                if s % 8 == 0:
                    if br == 0 and i >= 1:
                        pe.wait_ge(o_ev, 2 * i - 1)
                    if br == 1:
                        pe.wait_ge(co_ev, i + 1)
                slot = s % 8
                for k in range(nk):
                    mm = pe.matmul(c.bank(6 + br)[:, slot * HD:(slot + 1) * HD], pT[s % 2][:, k, :], c.vs[:, k0 + k, br, g, :],
                                   start=(k == 0), stop=(k == nk - 1))
                mm.then_inc(v_ps, 1)

            def compressed_scores(i):
                if i >= 1:
                    pe.wait_ge(o_ev, 2 * i)
                for j in range(REP):
                    mm = pe.matmul(c.bank(7)[:, 64 * j:64 * j + 64], c.qT[:, j, i * P:(i + 1) * P],
                                   c.kc_bd.rearrange("p g n -> p (g n)"), start=True, stop=True)
                mm.then_inc(cs_ps, 1)

            def compressed_turn(i):
                pe.wait_ge(cn_ev, i + 1)
                bank_free(("compressed", i))
                flat = pc.rearrange("p h n -> p (h n)")
                for m in range(2):
                    mm = pe.transpose(c.bank(4)[:, m * P:(m + 1) * P], flat[:, m * P:(m + 1) * P], c.ident)
                mm.then_inc(t_ps, 1)

            def compressed_values(i):
                pe.wait_ge(t_dve, number["compressed", i] + 1)
                for m in range(2):
                    mm = pe.matmul(c.bank(7)[:, 256 * m:256 * m + 256], pcT[:, m, :], c.vc_bd.rearrange("p x d -> p (x d)"),
                                   start=True, stop=True)
                mm.then_inc(co_ps, 1)

            def result_turn(i):
                pe.wait_ge(o_ev, 2 * i + 2)
                bank_free(("result", i))
                flat = oa.rearrange("p h d -> p (h d)")
                for m in range(4):
                    mm = pe.transpose(c.bank(4)[:, m * P:(m + 1) * P], flat[:, m * P:(m + 1) * P], c.ident)
                mm.then_inc(t_ps, 1)

            for s in range(NU + 3):
                i, r = s // 16, s % 16
                if s < NU:
                    scores(s)
                if 0 <= s - 2 < NU:
                    turn(s - 2)
                if s < NU:
                    if r == 5:
                        compressed_scores(i)
                    if r == 6 and i >= 1:
                        result_turn(i - 1)
                    if r == 8:
                        compressed_turn(i)
                    if r == 9:
                        compressed_values(i)
                if s >= 3:
                    values(s - 3)
            result_turn(NP_TILES - 1)

        @block.scalar
        def _(act):
            for s in range(NU + 3):
                if s < NU:
                    i, br, j, g, k0, nk = unit(s)
                    act.wait_ge(s_ev, s + 1)
                    if i >= 1:
                        act.wait_ge(o_ev, 2 * (i - 1) + br + 1)
                    act.activation(pb[s % 3][:, 0:nk * P], pb[s % 3][:, 0:nk * P], ACT.Exp, bias=mx[:, s % 3:s % 3 + 1],
                                   scale=-1.0, accum_out=sm[:, s % 16:s % 16 + 1]).then_inc(e_ev, 1)
                if 0 <= s - 2 < NU and by_act(("unit", s - 2)):
                    u = s - 2
                    nk = unit(u)[5]
                    act.wait_ge(t_ps, number["unit", u] + 1)
                    act.wait_ge(v_ps, u - 1)
                    act.copy(pT[u % 2][:, 4:nk, :].rearrange("p k q -> p (k q)"), c.bank(5)[:, 0:(nk - 4) * P]).then_inc(t_act, 1)
                if s < NU and s % 16 == 5:
                    n = 4 * (s // 16 + 1)
                    act.wait_ge(cs_ev, s // 16 + 1)
                    act.activation(pc[:, :, 0:n], pc[:, :, 0:n], ACT.Exp).then_inc(ce_ev, 1)

        @block.vector
        def _(dve):
            links = [0]

            def linked(ins):
                links[0] += 1
                ins.then_inc(link, 1)
                dve.wait_ge(link, links[0])

            def soft(s):
                i, br, j, g, k0, nk = unit(s)
                w = nk * P
                dve.wait_ge(s_ps, s + 1)
                if s >= 3:
                    dve.wait_ge(t_ps, number["unit", s - 3] + 1)
                dve.tensor_tensor_reduce(pb[s % 3][:, 0:w], c.psum[:, (s % 2) * 1024:(s % 2) * 1024 + w],
                                         c.bias[:, 4 * g + j, D - w:D], -1.0, 3e38, ALU.add, ALU.min,
                                         mx[:, s % 3:s % 3 + 1]).then_inc(s_ev, 1)

            def turned(what, dst, src):
                dve.wait_ge(t_ps, number[what] + 1)
                dve.tensor_copy(dst, src).then_inc(t_dve, 1)

            def weighted(out, sums, i, br):
                linked(dve.tensor_scalar(out, sums, 1e-30, None, ALU.max))
                linked(dve.reciprocal(out, out))
                gate = c.gates[:, i, :].rearrange("p (g j r) -> p j g r", g=2, j=4)[:, :, :, br]
                linked(dve.tensor_tensor(out.rearrange("p (j g) -> p j g", g=2), out.rearrange("p (j g) -> p j g", g=2), gate, ALU.mult))

            def branch_result(i, br):
                weighted(cf, sm[:, 8 * br:8 * br + 8], i, 1 + br)
                dve.wait_ge(v_ps, 16 * i + 8 * br + 8)
                linked(dve.tensor_tensor(tmp, c.bank(6 + br).rearrange("p (h d) -> p h d", d=HD),
                                         cf.unsqueeze(2).to_broadcast([P, NH, HD]), ALU.mult))
                if br == 0:
                    dve.wait_ge(co_ev, i + 1)
                o = oa.rearrange("p (g j) d -> p j g d", g=2)
                dve.tensor_tensor(o, o, tmp.rearrange("p (j g) d -> p j g d", g=2), ALU.add).then_inc(o_ev, 1)
                dve.wait_ge(o_ev, 2 * i + br + 1)

            def compressed_soft(i):
                n = 4 * (i + 1)
                x0 = 927 - P * i
                dve.wait_ge(cs_ps, i + 1)
                if i >= 1:
                    dve.wait_ge(t_ps, number["compressed", i - 1] + 1)
                view = pc[:, :, 0:n].rearrange("p (j g) n -> p j g n", g=2)
                linked(dve.tensor_tensor(view, c.bank(7)[:, 0:256].rearrange("p (j g n) -> p j g n", j=4, g=2)[:, :, :, 0:n],
                                         c.bias[:, :, x0:x0 + 32 * (n - 1) + 1:32].rearrange("p (g j) n -> p j g n", g=2), ALU.add))
                linked(dve.tensor_reduce(cm, pc[:, :, 0:n], AX.X, ALU.max))
                linked(dve.tensor_scalar(cm, cm, -1e29, None, ALU.max))
                dve.tensor_tensor(pc[:, :, 0:n], pc[:, :, 0:n], cm.unsqueeze(2).to_broadcast([P, NH, n]), ALU.subtract).then_inc(cs_ev, 1)
                dve.wait_ge(ce_ev, i + 1)
                linked(dve.tensor_reduce(cs, pc[:, :, 0:n], AX.X, ALU.add))
                weighted(cs, cs, i, 0)
                dve.tensor_tensor(pc[:, :, 0:n], pc[:, :, 0:n], cs.unsqueeze(2).to_broadcast([P, NH, n]), ALU.mult).then_inc(cn_ev, 1)

            dve.memset(pc, 0.0).then_inc(zero_set, 1)
            dve.tensor_copy(edge, edge_f).then_inc(edge_set, 1)
            dve.tensor_copy(ident_b, c.ident).then_inc(edge_set, 1)
            dve.wait_ge(zero_set, 1)
            for s in range(NU + 3):
                i, r = s // 16, s % 16
                if s < NU:
                    soft(s)
                if 0 <= s - 2 < NU:
                    u = s - 2
                    n = min(4, unit(u)[5])
                    if u >= 2:
                        dve.wait_ge(v_ps, u - 1)
                    turned(("unit", u), pT[u % 2][:, 0:n, :], c.bank(4)[:, 0:n * P].rearrange("p (k q) -> p k q", k=n))
                if s < NU:
                    if r == 5:
                        compressed_soft(i)
                    if r == 6 and i >= 1:
                        turned(("result", i - 1), c.mix[:, 4:8, (i - 1) * P:i * P], c.bank(4).rearrange("p (m q) -> p m q", m=4))
                    if r == 8:
                        turned(("compressed", i), pcT, c.bank(4)[:, 0:256].rearrange("p (m q) -> p m q", m=2))
                    if r == 9:
                        dve.wait_ge(co_ps, i + 1)
                        if i >= 1:
                            dve.wait_ge(t_ps, number["result", i - 1] + 1)
                        dve.tensor_copy(oa.rearrange("p (g j) d -> p j g d", g=2),
                                        c.bank(7).rearrange("p (j g d) -> p j g d", j=4, g=2)).then_inc(co_ev, 1)
                if s >= 3 and (s - 3) % 8 == 7:
                    branch_result((s - 3) // 16, (s - 3) % 16 // 8)
            turned(("result", NP_TILES - 1), c.mix[:, 4:8, SEQ - P:SEQ], c.bank(4).rearrange("p (m q) -> p m q", m=4))
            dve.wait_ge(t_dve, len(turns))


def row_broadcast(ap, offset, n, rows=P):
    return bass.AP(tensor=ap.tensor, offset=offset, ap=[[0, rows], [1, n]])


def sample_rows(c, v):
    return bass.AP(tensor=c.mod_d.tensor, offset=6 * D + v * D, ap=[[6 * D, NB], [0, JS], [1, D]])


def block_output(c):
    nc, t, sem = c.nc, c.t, c.sem
    o = W_ + KT * D
    g1, sc2, sh2, lng, lnb, t0, t1, t2 = (c.view(o + D * n, D) for n in range(8))
    assert o + 8 * D <= MIX_
    c.x1 = c.view(X1_, NT, D)
    h2T = c.view(S1_, KT, P)
    rw = c.view(S1_ + D, KT, NE)
    c.rb = c.view(S1_ + D + P, NE)
    c.logits = c.view(S1_ + D + P + NE, NT, NE)
    st = c.view(S1_ + D + P + NE + NT * NE, 24)
    stats, mv, rstd, nmr = st[:, 0:12], st[:, 12:14], st[:, 16:17], st[:, 20:21]
    c.w_up_in = sem("w_up_in"); c.w_gate_in = sem("w_gate_in"); c.w_down_in = sem("w_down_in")
    vec_in, ln_in, vec2_in, r_in, h2_out = sem("vec_in"), sem("ln_in"), sem("vec2_in"), sem("r_in"), sem("h2_out")
    x_in6 = [sem(f"x6_in{i}") for i in range(NT)]
    (o_ps, o_ev, st_ready, sq, nrm, x1_a, x1_ready, h2_ready, t_ps, t_act, t_dve, r_ps, r_ev, link, rs_done) = (
        sem(n) for n in ("oo_ps", "oo_ev", "o_st", "o_sq", "o_nrm", "x1_a", "x1_ready", "h2_ready", "ot_ps", "ot_act",
                         "ot_dve", "r_ps", "r_ev", "o_link", "rs_done"))
    smp = NP_TILES

    with nc.Block() as block:
        @block.sync
        def _(sp):
            for v, dst in ((2, g1), (4, sc2), (3, sh2)):
                sp.dma_start(dst, row_broadcast(c.mod_d, v * D, D)).then_inc(vec_in, 16)
            for i in range(NT):
                T = tile_rows(i)
                src = t["x_prompt"][0, i * P:(i + 1) * P, :] if i < smp else t["x_sample"].rearrange("b j d -> (b j) d")
                sp.dma_start(c.x1[0:T, i, :], src).then_inc(x_in6[i], 16)
                if i == 0:
                    sp.dma_start(lng, row_broadcast(t["ln_g"], 0, D)).then_inc(ln_in, 16)
                    sp.dma_start(lnb, row_broadcast(t["ln_b"], 0, D)).then_inc(ln_in, 16)
                    sp.dma_start(rw, t["router_w"].rearrange("(k p) e -> p k e", p=P)).then_inc(r_in, 16)
                    sp.dma_start(c.rb, row_broadcast(t["router_b"], 0, NE)).then_inc(r_in, 16)
            sp.dma_start(c.view(CPH_, CONST_SHAPES["cph4"][1]), t["cph4"]).then_inc(c.cph_in, 16)
            wb = WB_[0]
            sp.dma_start(c.view(wb, KT, DE), t["moe_w_gate"][0, 0].rearrange("(k p) f -> p k f", p=P)).then_inc(c.w_gate_in, 16)
            sp.dma_start(c.view(wb + KT * DE, KT, DE), t["moe_w_up"][0, 0].rearrange("(k p) f -> p k f", p=P)).then_inc(c.w_up_in, 16)
            sp.dma_start(c.view(wb + 2 * KT * DE, 4, D), t["moe_w_down"][0, 0].rearrange("(k p) f -> p k f", p=P)).then_inc(c.w_down_in, 16)
            for i in range(NT):
                T = tile_rows(i)
                sp.wait_ge(h2_ready, i + 1)
                sp.dma_start(c.h2_d[i * P:i * P + T, :], t2[0:T, :]).then_inc(h2_out, 16)
                if i == smp - 1:
                    for v, dst in ((2, g1), (4, sc2), (3, sh2)):
                        sp.dma_start(dst[0:NS, :], sample_rows(c, v)).then_inc(vec2_in, 16)
            sp.wait_ge(h2_out, 16 * NT)

        @block.tensor
        def _(pe):
            pe.wait_ge(c.w_out_in, 16)

            def project(i):
                T = tile_rows(i)
                if i >= 2:
                    pe.wait_ge(o_ev, i - 1)
                for n in range(2):
                    for k in range(KT):
                        mm = pe.matmul(c.bank(2 * (i % 2) + n)[0:T, :], c.mix[:, k, i * P:i * P + T],
                                       c.w_out[:, k, n * 512:(n + 1) * 512], start=(k == 0), stop=(k == KT - 1))
                mm.then_inc(o_ps, 1)

            def route(i):
                T = tile_rows(i)
                pe.wait_ge(h2_ready, i + 1)
                if i >= 1:
                    pe.wait_ge(t_act, i)
                    pe.wait_ge(t_dve, i)
                for k in range(KT):
                    mm = pe.transpose(c.bank(4 + k // 4)[:, (k % 4) * P:(k % 4) * P + T], t2[0:T, k * P:(k + 1) * P], c.ident[0:T, 0:T])
                mm.then_inc(t_ps, 1)
                if i == 0:
                    pe.wait_ge(r_in, 32)
                pe.wait_ge(t_act, i + 1)
                pe.wait_ge(t_dve, i + 1)
                if i >= 1:
                    pe.wait_ge(r_ev, i)
                for k in range(KT):
                    mm = pe.matmul(c.bank(6)[0:T, 0:NE], h2T[:, k, 0:T], rw[:, k, :], start=(k == 0), stop=(k == KT - 1))
                mm.then_inc(r_ps, 1)

            for i in range(NT + 1):
                if i < NT:
                    project(i)
                if i >= 1:
                    route(i - 1)

        @block.scalar
        def _(act):
            def part(i):
                T = tile_rows(i)
                act.wait_ge(st_ready, i + 1)
                act.activation(rstd[0:T, :], mv[0:T, 1:2], ACT.Sqrt).then_inc(sq, 1)
                act.wait_ge(rs_done, i + 1)
                if i >= 1:
                    act.wait_ge(x1_a, i)
                act.activation(t1[0:T, :], t0[0:T, :], ACT.Identity, bias=nmr[0:T, :], scale=rstd[0:T, :]).then_inc(nrm, 1)

            def turned(i):
                T = tile_rows(i)
                act.wait_ge(t_ps, i + 1)
                if i >= 1:
                    act.wait_ge(r_ps, i)
                act.copy(h2T[:, 0:4, 0:T], c.bank(4).rearrange("p (k q) -> p k q", k=4)[:, :, 0:T]).then_inc(t_act, 1)

            for i in range(NT):
                part(i)
                turned(i)

        @block.gpsimd
        def _(pool):
            pool.wait_ge(ln_in, 32)
            for i in range(NT):
                T = tile_rows(i)
                pool.wait_ge(nrm, i + 1)
                pool.tensor_tensor(c.x1[0:T, i, :], t1[0:T, :], lng[0:T, :], ALU.mult).then_inc(x1_a, 1)
                pool.wait_ge(x1_a, i + 1)
                pool.tensor_tensor(c.x1[0:T, i, :], c.x1[0:T, i, :], lnb[0:T, :], ALU.add).then_inc(x1_ready, 1)
            pool.wait_ge(x1_ready, NT)

        @block.vector
        def _(dve):
            links = [0]

            def linked(ins):
                links[0] += 1
                ins.then_inc(link, 1)
                dve.wait_ge(link, links[0])

            dve.memset(c.logits, 0.0)
            dve.wait_ge(vec_in, 48)

            def residual(i):
                T = tile_rows(i)
                if i == smp:
                    dve.wait_ge(vec2_in, 48)
                dve.wait_ge(o_ps, i + 1)
                if i >= 1:
                    dve.wait_ge(nrm, i)
                b = (i % 2) * 1024
                dve.tensor_tensor(t0[0:T, :], c.psum[0:T, b:b + D], g1[0:T, :], ALU.mult).then_inc(o_ev, 1)
                dve.wait_ge(o_ev, i + 1)
                dve.wait_ge(x_in6[i], 16)
                linked(dve.scalar_tensor_tensor(out=t0[0:T, :], in0=c.x1[0:T, i, :], scalar=ALPHA, in1=t0[0:T, :],
                                                op0=ALU.mult, op1=ALU.add))
                for n in range(2):
                    a = dve.bn_stats(stats[0:T, 6 * n:6 * n + 6], t0[0:T, 512 * n:512 * n + 512])
                linked(a)
                linked(dve.bn_aggr(mv[0:T, :], stats[0:T, :]))
                dve.tensor_scalar(mv[0:T, 1:2], mv[0:T, 1:2], EPS, None, ALU.add).then_inc(st_ready, 1)
                dve.wait_ge(sq, i + 1)
                linked(dve.reciprocal(rstd[0:T, :], rstd[0:T, :]))
                dve.scalar_tensor_tensor(out=nmr[0:T, :], in0=mv[0:T, 0:1], scalar=-1.0, in1=rstd[0:T, :],
                                         op0=ALU.mult, op1=ALU.mult).then_inc(rs_done, 1)

            def modulate(i):
                T = tile_rows(i)
                dve.wait_ge(x1_ready, i + 1)
                if i >= 1:
                    dve.wait_ge(h2_out, 16 * i)
                    dve.wait_ge(t_ps, i)
                linked(dve.tensor_tensor(t2[0:T, :], c.x1[0:T, i, :], sc2[0:T, :], ALU.mult))
                dve.tensor_tensor(t2[0:T, :], t2[0:T, :], sh2[0:T, :], ALU.add).then_inc(h2_ready, 1)

            def turned(i):
                T = tile_rows(i)
                dve.wait_ge(t_ps, i + 1)
                if i >= 1:
                    dve.wait_ge(r_ps, i)
                dve.tensor_copy(h2T[:, 4:8, 0:T], c.bank(5).rearrange("p (k q) -> p k q", k=4)[:, :, 0:T]).then_inc(t_dve, 1)
                dve.wait_ge(r_ps, i + 1)
                dve.tensor_copy(c.logits[0:T, i, :], c.bank(6)[0:T, 0:NE]).then_inc(r_ev, 1)

            for i in range(NT):
                residual(i)
                modulate(i)
                turned(i)
            dve.wait_ge(r_ev, NT)


def block_routing(c):
    nc, t, sem = c.nc, c.t, c.sem
    off = [MIX_]

    def new(*dims):
        v = c.view(off[0], *dims)
        n = 1
        for d in dims:
            n *= d
        off[0] += n
        return v

    o = CPH_
    strict = c.view(o, P); o += P
    key16 = c.view(o, NE); o += NE
    key4 = c.view(o, 4); o += 4
    limits = c.view(o, 8); o += 8
    before = c.view(o, NE, NE); o += NE * NE
    slot_n = c.view(o, MAX_SLOTS); o += MAX_SLOTS
    tok_id = c.view(o, NT)
    s, grp, y, y2, tmp, oh1, oh2, m, dest = (new(NT, NE) for _ in range(9))
    a4, b4, c4, d4, m1g, e4, f4, m2g, gs, gk, gsel, pen = (new(NT, 4) for _ in range(12))
    r1, r2, w1, w2, ws = (new(NT) for _ in range(5))
    pref, tot = new(NT + 1, NE), new(NT, NE)
    ones, over, nb, starts, tri = new(P), new(NE, 8), new(NE), new(NE), new(NE, NE)
    table, exps, ends = new(MAX_SLOTS, NE), new(MAX_SLOTS), new(NE + 1)
    dests, ids = new(NT, 2), new(P)
    assert off[0] <= L_
    sg, cnt_ready, cnt_ps, dest_ready, moved, tok_in, ids_ps, tab_ready, link = (
        sem(n) for n in ("sig_ready", "cnt_ready", "cnt_ps", "dest_ready", "tok_moved", "tok_in", "ids_ps", "tab_ready", "r_link"))

    with nc.Block() as block:
        @block.scalar
        def _(act):
            act.activation(s, c.logits, ACT.Sigmoid).then_inc(sg, 1)

        @block.vector
        def _(dve):
            links = [0]

            def linked(ins):
                links[0] += 1
                ins.then_inc(link, 1)
                dve.wait_ge(link, links[0])

            def tt(out, a, b, op):
                linked(dve.tensor_tensor(out, a, b, op))

            def over_last(a, n):
                return a.unsqueeze(len(a.shape)).to_broadcast(list(a.shape) + [n])

            def first_max(out, val, key, red, n):
                linked(dve.tensor_reduce(red, val, AX.X, ALU.max))
                tt(out, val, over_last(red, n), ALU.is_equal)
                tt(out, out, key.unsqueeze(1).to_broadcast([P, NT, n]), ALU.mult)
                linked(dve.tensor_reduce(red, out, AX.X, ALU.max))
                tt(out, out, over_last(red, n), ALU.is_equal)

            linked(dve.memset(ones, 1.0))
            linked(dve.memset(m, 0.0))
            linked(dve.memset(pref, 0.0))
            dve.wait_ge(sg, 1)
            dve.wait_ge(c.cph_in, 48)
            tt(grp, s, c.rb.unsqueeze(1).to_broadcast([P, NT, NE]), ALU.add)
            x = grp.rearrange("p i (g e) -> p i g e", g=4)
            tt(a4, x[:, :, :, 0], x[:, :, :, 1], ALU.max)
            tt(b4, x[:, :, :, 0], x[:, :, :, 1], ALU.min)
            tt(c4, x[:, :, :, 2], x[:, :, :, 3], ALU.max)
            tt(d4, x[:, :, :, 2], x[:, :, :, 3], ALU.min)
            tt(m1g, a4, c4, ALU.max)
            tt(e4, a4, c4, ALU.min)
            tt(f4, b4, d4, ALU.max)
            tt(m2g, e4, f4, ALU.max)
            tt(gs, m1g, m2g, ALU.add)
            first_max(gsel, gs, key4, r1, 4)
            linked(dve.tensor_scalar(pen, gsel, -1.0, BIG, ALU.add, ALU.mult))
            tt(y.rearrange("p i (g e) -> p i g e", g=4), x, over_last(pen, 4), ALU.add)
            first_max(oh1, y, key16, r1, NE)
            linked(dve.scalar_tensor_tensor(out=y2.rearrange("p i e -> p (i e)"), in0=oh1.rearrange("p i e -> p (i e)"), scalar=-BIG,
                                            in1=y.rearrange("p i e -> p (i e)"), op0=ALU.mult, op1=ALU.add))
            first_max(oh2, y2, key16, r2, NE)
            tt(m[:, 0:NP_TILES], oh1[:, 0:NP_TILES], oh2[:, 0:NP_TILES], ALU.add)
            dve.tensor_tensor(m[0:NS, NP_TILES], oh1[0:NS, NP_TILES], oh2[0:NS, NP_TILES], ALU.add).then_inc(cnt_ready, 1)
            for w, oh in ((w1, oh1), (w2, oh2)):
                tt(tmp, s, oh, ALU.mult)
                linked(dve.tensor_reduce(w, tmp, AX.X, ALU.add))
            tt(ws, w1, w2, ALU.add)
            linked(dve.reciprocal(ws, ws))
            tt(c.xw[:, :, 0], w1, ws, ALU.mult)
            tt(c.xw[:, :, 1], w2, ws, ALU.mult)
            dve.wait_ge(cnt_ps, 1)
            linked(dve.tensor_copy(tot, c.bank(1)[:, 0:NT * NE].rearrange("p (i e) -> p i e", i=NT)))
            for i in range(NT):
                tt(pref[:, i + 1], pref[:, i], tot[:, i], ALU.add)
            tt(over, over_last(pref[:, NT], 8), limits.unsqueeze(1).to_broadcast([P, NE, 8]), ALU.is_gt)
            linked(dve.tensor_reduce(nb, over, AX.X, ALU.add))
            linked(dve.tensor_scalar(nb, nb, 1.0, None, ALU.add))
            tt(tri, before, nb.unsqueeze(1).to_broadcast([P, NE, NE]), ALU.mult)
            linked(dve.tensor_reduce(starts, tri, AX.X, ALU.add))
            tt(dest, c.bank(0)[:, 0:NT * NE].rearrange("p (i e) -> p i e", i=NT), pref[:, 0:NT], ALU.add)
            linked(dve.tensor_scalar(y[:, 0], starts, float(MB), None, ALU.mult))
            tt(dest, dest, y[:, 0].unsqueeze(1).to_broadcast([P, NT, NE]), ALU.add)
            for k, oh in enumerate((oh1, oh2)):
                tt(tmp, dest, oh, ALU.mult)
                linked(dve.tensor_reduce(dests[:, :, k], tmp, AX.X, ALU.add))
            dve.tensor_copy(c.dest_i[:, :, :], dests).then_inc(dest_ready, 1)
            tt(table[0:1], starts[0:1].unsqueeze(1).to_broadcast([1, MAX_SLOTS, NE]), over_last(slot_n[0:1], NE), ALU.is_le)
            linked(dve.tensor_reduce(exps[0:1], table[0:1], AX.X, ALU.add))
            linked(dve.tensor_scalar(exps[0:1], exps[0:1], -1.0, None, ALU.add))
            linked(dve.tensor_copy(c.slot_e[:, :], exps[0:1]))
            linked(dve.tensor_copy(ends[0:1, 0:NE], starts[0:1]))
            tt(ends[0:1, NE:NE + 1], starts[0:1, NE - 1:NE], nb[0:1, NE - 1:NE], ALU.add)
            dve.tensor_copy(c.start_e[:, :], ends[0:1]).then_inc(tab_ready, 1)
            dve.wait_ge(ids_ps, 1)
            dve.tensor_copy(c.ids_i[:, :], c.bank(2)[:, 0:MAX_SLOTS + 1]).then_inc(tab_ready, 1)
            dve.wait_ge(tab_ready, 2)

        @block.tensor
        def _(pe):
            pe.wait_ge(cnt_ready, 1)
            flat = m.rearrange("p i e -> p (i e)")
            pe.matmul(c.bank(0)[:, 0:NT * NE], strict, flat, start=True, stop=True)
            pe.matmul(c.bank(1)[:, 0:NT * NE], ones, flat, start=True, stop=True).then_inc(cnt_ps, 1)
            pe.wait_ge(tok_in, 16)
            n = MAX_SLOTS + 1
            pe.transpose(c.bank(2)[:, 0:n], ids[0:n, :], c.ident[0:n, 0:n]).then_inc(ids_ps, 1)

        @block.gpsimd
        def _(pool):
            pool.wait_ge(dest_ready, 1)
            for i in range(NT):
                T = tile_rows(i)
                for k in range(2):
                    pool.indirect_dma_start(c.tok_d, bass.IndirectOffsetOnAxis(ap=c.dest_i[0:T, i, k:k + 1], axis=0),
                                            tok_id[0:T, i:i + 1], None).then_inc(moved, 16)
            pool.wait_ge(moved, 16 * 2 * NT)
            pool.dma_start(ids[0:MAX_SLOTS + 1, :], c.tok_d.rearrange("(s p) o -> s (p o)", p=MB)).then_inc(tok_in, 16)
            pool.wait_ge(tok_in, 16)


def block_experts(c):
    nc, t, sem = c.nc, c.t, c.sem
    o = W_ + WB_LEN
    xb = c.view(o, D)
    xT = c.view(o + D, KT, P)
    sg = c.view(o + 2 * D, DE)
    a = c.view(o + 2 * D + DE, DE)
    aT = c.view(o + 3 * D, 4, P)
    y = c.view(o + 3 * D + DE, D)
    o += 4 * D + DE
    c.g2, c.g2s, c.lng2, c.lnb2 = (c.view(o + D * n, D) for n in range(4))
    assert o + 4 * D <= L_
    c.v9_in = sem("v9_in")
    (xb_in, x_ps, x_act, x_dve, gate_done, up_done, down_done, sil, a_ready, a_ps, a_ev, y_act, y_dve, y_out, id_set) = (
        sem(n) for n in ("xb_in", "x8_ps", "x8_act", "x8_dve", "gate8_done", "up8_done", "down8_done", "silu8", "a_ready",
                         "a_ps", "a_ev", "y_act", "y_dve", "y_out", "id_set"))
    fetches, reloads, fill_out, filled = (sem(n) for n in ("fetches", "reloads", "fill_out", "filled"))
    arena = c.arena

    def buffer_of(e):
        return (1 - e % 2) * L_

    def slots(eng):
        return eng.value_load(c.start_e[0:1, NE:NE + 1], min_val=NE, max_val=MAX_SLOTS)

    with nc.Block() as block:
        @block.sync
        def _(sp):
            parts = ((t["moe_w_gate"], c.w_gate_in, gate_done, KT, DE, 0),
                     (t["moe_w_up"], c.w_up_in, up_done, KT, DE, KT * DE),
                     (t["moe_w_down"], c.w_down_in, down_done, DE // P, D, 2 * KT * DE))
            for w, landed, used, nk, n, at in parts:
                sp.wait_ge(landed, 16)
                sp.dma_start(c.view(WB_[1] + at, nk, n), w[0, 1].rearrange("(k p) f -> p k f", p=P)).then_inc(landed, 16)
            for dst, src in ((c.g2, row_broadcast(c.mod_d, 5 * D, D)), (c.g2s[0:NS, :], sample_rows(c, 5)),
                             (c.lng2, row_broadcast(t["ln_g"], D, D)), (c.lnb2, row_broadcast(t["ln_b"], D, D))):
                sp.dma_start(dst, src).then_inc(c.v9_in, 16)
            with sp.Fori(2, NE) as e:
                begun = sp.value_load(c.start_e[0:1, bass.ds(e - 1, 1)], min_val=1, max_val=MAX_SLOTS)
                for w, landed, used, nk, n, at in parts:
                    sp.wait_ge(landed, e * 16)
                    sp.wait_ge(used, begun)
                    sp.sem_inc(reloads, 1)
                    sp.dma_start(arena[:, bass.ds(buffer_of(e) + at, nk * n)].rearrange("p (k f) -> p k f", k=nk),
                                 w[0, bass.ds(e, 1)].rearrange("a (k p) f -> p (a k) f", p=P)).then_inc(landed, 16)
            sp.wait_ge(c.v9_in, 64)
            with sp.Fori(0, slots(sp)):
                sp.sem_inc(fill_out, 16)
            with sp.Fori(slots(sp), MAX_SLOTS + 1) as n:
                sp.dma_start(c.y_d[bass.ds(n * MB, MB), :], c.lng2).then_inc(fill_out, 16)
                sp.wait_ge(fill_out, n * 16 + 16)
                sp.sem_inc(filled, 1)

        @block.gpsimd
        def _(pool):
            def fetch(s, first):
                ins = pool.tensor_copy(c.id_now[:, :], c.ids_i[:, 0:1] if first else c.ids_i[:, bass.ds(s, 1)])
                ins.then_inc(id_set, 1)
                pool.wait_ge(id_set, s + 1)
                pool.sem_inc(fetches, 1)
                pool.indirect_dma_start(xb, None, c.h2_d, bass.IndirectOffsetOnAxis(ap=c.id_now[:, 0:1], axis=0)).then_inc(xb_in, 16)

            fetch(0, True)
            with pool.Fori(1, slots(pool) + 1) as s:
                pool.wait_ge(x_ps, s)
                fetch(s, False)
            pool.wait_ge(xb_in, slots(pool) * 16 + 16)

        @block.tensor
        def _(pe):
            def turn_x(s):
                pe.wait_ge(xb_in, s * 16 + 16)
                for k in range(KT):
                    mm = pe.transpose(c.bank(4 + k // 4)[:, (k % 4) * P:(k % 4 + 1) * P], xb[:, k * P:(k + 1) * P], c.ident)
                mm.then_inc(x_ps, 1)

            def product(n, e, at, landed, done):
                pe.wait_ge(landed, e * 16 + 16)
                for k in range(KT):
                    mm = pe.matmul(c.bank(n), xT[:, k, :], arena[:, bass.ds(buffer_of(e) + at + k * DE, DE)],
                                   start=(k == 0), stop=(k == KT - 1))
                mm.then_inc(done, 1)

            def turn_a(n):
                pe.wait_ge(a_ready, n)
                for f in range(4):
                    mm = pe.transpose(c.bank(6)[:, f * P:(f + 1) * P], a[:, f * P:(f + 1) * P], c.ident)
                mm.then_inc(a_ps, 1)

            def down(n, e):
                pe.wait_ge(a_ev, n)
                pe.wait_ge(c.w_down_in, e * 16 + 16)
                pe.wait_ge(y_act, n)
                pe.wait_ge(y_dve, n)
                for m in range(2):
                    for f in range(4):
                        mm = pe.matmul(c.bank(2 + m), aT[:, f, :], arena[:, bass.ds(buffer_of(e) + 2 * KT * DE + f * D + m * 512, 512)],
                                       start=(f == 0), stop=(f == 3))
                mm.then_inc(down_done, 1)

            turn_x(0)
            pe.wait_ge(x_act, 1)
            pe.wait_ge(x_dve, 1)
            zero = pe.value_load(c.slot_e[0:1, 0:1], min_val=0, max_val=NE - 1)
            product(0, zero, 0, c.w_gate_in, gate_done)
            product(1, zero, KT * DE, c.w_up_in, up_done)
            turn_x(1)
            with pe.Fori(1, slots(pe)) as s:
                e = pe.value_load(c.slot_e[0:1, bass.ds(s, 1)], min_val=0, max_val=NE - 1)
                e_last = pe.value_load(c.slot_e[0:1, bass.ds(s - 1, 1)], min_val=0, max_val=NE - 1)
                pe.wait_ge(x_act, s + 1)
                pe.wait_ge(x_dve, s + 1)
                pe.wait_ge(sil, s)
                product(0, e, 0, c.w_gate_in, gate_done)
                turn_a(s)
                product(1, e, KT * DE, c.w_up_in, up_done)
                turn_x(s + 1)
                down(s, e_last)
            n = slots(pe)
            turn_a(n)
            down(n, pe.value_load(c.slot_e[0:1, bass.ds(n - 1, 1)], min_val=0, max_val=NE - 1))

        @block.scalar
        def _(act):
            def x_part(s, ahead):
                act.wait_ge(x_ps, s + 1)
                if ahead is not None:
                    act.wait_ge(up_done, ahead)
                act.copy(xT[:, 0:4, :].rearrange("p k q -> p (k q)"), c.bank(4)).then_inc(x_act, 1)

            def silu(s, before):
                act.wait_ge(gate_done, s + 1)
                if before is not None:
                    act.wait_ge(a_ready, before)
                act.activation(sg, c.bank(0), ACT.Silu).then_inc(sil, 1)

            def y_part(n):
                act.wait_ge(down_done, n)
                act.wait_ge(y_out, n * 16)
                act.copy(y[:, 0:512], c.bank(2)).then_inc(y_act, 1)
                act.wait_ge(y_act, n + 1)
                act.wait_ge(y_dve, n + 1)
                act.dma_start(c.y_d[bass.ds(n * MB - MB, MB), :], y).then_inc(y_out, 16)

            act.sem_inc(y_act, 1)
            act.sem_inc(y_out, 16)
            x_part(0, None)
            silu(0, None)
            x_part(1, 1)
            with act.Fori(1, slots(act)) as s:
                silu(s, s)
                x_part(s + 1, s + 1)
                y_part(s)
            n = slots(act)
            y_part(n)
            act.wait_ge(y_out, n * 16 + 16)
            act.sem_inc(y_act, 1)

        @block.vector
        def _(dve):
            def x_part(s, ahead):
                dve.wait_ge(x_ps, s + 1)
                if ahead is not None:
                    dve.wait_ge(up_done, ahead)
                dve.tensor_copy(xT[:, 4:8, :].rearrange("p k q -> p (k q)"), c.bank(5)).then_inc(x_dve, 1)

            def a_part(s, before):
                dve.wait_ge(sil, s + 1)
                dve.wait_ge(up_done, s + 1)
                if before is not None:
                    dve.wait_ge(a_ps, before)
                dve.tensor_tensor(a, c.bank(1), sg, ALU.mult).then_inc(a_ready, 1)

            def aT_part(n):
                dve.wait_ge(a_ps, n)
                dve.tensor_copy(aT.rearrange("p k q -> p (k q)"), c.bank(6)).then_inc(a_ev, 1)

            def y_part(n):
                dve.wait_ge(down_done, n)
                dve.wait_ge(y_out, n * 16)
                dve.tensor_copy(y[:, 512:], c.bank(3)).then_inc(y_dve, 1)

            dve.sem_inc(y_dve, 1)
            x_part(0, None)
            a_part(0, None)
            x_part(1, 1)
            with dve.Fori(1, slots(dve)) as s:
                aT_part(s)
                a_part(s, s)
                x_part(s + 1, s + 1)
                y_part(s)
            n = slots(dve)
            aT_part(n)
            y_part(n)


def block_combine(c):
    nc, t, sem = c.nc, c.t, c.sem
    RY = 2
    yy = [[c.view(W_ + 2 * D * s + D * k, D) for k in range(2)] for s in range(RY)]
    acc = [c.view(W_ + 4 * D + D * s, D) for s in range(2)]
    nrm = [c.view(W_ + 6 * D + D * s, D) for s in range(2)]
    st = c.view(S1_, 48)
    y_in = [sem(f"y9_in{s}") for s in range(RY)]
    done = [sem(f"y9_out{s}") for s in range(2)]
    first, used, st_ready, sq, rs_done, n_done, g_done, b_done, link = (
        sem(n) for n in ("y9_first", "y9_used", "s9_ready", "s9_sq", "s9_rs", "n9_done", "g9_done", "b9_done", "l9"))
    smp = NP_TILES

    with nc.Block() as block:
        @block.gpsimd
        def _(pool):
            def fetch(i):
                T = tile_rows(i)
                if i >= RY:
                    pool.wait_ge(used, i - RY + 1)
                for k in range(2):
                    pool.indirect_dma_start(yy[i % RY][k][0:T, :], None, c.y_d,
                                            bass.IndirectOffsetOnAxis(ap=c.dest_i[0:T, i, k:k + 1], axis=0)).then_inc(y_in[i % RY], 16)

            for i in range(NT):
                fetch(i)
                if i >= 1:
                    j = i - 1
                    pool.wait_ge(n_done, j + 1)
                    pool.tensor_tensor(nrm[j % 2], nrm[j % 2], c.lng2, ALU.mult).then_inc(g_done, 1)
            pool.wait_ge(n_done, NT)
            pool.tensor_tensor(nrm[smp % 2][0:NS, :], nrm[smp % 2][0:NS, :], c.lng2[0:NS, :], ALU.mult).then_inc(g_done, 1)

        @block.scalar
        def _(act):
            def start(i):
                T = tile_rows(i)
                act.wait_ge(y_in[i % RY], 32 * (i // RY + 1))
                if i >= 2:
                    act.wait_ge(n_done, i - 1)
                act.activation(acc[i % 2][0:T, :], yy[i % RY][0][0:T, :], ACT.Identity, scale=c.xw[0:T, i, 0:1]).then_inc(first, 1)

            start(0)
            for i in range(NT):
                T = tile_rows(i)
                if i + 1 < NT:
                    start(i + 1)
                q = st[:, 24 * (i % 2):24 * (i % 2) + 24]
                act.wait_ge(st_ready, i + 1)
                act.activation(q[0:T, 16:17], q[0:T, 13:14], ACT.Sqrt).then_inc(sq, 1)
                act.wait_ge(rs_done, i + 1)
                if i >= 2:
                    act.wait_ge(done[i % 2], 16 * (i // 2))
                act.activation(nrm[i % 2][0:T, :], acc[i % 2][0:T, :], ACT.Identity, bias=q[0:T, 20:21],
                               scale=q[0:T, 16:17]).then_inc(n_done, 1)

        @block.vector
        def _(dve):
            links = [0]

            def linked(ins):
                links[0] += 1
                ins.then_inc(link, 1)
                dve.wait_ge(link, links[0])

            def bias_add(i):
                T = tile_rows(i)
                dve.wait_ge(g_done, i + 1)
                dve.tensor_tensor(nrm[i % 2][0:T, :], nrm[i % 2][0:T, :], c.lnb2[0:T, :], ALU.add).then_inc(b_done, 1)

            dve.wait_ge(c.v9_in, 64)
            for i in range(NT):
                T = tile_rows(i)
                ac = acc[i % 2][0:T, :]
                q = st[0:T, 24 * (i % 2):24 * (i % 2) + 24]
                dve.wait_ge(first, i + 1)
                dve.scalar_tensor_tensor(out=ac, in0=yy[i % RY][1][0:T, :], scalar=c.xw[0:T, i, 1:2], in1=ac,
                                         op0=ALU.mult, op1=ALU.add).then_inc(used, 1)
                dve.wait_ge(used, i + 1)
                linked(dve.tensor_tensor(ac, ac, (c.g2 if i < smp else c.g2s)[0:T, :], ALU.mult))
                linked(dve.scalar_tensor_tensor(out=ac, in0=c.x1[0:T, i, :], scalar=ALPHA, in1=ac, op0=ALU.mult, op1=ALU.add))
                for n in range(2):
                    a = dve.bn_stats(q[:, 6 * n:6 * n + 6], ac[:, 512 * n:512 * n + 512])
                linked(a)
                linked(dve.bn_aggr(q[:, 12:14], q[:, 0:12]))
                dve.tensor_scalar(q[:, 13:14], q[:, 13:14], EPS, None, ALU.add).then_inc(st_ready, 1)
                if i >= 1:
                    bias_add(i - 1)
                dve.wait_ge(sq, i + 1)
                linked(dve.reciprocal(q[:, 16:17], q[:, 16:17]))
                dve.scalar_tensor_tensor(out=q[:, 20:21], in0=q[:, 12:13], scalar=-1.0, in1=q[:, 16:17],
                                         op0=ALU.mult, op1=ALU.mult).then_inc(rs_done, 1)
            bias_add(smp)

        @block.sync
        def _(sp):
            for i in range(NT):
                T = tile_rows(i)
                sp.wait_ge(b_done, i + 1)
                dst = t["o_y_p"][0, i * P:(i + 1) * P, :] if i < smp else t["o_y_s"].rearrange("b j d -> (b j) d")
                sp.dma_start(dst, nrm[i % 2][0:T, :]).then_inc(done[i % 2], 16)
            sp.wait_ge(c.out_done, c.out_total)
            for s in range(2):
                sp.wait_ge(done[s], 16 * ((NT - s + 1) // 2))


BLOCKS = (block_modulation, block_projection, block_compression, block_decode_attention,
          retire_early_semaphores, block_prompt_attention,
          block_output, block_routing, block_experts, block_combine)


CONST_INPUTS = ("ident", "onehot", "cph1", "cph2", "cph3", "cph4")
INPUTS = ("x_prompt", "x_sample", "cache_cmp_kv", "cache_sel_kv", "state_win_kv", "state_pool", "page_table",
          "c_prompt", "c_sample", "w_in", "w_out", "pool_w", "pool_scale", "sgu_ln_g", "sgu_ln_b", "sgu_w", "sgu_b",
          "cmp_pe", "cmp_w1", "cmp_w2", "rel_bias", "w_mod", "b_mod", "ln_g", "ln_b", "router_w", "router_b",
          "moe_w_gate", "moe_w_up", "moe_w_down")
OUTPUTS = (("o_y_p", (1, SEQ, D)), ("o_y_s", (NB, JS, D)),
           ("o_cmp_p", (1, 1, SEQ, 2, NKV, HD)), ("o_cmp_s", (1, NB, JS, 2, NKV, HD)),
           ("o_sel_p", (1, 1, SEQ, 2, NKV, HD)), ("o_sel_s", (1, NB, JS, 2, NKV, HD)),
           ("o_win_p", (1, 1, 512, 2, NKV, HD)), ("o_win_s", (1, NB, PAST, 2, NKV, HD)),
           ("o_pool_p", (1, 1, PBUF, PW)), ("o_pool_s", (1, NB, PBUF, PW)), ("o_sgu_s", (1, NB, JS, PW)))


def build_program(nc, t):
    with ExitStack() as ctx:
        c = setup(nc, ctx, t)
        for part in BLOCKS:
            part(c)


def kernel(**inputs):
    import concourse.bacc as bacc
    from concourse.bass_utils import run_bass_kernel_spmd

    nc = bacc.Bacc("TRN2", target_bir_lowering=False, num_devices=1)
    arrays, t = {}, {}
    made = constants()
    for name in INPUTS + CONST_INPUTS:
        a = np.ascontiguousarray(made[name] if name in made else inputs[name])
        arrays[f"in_{name}"] = a
        t[name] = nc.dram_tensor(f"in_{name}", a.shape, mybir.dt.from_np(a.dtype), kind="ExternalInput").ap()
    for name, shape in OUTPUTS:
        t[name] = nc.dram_tensor(f"out_{name}", shape, F32, kind="ExternalOutput").ap()
    build_program(nc, t)
    r = run_bass_kernel_spmd(nc, [arrays], core_ids=[0])
    return tuple(r.results[0][f"out_{name}"] for name, _ in OUTPUTS)
```

```python
import math
from contextlib import ExitStack

import numpy as np
import concourse.bass as bass
from concourse import mybir

F32, F32R, BF16, I32 = mybir.dt.float32, mybir.dt.float32r, mybir.dt.bfloat16, mybir.dt.int32
ALU, ACT, AX = mybir.AluOpType, mybir.ActivationFunctionType, mybir.AxisListType

P = 128
D = 1024
KT = D // P
SEQ, NB, JS = 1024, 8, 8
NS = NB * JS
NP_TILES = SEQ // P
NT = NP_TILES + 1
TOK = SEQ + NS
PAST, PAGE = 256, 128
NPAGE = PAST // PAGE
PW = 256
WINDOWS = (2, 4, 8, 16)
PBUF = 15
HD, NKV, REP, NH = 64, 2, 4, 8
KVW = 2 * NKV * HD
Q0 = 3 * PW
KV0 = Q0 + NH * HD
G0 = KV0 + 3 * KVW
IN_W = G0 + 3 * NH
CB, NC_P, NC_S = 32, SEQ // 32, PAST // 32
WIN_TILES = 4
NBUCK = 32
TABW = 1152
NE, DE, MB = 16, 512, 128
ALPHA = 2.0 ** 0.25
EPS = 1e-5
NEG = -1e30
BIG = 1e30
MAX_SLOTS = (2 * TOK + NE * (MB - 1) + NE - 1) // MB
SCALE = HD ** -0.5

W_, MIX_ = 0, KT * IN_W
L_ = MIX_ + KT * TOK
QT_ = L_ + NH * D
KT_ = QT_ + 4 * TOK
VS_ = KT_ + 2 * TOK
KVR_ = VS_ + NT * 256
XH_ = KVR_ + 2 * 3 * KVW
S1_ = XH_ + 3 * D
CPH_ = S1_ + 2816
END_ = CPH_ + 2304
KEEP = 640
ZR_ = MIX_ + 4 * TOK
PART = KT * DE
X1_ = L_ + 3 * PART


def tile_rows(i):
    return P if i < NP_TILES else NS


def bucket(dist):
    n = np.maximum(dist, 0)
    half = NBUCK // 2
    nf = np.maximum(n, 1).astype(np.float32)
    large = half + (np.log(nf / np.float32(half)) / np.float32(math.log(128 / half)) * np.float32(NBUCK - half)).astype(np.int32)
    return np.where(n < half, n, np.minimum(large, NBUCK - 1))


def constants():
    c = {}
    r = np.arange(P)
    ident = np.eye(P)
    c["ident"] = ident
    dist = 1023 - np.arange(TABW)
    oh = np.zeros((NBUCK + 1, TABW))
    ok = dist >= 0
    oh[bucket(dist)[ok], np.arange(TABW)[ok]] = 1
    oh[NBUCK, ~ok] = 1
    c["onehot"] = oh
    first, same, prev = (np.zeros((P, 4, P)) for _ in range(3))
    buf, new = np.zeros((P, 4, NS)), np.zeros((P, 4, NS))
    for g, w in enumerate(WINDOWS):
        for t in range(P):
            lo = t - w + 1
            for s in range(lo, t + 1):
                if s >= 0:
                    first[s, g, t] += 1 / min(w, t + 1)
                    same[s, g, t] += 1 / w
                else:
                    prev[P + s, g, t] += 1 / w
            first[t, g, t] -= 1
            same[t, g, t] -= 1
        for b in range(NB):
            for j in range(JS):
                for s in range(PBUF + j - w + 1, PBUF + j + 1):
                    if s < PBUF:
                        buf[b * PBUF + s, g, b * JS + j] += 1 / w
                    else:
                        new[b * JS + s - PBUF, g, b * JS + j] += 1 / w
                new[b * JS + j, g, b * JS + j] -= 1
    tril = (r[:, None] <= r[None, :]).astype(float)
    s = np.arange(P) % NS
    blk = np.zeros((P, NS))
    blk[:NS] = (s[:NS, None] // JS == s[None, :NS] // JS)
    rep = np.zeros((P, NS))
    rep[:JS] = np.arange(JS)[:, None] == np.arange(NS)[None, :] % JS
    c["cph1"] = np.concatenate([a.reshape(P, -1) for a in (first, same, prev, tril, buf, new, blk, rep)], 1)
    b4, rr, jj = r // 32, r % 32 // JS, r % JS
    selg = np.zeros((P, 2, P))
    for half in range(2):
        selg[(4 * half + b4) * JS + jj, half, r] = 1
    rowm = np.zeros((P, 2, NH, 3))
    for g in range(2):
        rowm[r, g, 4 * g + rr, :] = 1
    selr = np.zeros((P, 4, P))
    for q in range(4):
        selr[jj, q, r] = (rr == q)
    mine = np.zeros((P, 2, NB, JS))
    for half in range(2):
        mine[r, half, 4 * half + b4, :] = 1
    c["cph2"] = np.concatenate([a.reshape(P, -1) for a in (selg, rowm, selr, mine, (1 - mine) * NEG)], 1)
    c["cph3"] = np.where(r[None, :] <= r[:, None], NEG, 0.0)
    strict = (r[:, None] < r[None, :]).astype(float)
    cols = [strict, np.tile(NE - np.arange(NE), (P, 1)), np.tile(4 - np.arange(4), (P, 1)),
            np.tile(MB * np.arange(1, 9), (P, 1)),
            np.tile((np.arange(NE)[:, None] > np.arange(NE)[None, :]).reshape(1, -1), (P, 1)),
            np.tile(np.arange(MAX_SLOTS + 1), (P, 1)), r[:, None] + P * np.arange(NT)[None, :], np.tile(r, (P, 1))]
    c["cph4"] = np.concatenate(cols, 1)
    return {k: np.ascontiguousarray(v, np.float32) for k, v in c.items()}


CONST_SHAPES = {"ident": (P, P), "onehot": (NBUCK + 1, TABW), "cph1": (P, 12 * P + P + 4 * 2 * NS + 2 * NS),
                "cph2": (P, 2 * P + 48 + 4 * P + 4 * NS), "cph3": (P, P),
                "cph4": (P, P + NE + 4 + 8 + NE * NE + MAX_SLOTS + 1 + NT + P)}


class Chip:
    pass


def allocate(c, drop, *tensors):
    for _ in range(drop):
        c.stacks.pop().close()
    c.stacks.append(ExitStack())
    return [c.stacks[-1].enter_context(c.nc.sbuf_tensor(name, [P, n], kind)) for name, n, kind in tensors]


def memory_mixer(c):
    c.low, = allocate(c, 0, ("low", L_, F32))
    c.high, = allocate(c, 0, ("high", END_ - L_, F32))


def memory_output(c):
    c.wo_parts, c.mix_parts, c.high = allocate(
        c, 1, ("wo_parts", 2 * KT * D, F32R), ("mix_parts", 4 * D, F32R), ("high_2", 6 * D + P, F32))


def memory_routing(c):
    c.raw, = allocate(c, 2, ("raw", 3 * PART, F32))
    c.scratch, = allocate(c, 0, ("scratch", 9216, F32))


def memory_experts(c):
    c.w_hi, c.w_lo, c.x_parts, c.a_parts, c.work = allocate(
        c, 1, ("w_hi", 4 * PART, F32R), ("w_lo", 4 * PART, F32R), ("x_parts", 2 * D, F32R), ("a_parts", 2 * DE, F32R),
        ("work", 2 * D + 2 * DE, F32))


def memory_combine(c):
    c.low, c.high = allocate(c, 2, ("low_2", L_, F32), ("high_3", END_ - L_, F32))


def setup(nc, ctx, t):
    c = Chip()
    c.nc, c.t = nc, t
    c.keep = ctx.enter_context(nc.sbuf_tensor("keep", [P, KEEP], F32))
    c.psum = ctx.enter_context(nc.psum_tensor("psum", [P, 8 * 512], F32))
    c.sem = lambda name: ctx.enter_context(nc.semaphore(name))
    c.early = []

    def early_sem(name):
        c.early.append(nc.alloc_semaphore(name))
        return c.early[-1]

    c.early_sem = early_sem

    def view(off, *dims):
        n = 1
        for d in dims:
            n *= d
        assert off >= L_ or off + n <= L_
        a = c.low[:, off:off + n] if off < L_ else c.high[:, off - L_:off - L_ + n]
        names = "abcd"[:len(dims)]
        if len(dims) == 1:
            return a
        lhs = " ".join(names)
        return a.rearrange(f"p ({lhs}) -> p {lhs}", **{k: d for k, d in zip(names, dims)})

    c.view = view
    c.bank = lambda b, n=512: c.psum[:, b * 512:b * 512 + n]
    keep = c.keep
    c.ident = keep[:, 0:P]
    c.gates = keep[:, P:P + 216].rearrange("p (a b) -> p a b", a=NT)
    c.xw = keep[:, P + 216:P + 234].rearrange("p (a b) -> p a b", a=NT)
    c.misc = keep[:, P + 234:KEEP]
    c.page = ctx.enter_context(nc.sbuf_tensor("page", [1, NB * NPAGE], I32))
    c.dest_i = ctx.enter_context(nc.sbuf_tensor("dest_i", [P, NT, 2], I32))
    c.dest_y = ctx.enter_context(nc.sbuf_tensor("dest_y", [P, NT, 2], I32))
    c.ids_i = ctx.enter_context(nc.sbuf_tensor("ids_i", [P, MAX_SLOTS + 1], I32))
    c.id_now = ctx.enter_context(nc.sbuf_tensor("id_now", [P, 1], I32))
    c.slot_e = ctx.enter_context(nc.sbuf_tensor("slot_e", [1, MAX_SLOTS], I32))
    c.start_e = ctx.enter_context(nc.sbuf_tensor("start_e", [1, NE + 1], I32))
    c.stacks = []
    memory_mixer(c)
    c.mod_d = nc.dram_tensor("mod_d", (9, 6 * D), F32).ap()
    c.tab_d = nc.dram_tensor("tab_d", (NH, P, TABW), F32).ap()
    c.h2_d = nc.dram_tensor("h2_d", (TOK, D), F32).ap()
    c.y_d = nc.dram_tensor("y_d", ((MAX_SLOTS + 2) * MB, D), F32).ap()
    c.x1_d = nc.dram_tensor("x1_d", (TOK, D), F32).ap()
    c.w_in = view(W_, KT, IN_W)
    c.mix = view(MIX_, KT, TOK)
    c.bias = view(L_, NH, D)
    c.qT = view(QT_, 4, TOK)
    c.kT = view(KT_, 2, TOK)
    c.vs = view(VS_, NT, 2, 2, HD)
    c.modw = [view(L_ + 4096 * s, 4, D) for s in range(2)]
    c.mods = view(ZR_ + 1792, D)
    c.modb = view(ZR_ + 1792 + D, D)
    c.mods_1, c.modb_1 = view(XH_ + 2 * D, D), view(XH_ + D, D)
    c.cT = view(S1_ + 2690, KT, 9)
    c.modT = c.misc[:, 0:144].rearrange("p (a b) -> p a b", a=2 * KT)
    c.modw_in = [c.sem(f"modw_in{s}") for s in range(2)]
    c.modb_in, c.mod_half_done = c.sem("modb_in"), c.sem("mod_half_done")
    c.mods_ready, c.mods_out = c.sem("mods_ready"), c.sem("mods_out")
    c.w_in_in = [c.sem(f"w_in_in{n}") for n in range(5)]
    c.x_in, c.out_done, c.cph_in, c.page_in = c.sem("x_in"), c.sem("out_done"), c.sem("cph_in"), c.sem("page_in")
    c.out_total = 0
    c.raw_in, c.lo_done, c.reloads = [c.sem(f"raw_in{p}") for p in range(3)], [c.sem(f"lo_done{p}") for p in range(3)], c.sem("reloads")
    o = 0
    c.pool_w = view(S1_, 4, HD); o += 4 * HD
    c.pool_sc = view(S1_ + o, 2); o += 2
    c.sgu_wT = view(S1_ + o, 4, P); o += 4 * P
    c.sgu_wS = view(S1_ + o, 4, NS); o += 4 * NS
    c.sgu_b = view(S1_ + o, 4); o += 4
    c.sgu_bS = view(S1_ + o, 4); o += 4
    c.lnv_g = view(S1_ + o, PW); o += PW
    c.lnv_b = view(S1_ + o, PW); o += PW
    c.vn = [view(S1_ + o + PW * s, PW) for s in range(2)]; o += 2 * PW
    c.sgo = view(S1_ + o, PW); o += PW
    c.pbuf = view(S1_ + o, PW); o += PW
    c.st = view(S1_ + o, 24); o += 24
    assert o <= 2690 and 2690 + 72 <= 2816, o
    return c


def mod_load(c, sp, n):
    v, hh = n // 2, n % 2
    if n >= 2:
        sp.wait_ge(c.mod_half_done, n - 1)
    src = c.t["w_mod"][0].rearrange("(k p) n -> p k n", p=P)[:, 4 * hh:4 * hh + 4, v * D:(v + 1) * D]
    sp.dma_start(c.modw[n % 2], src).then_inc(c.modw_in[n % 2], 16)


def mod_products(c, pe, n):
    v, hh = n // 2, n % 2
    pe.wait_ge(c.modw_in[n % 2], 16 * (n // 2 + 1))
    if hh == 0 and v >= 1:
        pe.wait_ge(c.mods_ready, v)
    for k in range(4):
        for m in range(2):
            mm = pe.matmul(c.bank(4 + m)[0:9, :], c.cT[:, 4 * hh + k, :], c.modw[n % 2][:, k, m * 512:(m + 1) * 512],
                           start=(hh == 0 and k == 0), stop=(hh == 1 and k == 3))
    mm.then_inc(c.mod_half_done, 1)


def mod_vector(c, dve, v):
    dve.wait_ge(c.mod_half_done, 2 * v + 2)
    dve.wait_ge(c.modb_in, 16 * max(v + 1, 2))
    if v >= 3:
        dve.wait_ge(c.mods_out, 16 * (v - 2))
    one = 0.0 if v in (0, 3) else 1.0
    mods, modb = (c.mods_1, c.modb_1) if v == 1 else (c.mods, c.modb)
    dve.scalar_tensor_tensor(out=mods[0:9, :], in0=c.psum[0:9, 2048:3072], scalar=one, in1=modb[0:9, :],
                             op0=ALU.add, op1=ALU.add).then_inc(c.mods_ready, 1)


def mod_bias_load(c, pool, v):
    if v >= 2:
        pool.wait_ge(c.mods_ready, v)
    src = bass.AP(tensor=c.t["b_mod"].tensor, offset=v * D, ap=[[0, 9], [1, D]])
    pool.dma_start((c.modb_1 if v == 1 else c.modb)[0:9, :], src).then_inc(c.modb_in, 16)


def mod_store(c, pool, v):
    pool.wait_ge(c.mods_ready, v + 1)
    pool.dma_start(c.mod_d[:, v * D:(v + 1) * D], c.mods[0:9, :]).then_inc(c.mods_out, 16)


W_CHUNKS = ((0, 512), (512, 256), (KV0, 512), (KV0 + 512, 280))


def block_modulation(c):
    nc, t, sem = c.nc, c.t, c.early_sem
    c_n = c.view(XH_, D)
    onehot = c.view(QT_, TABW)
    relb = c.view(QT_ + TABW, NH)
    tab = c.tab = c.view(VS_ + 1152, TABW)
    sgu_n = c.view(KVR_, 4, P)
    sgb_n = c.view(KVR_ + 512, P)
    c1 = c.view(CPH_, 2304)
    trilT, blk64 = c1[:, 1536:1664], c1[:, 1664 + 512:1664 + 512 + 64]
    rep8 = c1[:, 1664 + 576:1664 + 640]
    c_in, ident_in, small_in = sem("c_in"), sem("ident_in"), sem("small_in")
    silu_done, cT_ps, cT_done = sem("silu_done"), sem("cT_ps"), sem("cT_done")
    tab_ps, tab_done, c.tab_out, neg_set = sem("tab_ps"), sem("tab_done"), sem("tab_out"), sem("neg_set")
    sgu_ps, sgu_done, sguS_ps, modT_ps, modT_done, sguS_done = (sem(n) for n in (
        "sgu_ps", "sgu_done", "sguS_ps", "modT_ps", "modT_done", "sguS_done"))
    c.cph1 = c1

    with nc.Block() as block:
        @block.sync
        def _(sp):
            sp.dma_start(c_n[0:1, :], t["c_prompt"]).then_inc(c_in, 16)
            sp.dma_start(c_n[1:9, :], t["c_sample"]).then_inc(c_in, 16)
            sp.dma_start(c.ident, t["ident"]).then_inc(ident_in, 16)
            mod_load(c, sp, 0)
            mod_load(c, sp, 1)
            for dst, src in (
                (onehot[0:NBUCK + 1, :], t["onehot"]),
                (relb[0:NBUCK, :], t["rel_bias"]),
                (c1, t["cph1"]),
                (sgu_n, t["sgu_w"][0].rearrange("g i j -> i g j")),
                (sgb_n[0:4, :], t["sgu_b"][0]),
                (c.pool_w[0:HD, :, :], t["pool_w"][0].rearrange("g c d -> c g d")),
                (c.pool_sc, bass.AP(tensor=t["pool_scale"].tensor, offset=0, ap=[[1, P], [P, 2]])),
                (c.lnv_g, bass.AP(tensor=t["sgu_ln_g"].tensor, offset=0, ap=[[0, P], [1, PW]])),
                (c.lnv_b, bass.AP(tensor=t["sgu_ln_b"].tensor, offset=0, ap=[[0, P], [1, PW]])),
                (c.pbuf[0:NB * PBUF, :], t["state_pool"][0].rearrange("b r w -> (b r) w")),
                (c.page[0:1, :], t["page_table"].rearrange("(a b) q -> a (b q)", a=1)),
            ):
                sp.dma_start(dst, src, allow_slow_non_contiguous=dst is c.pool_sc).then_inc(small_in, 16)
            sp.wait_ge(silu_done, 1)
            sp.wait_ge(cT_ps, 1)
            sp.dma_start(c.view(XH_, D)[:, :], t["x_prompt"][0, 0:P, :]).then_inc(c.x_in, 16)
            mod_load(c, sp, 2)
            mod_load(c, sp, 3)
            src = t["w_in"][0].rearrange("(k p) n -> p k n", p=P)
            for n, (a, w) in enumerate(W_CHUNKS):
                sp.dma_start(c.w_in[:, :, a:a + w], src[:, :, a:a + w]).then_inc(c.w_in_in[n], 16)
            for j in range(REP):
                for g in range(NKV):
                    to, at = Q0 + P * j + HD * g, Q0 + HD * (REP * g + j)
                    sp.dma_start(c.w_in[:, :, to:to + HD], src[:, :, at:at + HD]).then_inc(c.w_in_in[4], 16)
            sp.wait_ge(tab_done, 1)

        @block.gpsimd
        def _(pool):
            mod_bias_load(c, pool, 0)
            mod_bias_load(c, pool, 1)

        @block.scalar
        def _(act):
            act.wait_ge(c_in, 32)
            act.activation(c_n[0:9, :], c_n[0:9, :], ACT.Silu).then_inc(silu_done, 1)

        @block.tensor
        def _(pe):
            pe.wait_ge(ident_in, 16)
            pe.wait_ge(silu_done, 1)
            for k in range(KT):
                mm = pe.transpose(c.bank(7)[:, 9 * k:9 * k + 9], c_n[0:9, k * P:(k + 1) * P], c.ident[0:9, 0:9])
            mm.then_inc(cT_ps, 1)
            pe.wait_ge(cT_done, 1)
            mod_products(c, pe, 0)
            pe.wait_ge(small_in, 16 * 11)
            pe.wait_ge(neg_set, 1)
            for n in range(3):
                w = TABW // 3
                mm = pe.matmul(c.bank(n)[0:NH, 0:w], relb[0:NBUCK + 1, :], onehot[0:NBUCK + 1, n * w:(n + 1) * w],
                               start=True, stop=True)
            mm.then_inc(tab_ps, 1)
            for g in range(4):
                pe.transpose(c.bank(3)[:, g * P:(g + 1) * P], sgu_n[:, g, :], c.ident)
            pe.transpose(c.bank(6)[:, 200:204], sgb_n[0:4, :], c.ident[0:4, 0:4]).then_inc(sgu_ps, 1)
            mod_products(c, pe, 1)
            pe.wait_ge(sgu_done, 2)
            for g in range(4):
                pe.matmul(c.bank(7)[0:NS, g * NS:(g + 1) * NS], rep8[0:JS, :],
                          c.sgu_wT[0:JS, g, 0:JS].unsqueeze(1).to_broadcast([JS, NB, JS]), start=True, stop=True)
            pe.matmul(c.bank(7)[0:NS, 256:260], rep8[0:JS, :], c.sgu_b[0:JS, :], start=True, stop=True).then_inc(sguS_ps, 1)
            mod_products(c, pe, 2)
            mod_products(c, pe, 3)
            for v in range(2):
                pe.wait_ge(c.mods_ready, v + 1)
                for k in range(KT):
                    o = (v * KT + k) * 9
                    mm = pe.transpose(c.bank(6)[:, o:o + 9], (c.mods, c.mods_1)[v][0:9, k * P:(k + 1) * P], c.ident[0:9, 0:9])
                mm.then_inc(modT_ps, 1)

        @block.vector
        def _(dve):
            dve.memset(relb[NBUCK:NBUCK + 1, :], NEG).then_inc(neg_set, 1)
            dve.wait_ge(cT_ps, 1)
            dve.tensor_copy(c.cT, c.bank(7, 72).rearrange("p (k a) -> p k a", k=KT)).then_inc(cT_done, 1)
            dve.wait_ge(tab_ps, 1)
            w = TABW // 3
            dve.tensor_copy(tab[0:NH, :].rearrange("p (a b) -> p a b", a=3),
                            c.psum[0:NH, 0:1536].rearrange("p (a b) -> p a b", a=3)[:, :, 0:w]).then_inc(tab_done, 1)
            dve.wait_ge(sgu_ps, 1)
            dve.tensor_tensor(c.sgu_wT, c.bank(3).rearrange("p (g i) -> p g i", g=4),
                              trilT.unsqueeze(1).to_broadcast([P, 4, P]), ALU.mult).then_inc(sgu_done, 1)
            dve.tensor_copy(c.sgu_b, c.bank(6)[:, 200:204]).then_inc(sgu_done, 1)
            dve.wait_ge(sguS_ps, 1)
            dve.tensor_tensor(c.sgu_wS[0:NS, :, :], c.bank(7)[0:NS, 0:256].rearrange("p (g i) -> p g i", g=4),
                              blk64[0:NS, :].unsqueeze(1).to_broadcast([NS, 4, NS]), ALU.mult).then_inc(sguS_done, 1)
            dve.tensor_copy(c.sgu_bS[0:NS, :], c.bank(7)[0:NS, 256:260]).then_inc(sguS_done, 1)
            mod_vector(c, dve, 0)
            dve.wait_ge(modT_ps, 1)
            dve.tensor_copy(c.modT[:, 0:KT, :], c.bank(6)[:, 0:72].rearrange("p (a b) -> p a b", a=KT)).then_inc(modT_done, 1)
            mod_vector(c, dve, 1)
            dve.wait_ge(modT_ps, 2)
            dve.tensor_copy(c.modT[:, KT:, :], c.bank(6)[:, 72:144].rearrange("p (a b) -> p a b", a=KT)).then_inc(modT_done, 1)
            dve.wait_ge(modT_done, 2)
            dve.wait_ge(sguS_done, 2)


def block_projection(c):
    nc, t, sem = c.nc, c.t, c.early_sem
    x = c.view(XH_, D)
    hT = [c.view(XH_ + D * (1 + s), KT, P) for s in range(2)]
    zp = [c.view(ZR_ + PW * s, PW) for s in range(3)]
    zuv = [c.view(ZR_ + 3 * PW + 2 * PW * s, 2, PW) for s in range(2)]
    kv = [c.view(KVR_ + 3 * KVW * s, 3, 2, P) for s in range(2)]
    dT = c.view(ZR_ + 3840, 4, P)
    first, same, prev = (c.cph1[:, 512 * n:512 * n + 512].rearrange("p (g t) -> p g t", g=4) for n in range(3))
    pb_new = c.cph1[:, 1664 + 256:1664 + 512].rearrange("p (g t) -> p g t", g=4)
    pb_buf = c.cph1[:, 1664:1664 + 256].rearrange("p (g t) -> p g t", g=4)
    stats, mv, rstd = c.st[:, 0:6], c.st[:, 8:10], c.st[:, 12:13]
    (xT_ready, h_act, h_dve, z_ready, z_act, z_dve, q_done, q_evac, kT_ready, kT_evac, pd_ready, pd_evac, po_ready,
     po_evac, sg_ready, sgo_ready, so_ready, so_evac, vn_ready, st_ready, sqrt_done, v_copied, sg_tmp,
     link) = (sem(n) for n in (
         "xT_ready", "h_act", "h_dve", "z_ready", "z_act", "z_dve", "q_done", "q_evac", "kT_ready", "kT_evac",
         "pd_ready", "pd_evac", "po_ready", "po_evac", "sg_ready", "sgo_ready", "so_ready", "so_evac", "vn_ready",
         "st_ready", "sqrt_done", "v_copied", "sg_tmp", "vn_link"))
    kv_out = [sem(f"kv_out{s}") for s in range(2)]
    p_out, sgv_out, rows_out = sem("p_out"), sem("sgv_out"), sem("rows_out")
    c.bias_in = c.sem("bias_in")
    smp = NP_TILES
    n_kv_out = [0, 0]

    with nc.Block() as block:
        @block.sync
        def _(sp):
            for i in range(1, NT):
                sp.wait_ge(xT_ready, i)
                T = tile_rows(i)
                src = t["x_prompt"][0, i * P:(i + 1) * P, :] if i < smp else t["x_sample"].rearrange("b j d -> (b j) d")
                sp.dma_start(x[0:T, :], src).then_inc(c.x_in, 16)
                if i + 3 <= 11:
                    mod_load(c, sp, i + 3)
                if i == 1:
                    sp.dma_start(c.tab_d, c.tab[0:NH, :].unsqueeze(1).to_broadcast([NH, P, TABW])).then_inc(c.tab_out, 16)
            sp.wait_ge(c.mod_half_done, 12)
            src = bass.AP(tensor=c.tab_d.tensor, offset=P - 1, ap=[[TABW - 1, P], [P * TABW, NH], [1, D]])
            sp.dma_start(c.bias, src).then_inc(c.bias_in, 16)
            sp.wait_ge(z_act, 3 * NT)
            for b in range(NB):
                rows = slice(JS * b, JS * b + JS)
                sp.dma_start(t["o_win_s"][0, b, PAST - JS:PAST].rearrange("s a g d -> s (a g d)"),
                             kv[smp % 2][rows, 2, :, :].rearrange("p a d -> p (a d)")).then_inc(rows_out, 16)
                sp.dma_start(t["o_pool_s"][0, b, PBUF - JS:PBUF, :], zp[smp % 3][rows, :]).then_inc(rows_out, 16)
            sp.wait_ge(rows_out, 32 * NB)

        @block.gpsimd
        def _(pool):
            mod_bias_load(c, pool, 2)
            vec = 2
            for i in range(NT):
                T, s = tile_rows(i), i % 2
                if i == 4:
                    pool.wait_ge(c.tab_out, 16)
                    pool.dma_start(t["o_pool_s"][0, :, 0:PBUF - JS, :], t["state_pool"][0, :, JS:PBUF, :]).then_inc(c.out_done, 16)
                    pool.dma_start(t["o_win_s"][0, :, 0:PAST - JS].rearrange("b s a g d -> b (s a g d)"),
                                   t["state_win_kv"][0, :, JS:PAST].rearrange("b s a g d -> b (s a g d)")).then_inc(c.out_done, 16)
                    c.out_total += 32
                pool.wait_ge(z_act, 3 * i + 3)
                for br in range(2):
                    cp = pool.tensor_copy(c.vs[0:T, i, br, :, :].rearrange("p g d -> p (g d)"), kv[s][0:T, 1 + br, 1, :])
                cp.then_inc(v_copied, 1)
                if i < smp:
                    outs = [("o_cmp_p", 0), ("o_sel_p", 1)] + ([("o_win_p", 2)] if i >= 4 else [])
                    for name, br in outs:
                        r0 = (i - 4 if br == 2 else i) * P
                        dst = t[name][0, 0, r0:r0 + P].rearrange("s a g d -> s (a g d)")
                        pool.dma_start(dst, kv[s][:, br, :, :].rearrange("p a d -> p (a d)")).then_inc(kv_out[s], 16)
                        n_kv_out[s] += 1
                else:
                    for name, br in (("o_cmp_s", 0), ("o_sel_s", 1)):
                        pool.dma_start(t[name][0].rearrange("b s a g d -> (b s) (a g d)"),
                                       kv[s][0:NS, br, :, :].rearrange("p a d -> p (a d)")).then_inc(kv_out[s], 16)
                        n_kv_out[s] += 1
                if i == smp - 1:
                    pool.dma_start(t["o_pool_p"][0, 0], zp[i % 3][P - PBUF:P, :]).then_inc(p_out, 16)
                if i == smp:
                    pool.wait_ge(vn_ready, NT)
                    pool.dma_start(t["o_sgu_s"][0].rearrange("b j w -> (b j) w"), c.vn[i % 2][0:NS, :]).then_inc(sgv_out, 16)
                if i >= 2 and i % 2 == 0:
                    mod_store(c, pool, vec)
                    if vec < 5:
                        mod_bias_load(c, pool, vec + 1)
                    vec += 1
            pool.wait_ge(p_out, 16)
            pool.wait_ge(sgv_out, 16)
            pool.wait_ge(c.mods_out, 16 * 4)
            for s in range(2):
                pool.wait_ge(kv_out[s], 16 * n_kv_out[s])

        kv_dmas = {}
        total = [0, 0]
        for i in range(NT):
            total[i % 2] += (2 if i < 4 else 3) if i < smp else 2
            kv_dmas[i] = 16 * total[i % 2]

        @block.tensor
        def _(pe):
            def transposes(i):
                T = tile_rows(i)
                pe.wait_ge(c.x_in, 16 * (i + 1))
                if i >= 1:
                    pe.wait_ge(h_act, i)
                    pe.wait_ge(h_dve, i)
                for k in range(KT):
                    mm = pe.transpose(c.bank(k // 4)[:, (k % 4) * P:(k % 4) * P + T], x[0:T, k * P:(k + 1) * P],
                                      c.ident[0:T, 0:T])
                mm.then_inc(xT_ready, 1)

            def chunk(i, n):
                T = tile_rows(i)
                a, w = W_CHUNKS[n]
                if i == 0:
                    pe.wait_ge(c.w_in_in[n], 16)
                if n == 0:
                    if i < smp:
                        pe.wait_ge(h_act, i + 1)
                    pe.wait_ge(h_dve, i + 1)
                if n <= 1 and i >= 1:
                    pe.wait_ge(z_act, 3 * (i - 1) + 2 + n)
                if n == 2:
                    pe.wait_ge(z_act, 3 * i + 1)
                if n == 3:
                    pe.wait_ge(z_dve, i + 1)
                for k in range(KT):
                    mm = pe.matmul(c.bank(2 + n % 2)[0:T, 0:w], hT[i % 2][:, k, 0:T], c.w_in[:, k, a:a + w],
                                   start=(k == 0), stop=(k == KT - 1))
                mm.then_inc(z_ready, 1)

            def queries(i):
                T = tile_rows(i)
                if i == 0:
                    pe.wait_ge(c.w_in_in[4], 16 * 2 * REP)
                else:
                    pe.wait_ge(q_evac, i)
                for j in range(REP):
                    for k in range(KT):
                        two = c.w_in[:, k, Q0 + P * j:Q0 + P * j + P]
                        mm = pe.matmul(c.bank(6)[:, j * P:j * P + T], two, hT[i % 2][:, k, 0:T],
                                       start=(k == 0), stop=(k == KT - 1))
                mm.then_inc(q_done, 1)

            def keys(i):
                T = tile_rows(i)
                pe.wait_ge(z_act, 3 * i + 3)
                if i >= 1:
                    pe.wait_ge(so_evac, i)
                for br in range(2):
                    mm = pe.transpose(c.bank(7)[:, br * P:br * P + T], kv[i % 2][0:T, 1 + br, 0, :], c.ident[0:T, 0:T])
                mm.then_inc(kT_ready, 1)

            def pool_window(i):
                T = tile_rows(i)
                pe.wait_ge(kT_evac, i + 1)
                for g in range(4):
                    out = c.bank(7)[0:HD, g * P:g * P + T]
                    cols = slice(g * HD, (g + 1) * HD)
                    if i == 0:
                        mm = pe.matmul(out, zp[0][:, cols], first[:, g, :], start=True, stop=True)
                    elif i < smp:
                        pe.matmul(out, zp[(i - 1) % 3][:, cols], prev[:, g, :], start=True, stop=False)
                        mm = pe.matmul(out, zp[i % 3][:, cols], same[:, g, :], start=False, stop=True)
                    else:
                        n = NB * PBUF
                        pe.matmul(out, c.pbuf[0:n, cols], pb_buf[0:n, g, :], start=True, stop=False)
                        mm = pe.matmul(out, zp[i % 3][0:NS, cols], pb_new[0:NS, g, :], start=False, stop=True)
                mm.then_inc(pd_ready, 1)

            def pool_mix(i):
                T = tile_rows(i)
                pe.wait_ge(pd_evac, i + 1)
                for g in range(4):
                    lo = HD * (g % 2)
                    mm = pe.matmul(c.bank(7)[lo:lo + HD, (g // 2) * P:(g // 2) * P + T], c.pool_w[0:HD, g, :],
                                   dT[0:HD, g, 0:T], start=True, stop=True)
                mm.then_inc(po_ready, 1)

            def gating(i):
                T = tile_rows(i)
                pe.wait_ge(po_evac, i + 1)
                pe.wait_ge(vn_ready, i + 1)
                w = c.sgu_wT if i < smp else c.sgu_wS
                for g in range(4):
                    mm = pe.matmul(c.bank(7)[0:T, g * HD:(g + 1) * HD], w[0:T, g, 0:T],
                                   c.vn[i % 2][0:T, g * HD:(g + 1) * HD], start=True, stop=True)
                mm.then_inc(sg_ready, 1)

            def gating_out(i):
                T = tile_rows(i)
                pe.wait_ge(sgo_ready, i + 1)
                for m in range(2):
                    mm = pe.transpose(c.bank(7)[:, m * P:m * P + T], c.sgo[0:T, m * P:(m + 1) * P], c.ident[0:T, 0:T])
                mm.then_inc(so_ready, 1)

            transposes(0)
            for i in range(NT + 1):
                last = i - 1
                if i + 1 < NT:
                    transposes(i + 1)
                if i < NT:
                    chunk(i, 0)
                if i >= 1:
                    keys(last)
                if i < NT:
                    chunk(i, 1)
                if i >= 1:
                    pool_window(last)
                if i < NT:
                    chunk(i, 2)
                if i >= 1:
                    pool_mix(last)
                    if i < NT:
                        mod_products(c, pe, i + 3)
                    gating(last)
                if i < NT:
                    chunk(i, 3)
                if i >= 1:
                    gating_out(last)
                if i < NT:
                    queries(i)

        @block.scalar
        def _(act):
            def h_part(i):
                act.wait_ge(xT_ready, i + 1)
                if i >= 2:
                    act.wait_ge(q_done, i - 1)
                for k in range(4):
                    a = act.activation(hT[i % 2][:, k, :], c.bank(0)[:, k * P:(k + 1) * P], ACT.Identity,
                                       bias=c.modT[:, k, 0:1], scale=c.modT[:, KT + k, 0:1])
                a.then_inc(h_act, 1)

            h_part(0)
            for i in range(NT):
                T, s = tile_rows(i), i % 2
                if i + 1 < smp:
                    h_part(i + 1)
                act.wait_ge(z_ready, 4 * i + 1)
                if i >= 2:
                    act.wait_ge(pd_ready, i - 1)
                    act.wait_ge(sgo_ready, i - 1)
                act.copy(zp[i % 3][0:T, :], c.bank(2)[0:T, 0:PW])
                act.copy(zuv[s][0:T, 0, :], c.bank(2)[0:T, PW:2 * PW]).then_inc(z_act, 1)
                act.wait_ge(z_ready, 4 * i + 3)
                if i >= 2:
                    act.wait_ge(kv_out[s], kv_dmas[i - 2])
                    act.wait_ge(v_copied, i - 1)
                    act.wait_ge(kT_ready, i - 1)
                act.copy(kv[s][0:T, 0:2, :, :].rearrange("p b a d -> p (b a d)"), c.bank(2)[0:T, :]).then_inc(z_act, 1)
                act.wait_ge(z_ready, 4 * i + 4)
                act.copy(kv[s][0:T, 2, :, :].rearrange("p a d -> p (a d)"), c.bank(3)[0:T, 0:KVW])
                act.copy(c.gates[0:T, i, :], c.bank(3)[0:T, KVW:KVW + 24]).then_inc(z_act, 1)
                act.wait_ge(st_ready, i + 1)
                act.activation(rstd[0:T, :], mv[0:T, 1:2], ACT.Sqrt).then_inc(sqrt_done, 1)

        @block.vector
        def _(dve):
            links = [0]

            def linked(ins):
                links[0] += 1
                ins.then_inc(link, 1)
                dve.wait_ge(link, links[0])

            def h_part(i):
                dve.wait_ge(xT_ready, i + 1)
                if i >= 2:
                    dve.wait_ge(q_done, i - 1)
                if i < smp:
                    for k in range(4, KT):
                        a = dve.tensor_scalar(hT[i % 2][:, k, :], c.bank(1)[:, (k - 4) * P:(k - 3) * P],
                                              c.modT[:, KT + k, 0:1], c.modT[:, k, 0:1], ALU.mult, ALU.add)
                    a.then_inc(h_dve, 1)
                    return
                for k in range(KT):
                    src = c.bank(k // 4)[:, (k % 4) * P:(k % 4) * P + NS].rearrange("p (b j) -> p b j", b=NB)
                    dst = hT[i % 2][:, k, 0:NS].rearrange("p (b j) -> p b j", b=NB)
                    scale = c.modT[:, KT + k, 1:9].unsqueeze(2).to_broadcast([P, NB, JS])
                    shift = c.modT[:, k, 1:9].unsqueeze(2).to_broadcast([P, NB, JS])
                    linked(dve.tensor_tensor(dst, src, scale, ALU.mult))
                    a = dve.tensor_tensor(dst, dst, shift, ALU.add)
                a.then_inc(h_dve, 1)

            h_part(0)
            for i in range(NT + 1):
                last = i - 1
                if i + 1 < NT:
                    h_part(i + 1)
                if i >= 1:
                    T = tile_rows(last)
                    dve.wait_ge(kT_ready, i)
                    dve.tensor_copy(c.kT[:, :, last * P:last * P + T],
                                    c.bank(7, 256).rearrange("p (b t) -> p b t", b=2)[:, :, 0:T]).then_inc(kT_evac, 1)
                if i < NT:
                    Ti = tile_rows(i)
                    dve.wait_ge(z_ready, 4 * i + 2)
                    dve.tensor_copy(zuv[i % 2][0:Ti, 1, :], c.bank(3)[0:Ti, 0:PW]).then_inc(z_dve, 1)
                if i >= 1:
                    dve.wait_ge(pd_ready, i)
                    if i >= 2:
                        dve.wait_ge(po_ready, i - 1)
                    dve.tensor_copy(dT[0:HD, :, 0:T], c.bank(7)[0:HD, :].rearrange("p (g t) -> p g t", g=4)[:, :, 0:T])\
                        .then_inc(pd_evac, 1)
                    dve.wait_ge(po_ready, i)
                    for m in range(2):
                        a = dve.tensor_scalar(c.mix[:, m, last * P:last * P + T], c.bank(7)[:, m * P:m * P + T],
                                              c.pool_sc[:, m:m + 1], None, ALU.mult)
                    a.then_inc(po_evac, 1)
                    if i < NT and i % 2 == 0:
                        mod_vector(c, dve, i // 2 + 1)
                    bias = c.sgu_b if last < smp else c.sgu_bS
                    dve.wait_ge(sg_ready, i)
                    if i >= 2:
                        dve.wait_ge(so_ready, i - 1)
                    linked(dve.tensor_tensor(c.sgo[0:T, :].rearrange("p (g d) -> p g d", g=4),
                                             c.bank(7)[0:T, 0:PW].rearrange("p (g d) -> p g d", g=4),
                                             bias[0:T, :].unsqueeze(2).to_broadcast([T, 4, HD]), ALU.add))
                    dve.tensor_tensor(c.sgo[0:T, :], c.sgo[0:T, :], zuv[last % 2][0:T, 0, :], ALU.mult).then_inc(sgo_ready, 1)
                    dve.wait_ge(so_ready, i)
                    dve.tensor_copy(c.mix[:, 2:4, last * P:last * P + T],
                                    c.bank(7, 256).rearrange("p (m t) -> p m t", m=2)[:, :, 0:T]).then_inc(so_evac, 1)
                if i < NT:
                    v, vn = zuv[i % 2][0:Ti, 1, :], c.vn[i % 2][0:Ti, :]
                    dve.wait_ge(z_dve, i + 1)
                    linked(dve.bn_stats(stats[0:Ti, :], v))
                    linked(dve.bn_aggr(mv[0:Ti, :], stats[0:Ti, :]))
                    dve.tensor_scalar(mv[0:Ti, 1:2], mv[0:Ti, 1:2], EPS, None, ALU.add).then_inc(st_ready, 1)
                    dve.wait_ge(sqrt_done, i + 1)
                    linked(dve.reciprocal(rstd[0:Ti, :], rstd[0:Ti, :]))
                    linked(dve.tensor_scalar(vn, v, mv[0:Ti, 0:1], rstd[0:Ti, :], ALU.subtract, ALU.mult))
                    linked(dve.tensor_tensor(vn, vn, c.lnv_g[0:Ti, :], ALU.mult))
                    dve.tensor_tensor(vn, vn, c.lnv_b[0:Ti, :], ALU.add).then_inc(vn_ready, 1)
                    dve.wait_ge(q_done, i + 1)
                    dve.tensor_scalar(c.qT[:, :, i * P:i * P + Ti],
                                      c.bank(6).rearrange("p (j t) -> p j t", j=4)[:, :, 0:Ti], SCALE, None, ALU.mult)\
                        .then_inc(q_evac, 1)


C2_ = KVR_ + 5120
NATW_ = W_ + 12480


def block_compression(c):
    nc, t, sem = c.nc, c.t, c.early_sem
    NPAIR = (SEQ + NB * PAST) // 2
    xcT = c.view(W_, 4, NPAIR)
    w1 = c.view(W_ + 4 * NPAIR, 2, CB // 2, P)
    o = W_ + 4 * NPAIR + 2 * (CB // 2) * P
    nat = [c.view(o + 512 * s, 4, 2, HD) for s in range(3)]
    o += 3 * 512
    w2 = c.view(o, 2, HD)
    pe_n = c.view(o + P, P)
    peT = c.view(o + 2 * P, 2, CB // 2)
    hid = c.view(o + 2 * P + 32, 2, 2, NC_P + NC_S * NB)
    assert o + 2 * P + 32 + 384 <= NATW_
    nblk = NC_P + NC_S * NB
    c.kcS = c.view(C2_, nblk)
    c.kc_bd = c.view(C2_ + 96, 2, NC_P)
    c.vc_bd = c.view(C2_ + 160, 4, HD)
    c.vcS = c.view(C2_ + 416, 2, HD)
    c.nat_win = c.view(NATW_, NB * NPAGE, 256)
    cw_in, pe_in = sem("cw_in"), sem("pe_in")
    nat_in = [sem(f"nat_in{s}") for s in range(3)]
    nt_ps, nt_ev, pe_ps, pe_ev, hid_ps, hid_ev, kc_ps, kc_ev, zeroed = (sem(n) for n in (
        "nt_ps", "nt_ev", "pe_ps", "pe_ev", "hid_ps", "hid_ev", "kc_ps", "kc_ev", "zeroed"))
    c.natw_in, c.gate_done = c.sem("natw_in"), c.sem("gate_done")
    tiles = NPAIR // P
    n_dma = [0, 0, 0]
    need = []
    for n in range(tiles):
        n_dma[n % 3] += 2 if n < 4 else 4
        need.append(16 * n_dma[n % 3])

    with nc.Block() as block:
        @block.sync
        def _(sp):
            sp.dma_start(pe_n[0:32, :], t["cmp_pe"][0].rearrange("s (c q) d -> (s c) (q d)", q=2)).then_inc(pe_in, 16)
            for n in range(tiles):
                if n >= 3:
                    sp.wait_ge(nt_ps, n - 2)
                dst = nat[n % 3]
                if n < 4:
                    src = t["o_cmp_p"][0, 0, n * 256:(n + 1) * 256].rearrange("(p q) s g d -> p q (s g) d", q=2)
                    for q in range(2):
                        sp.dma_start(dst[:, :, q, :], src[:, q]).then_inc(nat_in[n % 3], 16)
                else:
                    b = n - 4
                    for pg in range(NPAGE):
                        at = b * NPAGE + pg
                        page = sp.value_load(c.page[0:1, at:at + 1], min_val=0, max_val=t["cache_cmp_kv"].shape[1] - 1)
                        src = t["cache_cmp_kv"][0, bass.ds(page, 1)].rearrange("n (p q) s g d -> p q (n s g) d", q=2)
                        for q in range(2):
                            sp.dma_start(dst[64 * pg:64 * pg + 64, :, q, :], src[:, q]).then_inc(nat_in[n % 3], 16)
                if n == 3:
                    sp.dma_start(w1, t["cmp_w1"][0].rearrange("s (c p) h -> p s c h", p=P)).then_inc(cw_in, 16)
                    sp.dma_start(w2, t["cmp_w2"][0].rearrange("s h d -> h s d")).then_inc(cw_in, 16)
            sp.dma_start(c.view(CPH_, 1072), t["cph2"]).then_inc(c.cph_in, 16)
            sp.dma_start(c.view(CPH_ + 1072, P), t["cph3"]).then_inc(c.cph_in, 16)
            sp.dma_start(c.nat_win, t["state_win_kv"][0].rearrange("b (q s) a g d -> s (b q) (a g d)", s=P)).then_inc(c.natw_in, 16)

        @block.tensor
        def _(pe):
            pe.wait_ge(pe_in, 16)
            pe.transpose(c.bank(7)[:, 0:32], pe_n[0:32, :], c.ident[0:32, 0:32]).then_inc(pe_ps, 1)
            for n in range(tiles):
                pe.wait_ge(nat_in[n % 3], need[n])
                if n >= 2:
                    pe.wait_ge(nt_ev, n - 1)
                for sg in range(4):
                    mm = pe.transpose(c.bank(n % 2)[:, sg * P:(sg + 1) * P],
                                      nat[n % 3][:, sg, :, :].rearrange("p q d -> p (q d)"), c.ident)
                mm.then_inc(nt_ps, 1)
            pe.wait_ge(nt_ev, tiles)
            pe.wait_ge(cw_in, 32)
            for s in range(2):
                for k in range(CB // 2):
                    cols = xcT[:, 2 * s:2 * s + 2, :].rearrange("p g (n c) -> p g n c", c=CB // 2)[:, :, :, k]
                    mm = pe.matmul(c.bank(2 + s)[:, 0:2 * nblk].rearrange("p (g n) -> p g n", g=2), w1[:, s, k, :], cols,
                                   start=(k == 0), stop=(k == CB // 2 - 1))
                mm.then_inc(hid_ps, 1)
            pe.wait_ge(hid_ev, 1)
            for g in range(2):
                mm = pe.matmul(c.bank(6)[HD * g:HD * g + HD, 0:nblk], w2[:, 0, :], hid[:, 0, g, :], start=True, stop=True)
            pe.wait_ge(hid_ev, 2)
            for x in range(4):
                pe.matmul(c.bank(4)[32 * x:32 * x + 32, 0:HD], hid[:, 1, x % 2, 0:NC_P], w2[:, 1, :], start=True, stop=True)
            for g in range(2):
                mm = pe.matmul(c.bank(5)[0:NB * NC_S, HD * g:HD * g + HD], hid[:, 1, g, NC_P:], w2[:, 1, :],
                               start=True, stop=True)
            mm.then_inc(kc_ps, 1)

        @block.scalar
        def _(act):
            for s in range(2):
                act.wait_ge(hid_ps, s + 1)
                act.activation(hid[:, s, :, :].rearrange("p g n -> p (g n)"), c.bank(2 + s)[:, 0:2 * nblk],
                               ACT.Gelu_apprx_tanh).then_inc(hid_ev, 1)
            act.activation(c.gates[:, 0:NP_TILES, :].rearrange("p a b -> p (a b)"),
                           c.gates[:, 0:NP_TILES, :].rearrange("p a b -> p (a b)"), ACT.Sigmoid).then_inc(c.gate_done, 1)
            act.activation(c.gates[0:NS, NP_TILES, :], c.gates[0:NS, NP_TILES, :], ACT.Sigmoid).then_inc(c.gate_done, 1)

        @block.vector
        def _(dve):
            dve.memset(c.kc_bd, 0.0)
            dve.memset(c.vc_bd, 0.0).then_inc(zeroed, 1)
            dve.wait_ge(pe_ps, 1)
            dve.tensor_copy(peT, c.bank(7)[:, 0:32].rearrange("p (s c) -> p s c", s=2)).then_inc(pe_ev, 1)
            dve.wait_ge(pe_ev, 1)
            for n in range(tiles):
                dve.wait_ge(nt_ps, n + 1)
                for s in range(2):
                    a = None
                    for g in range(2):
                        a = dve.tensor_tensor(
                            xcT[:, 2 * s + g, n * P:(n + 1) * P].rearrange("p (n c) -> p n c", c=CB // 2),
                            c.bank(n % 2)[:, (2 * s + g) * P:(2 * s + g + 1) * P].rearrange("p (n c) -> p n c", c=CB // 2),
                            peT[:, s, :].unsqueeze(1).to_broadcast([P, 8, CB // 2]), ALU.add)
                a.then_inc(nt_ev, 1)
            dve.wait_ge(kc_ps, 1)
            dve.wait_ge(zeroed, 1)
            dve.tensor_copy(c.kcS, c.bank(6)[:, 0:nblk])
            for g in range(2):
                dve.tensor_copy(c.kc_bd[HD * g:HD * g + HD, g, :], c.bank(6)[HD * g:HD * g + HD, 0:NC_P])
            for x in range(4):
                dve.tensor_copy(c.vc_bd[32 * x:32 * x + 32, x, :], c.bank(4)[32 * x:32 * x + 32, 0:HD])
            dve.tensor_copy(c.vcS[0:NB * NC_S, :, :], c.bank(5)[0:NB * NC_S, 0:P].rearrange("p (g d) -> p g d", g=2))\
                .then_inc(kc_ev, 1)
            dve.wait_ge(kc_ev, 1)


def block_decode_attention(c):
    nc, t, sem = c.nc, c.t, c.early_sem
    nat_sel = c.view(W_, NB * NPAGE, 256)
    nats = [nat_sel, c.nat_win]
    kTs = [c.view(W_ + 4096 + 2048 * s, NB, PAST) for s in range(2)]
    o = W_ + 8192
    WK = PAST + NS
    bS = c.view(o, 2, 2, WK); o += 4 * WK
    bC = c.view(o, 2, 2, NS); o += 4 * NS
    qs = c.view(o, 2, P); o += 2 * P
    acc = c.view(o, 2, 2, HD); o += 4 * HD
    acc2 = c.view(o, 2, 2, 2, HD); o += 8 * HD
    gS = c.view(o, 2, 2, 3); o += 12
    gt = c.view(o, 24); o += 24
    mx = c.view(o, 12); sm = c.view(o + 12, 12); cf = c.view(o + 24, 12); o += 36
    pbuf = [c.view(o + WK * s, WK) for s in range(2)]; o += 2 * WK
    pT = [c.view(o + 3 * P * s, 3, P) for s in range(2)]; o += 6 * P
    assert o <= NATW_, o
    selg, rowm, selr = c.view(CPH_, 2, P), c.view(CPH_ + 256, 2, 24), c.view(CPH_ + 304, 4, P)
    mine, notmine = c.view(CPH_ + 816, 2, NB, JS), c.view(CPH_ + 944, 2, NB, JS)
    nats_in = sem("nats_in")
    (kt_ps, kt_ev, bs_ps, bs_ev, g_ps, g_ev, qs_ev, s_ps, s_ev, e_ev, t_ps, t_ev, o_ps, o_ev, f_ps, f_ev, link,
     a2_ev) = (sem(n) for n in (
         "dk_ps", "dk_ev", "db_ps", "db_ev", "dg_ps", "dg_ev", "dq_ev", "ds_ps", "ds_ev", "de_ev", "dt_ps", "dt_ev",
         "do_ps", "do_ev", "df_ps", "df_ev", "d_link", "da_ev"))
    units = [(br, g, half) for br in range(3) for g in range(2) for half in range(2)]

    with nc.Block() as block:
        @block.sync
        def _(sp):
            for at in range(NB * NPAGE):
                page = sp.value_load(c.page[0:1, at:at + 1], min_val=0, max_val=t["cache_sel_kv"].shape[1] - 1)
                sp.dma_start(nat_sel[:, at, :], t["cache_sel_kv"][0, bass.ds(page, 1)].rearrange("n s a g d -> s (n a g d)"))\
                    .then_inc(nats_in, 16)

        @block.tensor
        def _(pe):
            pe.wait_ge(c.bias_in, 16)
            pe.wait_ge(c.cph_in, 32)
            for g in range(2):
                for r in range(REP):
                    pe.matmul(c.bank(6 + g)[:, 0:264], selr[0:JS, r, :], c.bias[0:JS, 4 * g + r, 640:904],
                              start=(r == 0), stop=(r == REP - 1))
                for r in range(REP):
                    mm = pe.matmul(c.bank(6 + g)[:, 272:280], selr[0:JS, r, :],
                                   c.bias[0:JS, 4 * g + r, 671:671 + 32 * 7 + 1:32], start=(r == 0), stop=(r == REP - 1))
                mm.then_inc(bs_ps, 1)
            pe.wait_ge(c.gate_done, 2)
            for half in range(2):
                mm = pe.matmul(c.bank(4)[:, 24 * half:24 * half + 24], selg[0:NS, half, :], c.gates[0:NS, NP_TILES, :],
                               start=True, stop=True)
            mm.then_inc(g_ps, 1)
            pe.wait_ge(qs_ev, 1)
            n_kt = [0]

            def keys(br):
                pe.wait_ge(nats_in if br == 1 else c.natw_in, 16 * 16 if br == 1 else 16)
                for m in range(4):
                    if n_kt[0] >= 2:
                        pe.wait_ge(kt_ev, n_kt[0] - 1)
                    for q in range(4):
                        mm = pe.transpose(c.bank(2 + n_kt[0] % 2)[:, q * P:(q + 1) * P], nats[br - 1][:, 4 * m + q, 0:P], c.ident)
                    mm.then_inc(kt_ps, 1)
                    n_kt[0] += 1

            def scores(u):
                br, g, half = units[u]
                if u >= 2:
                    pe.wait_ge(s_ev, u - 1)
                if br == 1:
                    pe.wait_ge(kt_ev, 4)
                if br == 2:
                    pe.wait_ge(kt_ev, 8)
                lo = HD * g
                q = qs[lo:lo + HD, half, :]
                if br == 0:
                    pe.matmul(c.bank(u % 2)[:, 0:NS], q, c.kcS[lo:lo + HD, NC_P:], start=True, stop=True).then_inc(s_ps, 1)
                    return
                for b4 in range(4):
                    pe.matmul(c.bank(u % 2)[32 * b4:32 * b4 + 32, 0:PAST], q[:, 32 * b4:32 * b4 + 32],
                              kTs[br - 1][lo:lo + HD, 4 * half + b4, :], start=True, stop=True)
                pe.matmul(c.bank(u % 2)[:, PAST:WK], q, c.kT[lo:lo + HD, br - 1, SEQ:], start=True, stop=True).then_inc(s_ps, 1)

            def turns(u):
                br = units[u][0]
                pe.wait_ge(e_ev, u + 1)
                if u >= 2:
                    pe.wait_ge(t_ev, u - 1)
                if u < 2:
                    pe.wait_ge(kt_ev, 8)
                for k, w in enumerate((NS,) if br == 0 else (P, P, NS)):
                    mm = pe.transpose(c.bank(2 + u % 2)[0:w, k * P:(k + 1) * P], pbuf[u % 2][:, k * P:k * P + w], c.ident)
                mm.then_inc(t_ps, 1)

            def values(u):
                br, g, half = units[u]
                pe.wait_ge(t_ev, u + 1)
                if u >= 2:
                    pe.wait_ge(o_ev, u - 1)
                elif u == 0:
                    pe.wait_ge(g_ev, 1)
                out = c.bank(4 + u % 2)[:, 0:HD]
                if br == 0:
                    pe.matmul(out, pT[u % 2][0:NS, 0, :], c.vcS[0:NS, g, :], start=True, stop=True).then_inc(o_ps, 1)
                    return
                pe.matmul(out, pT[u % 2][0:NS, 2, :], c.vs[0:NS, NP_TILES, br - 1, g, :], start=True, stop=False,
                          skip_group_check=True)
                for b4 in range(4):
                    for pg in range(NPAGE):
                        mm = pe.matmul(out[32 * b4:32 * b4 + 32, :], pT[u % 2][:, pg, 32 * b4:32 * b4 + 32],
                                       nats[br - 1][:, (4 * half + b4) * NPAGE + pg, P + HD * g:P + HD * g + HD],
                                       start=False, stop=(pg == NPAGE - 1), skip_group_check=True)
                mm.then_inc(o_ps, 1)

            keys(2)
            keys(1)
            n = len(units)
            for s in range(n + 2):
                if s < n:
                    scores(s)
                if 1 <= s <= n:
                    turns(s - 1)
                if s >= 2:
                    values(s - 2)
            for g in range(2):
                for half in range(2):
                    pe.wait_ge(a2_ev, 1)
                    pe.transpose(c.bank(6 + g)[:, half * P:(half + 1) * P],
                                 acc2[:, g, half, :, :].rearrange("p a d -> p (a d)"), c.ident).then_inc(f_ps, 1)

        @block.scalar
        def _(act):
            for u, (br, g, half) in enumerate(units):
                w = NS if br == 0 else WK
                act.wait_ge(s_ev, u + 1)
                act.activation(pbuf[u % 2][:, 0:w], pbuf[u % 2][:, 0:w], ACT.Exp, bias=mx[:, u:u + 1], scale=-1.0,
                               accum_out=sm[:, u:u + 1]).then_inc(e_ev, 1)

        @block.vector
        def _(dve):
            links = [0]

            def linked(ins):
                links[0] += 1
                ins.then_inc(link, 1)
                dve.wait_ge(link, links[0])

            for half in range(2):
                for b4 in range(4):
                    b = SEQ + (4 * half + b4) * JS
                    a = dve.tensor_copy(qs[:, half, 32 * b4:32 * b4 + 32].rearrange("p (r j) -> p r j", r=REP), c.qT[:, :, b:b + JS])
            a.then_inc(qs_ev, 1)
            dve.wait_ge(c.cph_in, 32)
            for g in range(2):
                dve.wait_ge(bs_ps, g + 1)
                for half in range(2):
                    dve.tensor_copy(bS[:, g, half, 0:PAST], c.bank(6 + g)[:, 0:PAST])
                    for dst, at in ((bS[:, g, half, PAST:], PAST), (bC[:, g, half, :], 272)):
                        dst = dst.rearrange("p (b j) -> p b j", b=NB)
                        src = c.bank(6 + g)[:, at:at + JS].unsqueeze(1).to_broadcast([P, NB, JS])
                        linked(dve.tensor_tensor(dst, src, mine[:, half], ALU.mult))
                        linked(dve.tensor_tensor(dst, dst, notmine[:, half], ALU.add))
            dve.wait_ge(g_ps, 1)
            for half in range(2):
                for g in range(2):
                    linked(dve.tensor_tensor(gt, c.bank(4)[:, 24 * half:24 * half + 24], rowm[:, g, :], ALU.mult))
                    linked(dve.tensor_reduce(gS[:, g, half, :], gt.rearrange("p (h r) -> p r h", r=3), AX.X, ALU.add))
            dve.engine_nop().then_inc(g_ev, 1)
            for n in range(8):
                dve.wait_ge(kt_ps, n + 1)
                dst = kTs[1 - n // 4][:, :, :].rearrange("p b s -> p (b s)")[:, (n % 4) * 512:(n % 4) * 512 + 512]
                dve.tensor_copy(dst, c.bank(2 + n % 2)).then_inc(kt_ev, 1)

            def soft(u):
                br, g, half = units[u]
                w = NS if br == 0 else WK
                dve.wait_ge(s_ps, u + 1)
                if u >= 2:
                    dve.wait_ge(t_ps, u - 1)
                bias = bC if br == 0 else bS
                dve.tensor_tensor_reduce(pbuf[u % 2][:, 0:w], c.bank(u % 2)[:, 0:w], bias[:, g, half, :], -1.0, 3e38,
                                         ALU.add, ALU.min, mx[:, u:u + 1]).then_inc(s_ev, 1)

            def turned(u):
                dve.wait_ge(t_ps, u + 1)
                if u >= 2:
                    dve.wait_ge(o_ps, u - 1)
                if units[u][0] == 0:
                    dve.tensor_copy(pT[u % 2][0:NS, 0, :], c.bank(2 + u % 2)[0:NS, 0:P]).then_inc(t_ev, 1)
                else:
                    dve.tensor_copy(pT[u % 2][:, 0:2, :], c.bank(2 + u % 2)[:, 0:256].rearrange("p (a b) -> p a b", a=2))
                    dve.tensor_copy(pT[u % 2][0:NS, 2, :], c.bank(2 + u % 2)[0:NS, 256:384]).then_inc(t_ev, 1)

            def gather(u):
                br, g, half = units[u]
                linked(dve.tensor_scalar(cf[:, u:u + 1], sm[:, u:u + 1], 1e-30, None, ALU.max))
                linked(dve.reciprocal(cf[:, u:u + 1], cf[:, u:u + 1]))
                linked(dve.tensor_tensor(cf[:, u:u + 1], cf[:, u:u + 1], gS[:, g, half, br:br + 1], ALU.mult))
                dve.wait_ge(o_ps, u + 1)
                o = c.bank(4 + u % 2)[:, 0:HD]
                if br == 0:
                    a = dve.tensor_scalar(acc[:, g, half, :], o, cf[:, u:u + 1], None, ALU.mult)
                else:
                    a = dve.scalar_tensor_tensor(out=acc[:, g, half, :], in0=o, scalar=cf[:, u:u + 1],
                                                 in1=acc[:, g, half, :], op0=ALU.mult, op1=ALU.add)
                a.then_inc(o_ev, 1)
                dve.wait_ge(o_ev, u + 1)

            n = len(units)
            for s in range(n + 2):
                if s < n:
                    soft(s)
                if 1 <= s <= n:
                    turned(s - 1)
                if s >= 2:
                    gather(s - 2)
            for d in range(2):
                a = dve.tensor_copy(acc2[:, :, :, d, :].rearrange("p g h d -> p (g h) d"),
                                    acc.rearrange("p g h d -> p (g h) d"))
            a.then_inc(a2_ev, 1)
            for g in range(2):
                for half in range(2):
                    dve.wait_ge(f_ps, 2 * g + half + 1)
                for r in range(REP):
                    h = REP * g + r
                    lo = HD * (h % 2)
                    src = c.bank(6 + g)[lo:lo + HD, 0:256].rearrange("p (b r j) -> p b r j", b=NB, r=REP)[:, :, r, :]
                    dve.tensor_copy(c.mix[lo:lo + HD, 4 + h // 2, SEQ:].rearrange("p (b j) -> p b j", b=NB), src).then_inc(f_ev, 1)
            dve.wait_ge(f_ev, 8)


def retire_early_semaphores(c):
    c.nc.clear_and_free_semaphores(c.early)
    c.nc.all_engine_barrier()


def block_prompt_attention(c):
    nc, t, sem = c.nc, c.t, c.sem
    NU = 16 * NP_TILES
    c.w_out = c.view(W_, KT, D)
    kz = c.view(W_ + KT * D, 2, NKV, SEQ)
    pb = [c.view(KVR_ + D * s, D) for s in range(3)]
    pT = [c.view(KVR_ + D * (3 + s), KT, P) for s in range(2)]
    o = C2_ + 544
    oa = c.view(o, NH, HD)
    pc, pcT, tmp = c.view(o + 512, NH, NC_P), c.view(o + 768, 2, P), c.view(o + 1024, NH, HD)
    o += 1536
    mx, sm, cf = c.view(o, 3), c.view(o + 4, 16), c.view(o + 20, NH)
    cm, cs = c.view(o + 28, NH), c.view(o + 36, NH)
    assert o + 44 <= C2_ + 2304
    edge_f = c.view(CPH_ + 1072, P)
    edge = c.view(CPH_ + 1200, HD).bitcast(BF16)
    ident_b = c.view(CPH_ + 1264, HD).bitcast(BF16)
    (s_ps, s_ev, e_ev, t_ps, t_dve, t_act, v_ps, o_ev, cs_ps, cs_ev, ce_ev, cn_ev, co_ps, co_ev, edge_set,
     link, zero_set) = (sem(n) for n in ("ps_ps", "ps_ev", "pexp_ev", "pt_ps", "pt_dve", "pt_act", "pv_ps", "po_ev", "cs_ps", "cs_ev",
                               "ce_ev", "cn_ev", "co_ps", "co_ev", "edge_set", "p_link", "pc_zero"))
    c.w_out_in, kz_done = sem("w_out_in"), sem("kz_done")

    def unit(s):
        i, br, slot = s // 16, s % 16 // 8, s % 8
        k0 = max(0, i - WIN_TILES) if br else 0
        return i, br, slot // 2, slot % 2, k0, i + 1 - k0

    turns, number = [], {}
    for s in range(NU + 2):
        if 0 <= s - 2 < NU:
            turns.append(("unit", s - 2))
        if s < NU and s % 16 == 6 and s >= 16:
            turns.append(("result", s // 16 - 1))
        if s < NU and s % 16 == 8:
            turns.append(("compressed", s // 16))
    turns.append(("result", NP_TILES - 1))
    for n, what in enumerate(turns):
        number[what] = n

    def by_act(what):
        return what[0] == "unit" and unit(what[1])[5] > 4

    act_before = [sum(by_act(w) for w in turns[:n]) for n in range(len(turns) + 1)]

    with nc.Block() as block:
        @block.sync
        def _(sp):
            sp.dma_start(c.w_out, t["w_out"][0].rearrange("(k p) n -> p k n", p=P)).then_inc(c.w_out_in, 16)

        @block.tensor
        def _(pe):
            def bank_free(what):
                n = number[what]
                if n:
                    pe.wait_ge(t_dve, n)
                    if act_before[n]:
                        pe.wait_ge(t_act, act_before[n])

            def scores(s):
                i, br, j, g, k0, nk = unit(s)
                if s >= 2:
                    pe.wait_ge(s_ev, s - 1)
                if s % 16 == 0:
                    pe.wait_ge(kz_done, 4 * (i + 1))
                base = (s % 2) * 1024
                edge_here = br == 1 and i >= WIN_TILES
                for c0 in range(0, nk * P, 512):
                    w = min(512, nk * P - c0)
                    masked = edge_here and c0 == 0
                    mm = pe.matmul(c.psum[:, base + c0:base + c0 + w], c.qT[:, j, i * P:(i + 1) * P],
                                   kz[:, br, g, k0 * P + c0:k0 * P + c0 + w], start=True, stop=not masked)
                    if masked:
                        if s == 16 * WIN_TILES + 8:
                            pe.wait_ge(edge_set, 2)
                        mm = pe.matmul(c.psum[:, base:base + P], ident_b, edge, start=False, stop=True)
                mm.then_inc(s_ps, 1)

            def turn(s):
                nk = unit(s)[5]
                pe.wait_ge(e_ev, s + 1)
                bank_free(("unit", s))
                for k in range(nk):
                    mm = pe.transpose(c.psum[:, 2048 + k * P:2048 + (k + 1) * P], pb[s % 3][:, k * P:(k + 1) * P], c.ident)
                mm.then_inc(t_ps, 1)

            def values(s):
                i, br, j, g, k0, nk = unit(s)
                pe.wait_ge(t_dve, number["unit", s] + 1)
                if nk > 4:
                    pe.wait_ge(t_act, act_before[number["unit", s] + 1])
                if s % 8 == 0:
                    if br == 0 and i >= 1:
                        pe.wait_ge(o_ev, 2 * i - 1)
                    if br == 1:
                        pe.wait_ge(co_ev, i + 1)
                slot = s % 8
                for k in range(nk):
                    mm = pe.matmul(c.bank(6 + br)[:, slot * HD:(slot + 1) * HD], pT[s % 2][:, k, :], c.vs[:, k0 + k, br, g, :],
                                   start=(k == 0), stop=(k == nk - 1))
                mm.then_inc(v_ps, 1)

            def compressed_scores(i):
                if i >= 1:
                    pe.wait_ge(o_ev, 2 * i)
                for j in range(REP):
                    mm = pe.matmul(c.bank(7)[:, 64 * j:64 * j + 64], c.qT[:, j, i * P:(i + 1) * P],
                                   c.kc_bd.rearrange("p g n -> p (g n)"), start=True, stop=True)
                mm.then_inc(cs_ps, 1)

            def compressed_turn(i):
                pe.wait_ge(cn_ev, i + 1)
                bank_free(("compressed", i))
                flat = pc.rearrange("p h n -> p (h n)")
                for m in range(2):
                    mm = pe.transpose(c.bank(4)[:, m * P:(m + 1) * P], flat[:, m * P:(m + 1) * P], c.ident)
                mm.then_inc(t_ps, 1)

            def compressed_values(i):
                pe.wait_ge(t_dve, number["compressed", i] + 1)
                for m in range(2):
                    mm = pe.matmul(c.bank(7)[:, 256 * m:256 * m + 256], pcT[:, m, :], c.vc_bd.rearrange("p x d -> p (x d)"),
                                   start=True, stop=True)
                mm.then_inc(co_ps, 1)

            def result_turn(i):
                pe.wait_ge(o_ev, 2 * i + 2)
                bank_free(("result", i))
                flat = oa.rearrange("p h d -> p (h d)")
                for m in range(4):
                    mm = pe.transpose(c.bank(4)[:, m * P:(m + 1) * P], flat[:, m * P:(m + 1) * P], c.ident)
                mm.then_inc(t_ps, 1)

            for s in range(NU + 3):
                i, r = s // 16, s % 16
                if 0 <= s - 2 < NU:
                    turn(s - 2)
                if s < NU:
                    scores(s)
                    if r == 5:
                        compressed_scores(i)
                    if r == 6 and i >= 1:
                        result_turn(i - 1)
                    if r == 8:
                        compressed_turn(i)
                    if r == 9:
                        compressed_values(i)
                if s >= 3:
                    values(s - 3)
            result_turn(NP_TILES - 1)

        @block.gpsimd
        def _(pool):
            for i in range(NP_TILES):
                tile = slice(i * P, (i + 1) * P)
                for g in range(NKV):
                    own, other = slice(HD * g, HD * g + HD), slice(HD - HD * g, 2 * HD - HD * g)
                    pool.memset(kz[other, :, g, tile], 0.0).then_inc(kz_done, 1)
                    pool.tensor_copy(kz[own, :, g, tile], c.kT[own, :, tile]).then_inc(kz_done, 1)

        @block.scalar
        def _(act):
            for s in range(NU + 2):
                if s >= 2 and by_act(("unit", s - 2)):
                    u = s - 2
                    nk = unit(u)[5]
                    act.wait_ge(t_ps, number["unit", u] + 1)
                    act.wait_ge(v_ps, u - 1)
                    act.copy(pT[u % 2][:, 4:nk, :].rearrange("p k q -> p (k q)"), c.bank(5)[:, 0:(nk - 4) * P]).then_inc(t_act, 1)
                if s < NU:
                    i, br, j, g, k0, nk = unit(s)
                    act.wait_ge(s_ev, s + 1)
                    if i >= 1:
                        act.wait_ge(o_ev, 2 * (i - 1) + br + 1)
                    act.activation(pb[s % 3][:, 0:nk * P], pb[s % 3][:, 0:nk * P], ACT.Exp, bias=mx[:, s % 3:s % 3 + 1],
                                   scale=-1.0, accum_out=sm[:, s % 16:s % 16 + 1]).then_inc(e_ev, 1)
                if s < NU and s % 16 == 5:
                    n = 4 * (s // 16 + 1)
                    act.wait_ge(cs_ev, s // 16 + 1)
                    act.activation(pc[:, :, 0:n], pc[:, :, 0:n], ACT.Exp).then_inc(ce_ev, 1)

        @block.vector
        def _(dve):
            links = [0]

            def linked(ins):
                links[0] += 1
                ins.then_inc(link, 1)
                dve.wait_ge(link, links[0])

            def soft(s):
                i, br, j, g, k0, nk = unit(s)
                w = nk * P
                dve.wait_ge(s_ps, s + 1)
                if s >= 3:
                    dve.wait_ge(t_ps, number["unit", s - 3] + 1)
                dve.tensor_tensor_reduce(pb[s % 3][:, 0:w], c.psum[:, (s % 2) * 1024:(s % 2) * 1024 + w],
                                         c.bias[:, 4 * g + j, D - w:D], -1.0, 3e38, ALU.add, ALU.min,
                                         mx[:, s % 3:s % 3 + 1]).then_inc(s_ev, 1)

            def turned(what, dst, src):
                dve.wait_ge(t_ps, number[what] + 1)
                dve.tensor_copy(dst, src).then_inc(t_dve, 1)

            def weighted(out, sums, i, br):
                linked(dve.tensor_scalar(out, sums, 1e-30, None, ALU.max))
                linked(dve.reciprocal(out, out))
                gate = c.gates[:, i, :].rearrange("p (g j r) -> p j g r", g=2, j=4)[:, :, :, br]
                linked(dve.tensor_tensor(out.rearrange("p (j g) -> p j g", g=2), out.rearrange("p (j g) -> p j g", g=2), gate, ALU.mult))

            def branch_result(i, br):
                weighted(cf, sm[:, 8 * br:8 * br + 8], i, 1 + br)
                dve.wait_ge(v_ps, 16 * i + 8 * br + 8)
                linked(dve.tensor_tensor(tmp, c.bank(6 + br).rearrange("p (h d) -> p h d", d=HD),
                                         cf.unsqueeze(2).to_broadcast([P, NH, HD]), ALU.mult))
                if br == 0:
                    dve.wait_ge(co_ev, i + 1)
                o = oa.rearrange("p (g j) d -> p j g d", g=2)
                dve.tensor_tensor(o, o, tmp.rearrange("p (j g) d -> p j g d", g=2), ALU.add).then_inc(o_ev, 1)
                dve.wait_ge(o_ev, 2 * i + br + 1)

            def compressed_soft(i):
                n = 4 * (i + 1)
                x0 = 927 - P * i
                dve.wait_ge(cs_ps, i + 1)
                if i >= 1:
                    dve.wait_ge(t_ps, number["compressed", i - 1] + 1)
                view = pc[:, :, 0:n].rearrange("p (j g) n -> p j g n", g=2)
                linked(dve.tensor_tensor(view, c.bank(7)[:, 0:256].rearrange("p (j g n) -> p j g n", j=4, g=2)[:, :, :, 0:n],
                                         c.bias[:, :, x0:x0 + 32 * (n - 1) + 1:32].rearrange("p (g j) n -> p j g n", g=2), ALU.add))
                linked(dve.tensor_reduce(cm, pc[:, :, 0:n], AX.X, ALU.max))
                linked(dve.tensor_scalar(cm, cm, -1e29, None, ALU.max))
                dve.tensor_tensor(pc[:, :, 0:n], pc[:, :, 0:n], cm.unsqueeze(2).to_broadcast([P, NH, n]), ALU.subtract).then_inc(cs_ev, 1)
                dve.wait_ge(ce_ev, i + 1)
                linked(dve.tensor_reduce(cs, pc[:, :, 0:n], AX.X, ALU.add))
                weighted(cs, cs, i, 0)
                dve.tensor_tensor(pc[:, :, 0:n], pc[:, :, 0:n], cs.unsqueeze(2).to_broadcast([P, NH, n]), ALU.mult).then_inc(cn_ev, 1)

            dve.memset(pc, 0.0).then_inc(zero_set, 1)
            dve.tensor_copy(edge, edge_f).then_inc(edge_set, 1)
            dve.tensor_copy(ident_b, c.ident).then_inc(edge_set, 1)
            dve.wait_ge(zero_set, 1)
            for s in range(NU + 3):
                i, r = s // 16, s % 16
                if 0 <= s - 2 < NU:
                    u = s - 2
                    n = min(4, unit(u)[5])
                    if u >= 2:
                        dve.wait_ge(v_ps, u - 1)
                    turned(("unit", u), pT[u % 2][:, 0:n, :], c.bank(4)[:, 0:n * P].rearrange("p (k q) -> p k q", k=n))
                if s < NU:
                    soft(s)
                    if r == 5:
                        compressed_soft(i)
                    if r == 6 and i >= 1:
                        turned(("result", i - 1), c.mix[:, 4:8, (i - 1) * P:i * P], c.bank(4).rearrange("p (m q) -> p m q", m=4))
                    if r == 8:
                        turned(("compressed", i), pcT, c.bank(4)[:, 0:256].rearrange("p (m q) -> p m q", m=2))
                    if r == 9:
                        dve.wait_ge(co_ps, i + 1)
                        if i >= 1:
                            dve.wait_ge(t_ps, number["result", i - 1] + 1)
                        dve.tensor_copy(oa.rearrange("p (g j) d -> p j g d", g=2),
                                        c.bank(7).rearrange("p (j g d) -> p j g d", j=4, g=2)).then_inc(co_ev, 1)
                if s >= 3 and (s - 3) % 8 == 7:
                    branch_result((s - 3) // 16, (s - 3) % 16 // 8)
            turned(("result", NP_TILES - 1), c.mix[:, 4:8, SEQ - P:SEQ], c.bank(4).rearrange("p (m q) -> p m q", m=4))
            dve.wait_ge(t_dve, len(turns))


def row_broadcast(ap, offset, n, rows=P):
    return bass.AP(tensor=ap.tensor, offset=offset, ap=[[0, rows], [1, n]])


def sample_rows(c, v):
    return bass.AP(tensor=c.mod_d.tensor, offset=6 * D + v * D, ap=[[6 * D, NB], [0, JS], [1, D]])


def block_output(c):
    nc, t, sem = c.nc, c.t, c.sem
    o = W_ + KT * D
    g1, sc2, sh2, lng, lnb, t0, *t2 = (c.view(o + D * n, D) for n in range(8))
    g1s, sc2s, sh2s = (c.view(L_ + D * n, D) for n in range(3))
    st = c.view(o + 8 * D, 24)
    assert o + 8 * D + 24 <= MIX_
    x1 = [c.view(L_ + D * (3 + n), D) for n in range(2)]
    h2T = c.view(L_ + 5 * D, KT, P)
    rw = c.view(L_ + 6 * D, KT, NE)
    wo = [c.wo_parts[:, KT * D * n:KT * D * (n + 1)].rearrange("p (k d) -> p k d", k=KT) for n in range(2)]
    mixed = [[c.mix_parts[:, D * (2 * s + n):D * (2 * s + n + 1)].rearrange("p (k q) -> p k q", k=KT) for n in range(2)]
             for s in range(2)]
    c.logits = c.misc[:, 0:NT * NE].rearrange("p (a b) -> p a b", a=NT)
    c.rb = c.misc[:, NT * NE:NT * NE + NE]
    stats, mv, rstd, nmr = st[:, 0:12], st[:, 12:14], st[:, 16:17], st[:, 20:21]
    vec_in, ln_in, vec2_in, r_in, h2_out, x1_out = (sem(n) for n in ("vec_in", "ln_in", "vec2_in", "r_in", "h2_out", "x1_out"))
    x_in6 = [sem(f"x6_in{i}") for i in range(NT)]
    (o_ps, o_ev, st_ready, sq, nrm, x1_a, x1_ready, h2_ready, t_ps, t_act, t_dve, r_ps, r_ev, link, rs_done) = (
        sem(n) for n in ("oo_ps", "oo_ev", "o_st", "o_sq", "o_nrm", "x1_a", "x1_ready", "h2_ready", "ot_ps", "ot_act",
                         "ot_dve", "r_ps", "r_ev", "o_link", "rs_done"))
    wo_hi, wo_lo, mix_hi, mix_lo = (sem(n) for n in ("wo_hi", "wo_lo", "mix_hi", "mix_lo"))
    smp = NP_TILES

    with nc.Block() as block:
        @block.sync
        def _(sp):
            sp.dma_start(rw, t["router_w"].rearrange("(k p) e -> p k e", p=P)).then_inc(r_in, 16)
            sp.dma_start(c.rb, row_broadcast(t["router_b"], 0, NE)).then_inc(r_in, 16)
            for v, dst in ((2, g1), (4, sc2), (3, sh2)):
                sp.dma_start(dst, row_broadcast(c.mod_d, v * D, D)).then_inc(vec_in, 16)
            def load_x(i):
                T = tile_rows(i)
                src = t["x_prompt"][0, i * P:(i + 1) * P, :] if i < smp else t["x_sample"].rearrange("b j d -> (b j) d")
                sp.dma_start(x1[i % 2][0:T, :], src).then_inc(x_in6[i], 16)

            for i in range(2):
                load_x(i)
                if i == 0:
                    sp.dma_start(lng, row_broadcast(t["ln_g"], 0, D)).then_inc(ln_in, 16)
                    sp.dma_start(lnb, row_broadcast(t["ln_b"], 0, D)).then_inc(ln_in, 16)
            for v, dst in ((2, g1s), (4, sc2s), (3, sh2s)):
                sp.dma_start(dst[0:NS, :], sample_rows(c, v)).then_inc(vec2_in, 16)
            for i in range(NT):
                T = tile_rows(i)
                sp.wait_ge(h2_ready, i + 1)
                sp.dma_start(c.h2_d[i * P:i * P + T, :], t2[i % 2][0:T, :]).then_inc(h2_out, 16)
                sp.dma_start(c.x1_d[i * P:i * P + T, :], x1[i % 2][0:T, :]).then_inc(x1_out, 16)
                if i + 2 < NT:
                    sp.wait_ge(x1_out, 16 * (i + 1))
                    load_x(i + 2)
            sp.wait_ge(h2_out, 16 * NT)
            sp.wait_ge(x1_out, 16 * NT)

        @block.tensor
        def _(pe):
            def project(i):
                T = tile_rows(i)
                if i >= 2:
                    pe.wait_ge(o_ev, i - 1)
                pe.wait_ge(mix_lo, i + 1)
                for k in range(KT):
                    if i == 0:
                        pe.wait_ge(wo_lo, k + 1)
                    for n in range(2):
                        for l, w in ((0, 0), (0, 1), (1, 0)):
                            mm = pe.matmul(c.bank(2 * (i % 2) + n)[0:T, :], mixed[i % 2][l][:, k, 0:T],
                                           wo[w][:, k, n * 512:(n + 1) * 512], start=(k == 0 and l + w == 0),
                                           stop=(k == KT - 1 and l == 1))
                mm.then_inc(o_ps, 1)

            def route(i):
                T = tile_rows(i)
                pe.wait_ge(h2_ready, i + 1)
                if i >= 1:
                    pe.wait_ge(t_act, i)
                    pe.wait_ge(t_dve, i)
                for k in range(KT):
                    mm = pe.transpose(c.bank(4 + k // 4)[:, (k % 4) * P:(k % 4) * P + T], t2[i % 2][0:T, k * P:(k + 1) * P], c.ident[0:T, 0:T])
                mm.then_inc(t_ps, 1)
                if i == 0:
                    pe.wait_ge(r_in, 32)
                pe.wait_ge(t_act, i + 1)
                pe.wait_ge(t_dve, i + 1)
                if i >= 1:
                    pe.wait_ge(r_ev, i)
                for k in range(KT):
                    mm = pe.matmul(c.bank(6)[0:T, 0:NE], h2T[:, k, 0:T], rw[:, k, :], start=(k == 0), stop=(k == KT - 1))
                mm.then_inc(r_ps, 1)

            for i in range(NT + 2):
                if i < NT:
                    project(i)
                if i >= 2:
                    route(i - 2)

        @block.scalar
        def _(act):
            def part(i):
                T = tile_rows(i)
                act.wait_ge(st_ready, i + 1)
                act.activation(rstd[0:T, :], mv[0:T, 1:2], ACT.Sqrt).then_inc(sq, 1)
                act.wait_ge(rs_done, i + 1)
                act.activation(x1[i % 2][0:T, :], t0[0:T, :], ACT.Identity, bias=nmr[0:T, :], scale=rstd[0:T, :]).then_inc(nrm, 1)

            def turned(i):
                T = tile_rows(i)
                act.wait_ge(t_ps, i + 1)
                if i >= 1:
                    act.wait_ge(r_ps, i)
                act.copy(h2T[:, 0:4, 0:T], c.bank(4).rearrange("p (k q) -> p k q", k=4)[:, :, 0:T]).then_inc(t_act, 1)

            def high_parts(i):
                T = tile_rows(i)
                if i >= 2:
                    act.wait_ge(o_ps, i - 1)
                act.copy(mixed[i % 2][0][:, :, 0:T], c.mix[:, :, i * P:i * P + T]).then_inc(mix_hi, 1)

            high_parts(0)
            act.wait_ge(c.w_out_in, 16)
            for k in range(KT):
                act.copy(wo[0][:, k, :], c.w_out[:, k, :]).then_inc(wo_hi, 1)
            high_parts(1)
            for i in range(NT + 2):
                if i >= 2:
                    turned(i - 2)
                if i < NT:
                    part(i)
                if i + 2 < NT:
                    high_parts(i + 2)

        @block.gpsimd
        def _(pool):
            pool.wait_ge(ln_in, 32)
            for i in range(NT):
                T = tile_rows(i)
                pool.wait_ge(nrm, i + 1)
                pool.tensor_tensor(x1[i % 2][0:T, :], x1[i % 2][0:T, :], lng[0:T, :], ALU.mult).then_inc(x1_a, 1)
                pool.wait_ge(x1_a, i + 1)
                pool.tensor_tensor(x1[i % 2][0:T, :], x1[i % 2][0:T, :], lnb[0:T, :], ALU.add).then_inc(x1_ready, 1)
            pool.wait_ge(x1_ready, NT)

        @block.vector
        def _(dve):
            links = [0]

            def linked(ins):
                links[0] += 1
                ins.then_inc(link, 1)
                dve.wait_ge(link, links[0])

            dve.memset(c.logits, 0.0)

            def residual(i):
                T = tile_rows(i)
                if i == smp:
                    dve.wait_ge(vec2_in, 48)
                dve.wait_ge(o_ps, i + 1)
                if i >= 1:
                    dve.wait_ge(nrm, i)
                b = (i % 2) * 1024
                dve.tensor_tensor(t0[0:T, :], c.psum[0:T, b:b + D], (g1 if i < smp else g1s)[0:T, :], ALU.mult).then_inc(o_ev, 1)
                dve.wait_ge(o_ev, i + 1)
                dve.wait_ge(x_in6[i], 16)
                linked(dve.scalar_tensor_tensor(out=t0[0:T, :], in0=x1[i % 2][0:T, :], scalar=ALPHA, in1=t0[0:T, :],
                                                op0=ALU.mult, op1=ALU.add))
                for n in range(2):
                    a = dve.bn_stats(stats[0:T, 6 * n:6 * n + 6], t0[0:T, 512 * n:512 * n + 512])
                linked(a)
                linked(dve.bn_aggr(mv[0:T, :], stats[0:T, :]))
                dve.tensor_scalar(mv[0:T, 1:2], mv[0:T, 1:2], EPS, None, ALU.add).then_inc(st_ready, 1)
                dve.wait_ge(sq, i + 1)
                linked(dve.reciprocal(rstd[0:T, :], rstd[0:T, :]))
                dve.scalar_tensor_tensor(out=nmr[0:T, :], in0=mv[0:T, 0:1], scalar=-1.0, in1=rstd[0:T, :],
                                         op0=ALU.mult, op1=ALU.mult).then_inc(rs_done, 1)

            def modulate(i):
                T = tile_rows(i)
                dve.wait_ge(x1_ready, i + 1)
                if i >= 2:
                    dve.wait_ge(h2_out, 16 * (i - 1))
                    dve.wait_ge(t_ps, i - 1)
                linked(dve.tensor_tensor(t2[i % 2][0:T, :], x1[i % 2][0:T, :], (sc2 if i < smp else sc2s)[0:T, :], ALU.mult))
                dve.tensor_tensor(t2[i % 2][0:T, :], t2[i % 2][0:T, :], (sh2 if i < smp else sh2s)[0:T, :], ALU.add).then_inc(h2_ready, 1)

            def turned(i):
                T = tile_rows(i)
                dve.wait_ge(t_ps, i + 1)
                if i >= 1:
                    dve.wait_ge(r_ps, i)
                dve.tensor_copy(h2T[:, 4:8, 0:T], c.bank(5).rearrange("p (k q) -> p k q", k=4)[:, :, 0:T]).then_inc(t_dve, 1)

            def logits(i):
                T = tile_rows(i)
                dve.wait_ge(r_ps, i + 1)
                dve.tensor_copy(c.logits[0:T, i, :], c.bank(6)[0:T, 0:NE]).then_inc(r_ev, 1)

            def low_parts(i):
                T = tile_rows(i)
                dve.wait_ge(mix_hi, i + 1)
                dve.tensor_tensor(mixed[i % 2][1][:, :, 0:T], c.mix[:, :, i * P:i * P + T],
                                  mixed[i % 2][0][:, :, 0:T].bitcast(F32), ALU.subtract).then_inc(mix_lo, 1)

            low_parts(0)
            for k in range(KT):
                dve.wait_ge(wo_hi, k + 1)
                dve.tensor_tensor(wo[1][:, k, :], c.w_out[:, k, :], wo[0][:, k, :].bitcast(F32), ALU.subtract).then_inc(wo_lo, 1)
            low_parts(1)
            dve.wait_ge(vec_in, 48)
            for i in range(NT + 2):
                if i >= 2:
                    turned(i - 2)
                if i < NT:
                    residual(i)
                if i >= 2:
                    logits(i - 2)
                if i + 2 < NT:
                    low_parts(i + 2)
                if i < NT:
                    modulate(i)
            dve.wait_ge(r_ev, NT)


def block_routing(c):
    nc, t, sem = c.nc, c.t, c.sem
    off = [0]

    def new(*dims):
        n = 1
        for d in dims:
            n *= d
        v = c.scratch[:, off[0]:off[0] + n]
        off[0] += n
        return v if len(dims) == 1 else v.rearrange("p (a b) -> p a b", a=dims[0])

    strict, key16, key4, limits, before, slot_n, tok_id, place_n = (
        new(*d) for d in ((P,), (NE,), (4,), (8,), (NE, NE), (MAX_SLOTS + 1,), (NT,), (P,)))
    consts = c.scratch[:, 0:off[0]]
    s, grp, y, y2, tmp, oh1, oh2, m, dest = (new(NT, NE) for _ in range(9))
    a4, b4, c4, d4, m1g, e4, f4, m2g, gs, gk, gsel, pen = (new(NT, 4) for _ in range(12))
    r1, r2, w1, w2, ws = (new(NT) for _ in range(5))
    pref, tot = new(NT + 1, NE), new(NT, NE)
    ones, over, nb, starts, tri = new(P), new(NE, 8), new(NE), new(NE), new(NE, NE)
    table, exps, ends = new(MAX_SLOTS, NE), new(MAX_SLOTS), new(NE + 1)
    dests, slot_f, place_f = (new(NT, 2) for _ in range(3))
    one_place, one_slot = new(2 * NT, P), new(2 * NT, MAX_SLOTS + 1)
    assert off[0] <= 9216
    sg, cnt_ready, cnt_ps, dest_ready, ids_ps, tab_ready, link = (
        sem(n) for n in ("sig_ready", "cnt_ready", "cnt_ps", "dest_ready", "ids_ps", "tab_ready", "r_link"))

    with nc.Block() as block:
        @block.sync
        def _(sp):
            sp.dma_start(consts, t["cph4"]).then_inc(c.cph_in, 16)
            load_expert(c, sp, 0)

        @block.scalar
        def _(act):
            act.activation(s, c.logits, ACT.Sigmoid).then_inc(sg, 1)

        @block.vector
        def _(dve):
            links = [0]

            def linked(ins):
                links[0] += 1
                ins.then_inc(link, 1)
                dve.wait_ge(link, links[0])

            def tt(out, a, b, op):
                linked(dve.tensor_tensor(out, a, b, op))

            def over_last(a, n):
                return a.unsqueeze(len(a.shape)).to_broadcast(list(a.shape) + [n])

            def first_max(out, val, key, red, n):
                linked(dve.tensor_reduce(red, val, AX.X, ALU.max))
                tt(out, val, over_last(red, n), ALU.is_equal)
                tt(out, out, key.unsqueeze(1).to_broadcast([P, NT, n]), ALU.mult)
                linked(dve.tensor_reduce(red, out, AX.X, ALU.max))
                tt(out, out, over_last(red, n), ALU.is_equal)

            linked(dve.memset(ones, 1.0))
            linked(dve.memset(m, 0.0))
            linked(dve.memset(pref, 0.0))
            dve.wait_ge(sg, 1)
            dve.wait_ge(c.cph_in, 48)
            tt(grp, s, c.rb.unsqueeze(1).to_broadcast([P, NT, NE]), ALU.add)
            x = grp.rearrange("p i (g e) -> p i g e", g=4)
            tt(a4, x[:, :, :, 0], x[:, :, :, 1], ALU.max)
            tt(b4, x[:, :, :, 0], x[:, :, :, 1], ALU.min)
            tt(c4, x[:, :, :, 2], x[:, :, :, 3], ALU.max)
            tt(d4, x[:, :, :, 2], x[:, :, :, 3], ALU.min)
            tt(m1g, a4, c4, ALU.max)
            tt(e4, a4, c4, ALU.min)
            tt(f4, b4, d4, ALU.max)
            tt(m2g, e4, f4, ALU.max)
            tt(gs, m1g, m2g, ALU.add)
            first_max(gsel, gs, key4, r1, 4)
            linked(dve.tensor_scalar(pen, gsel, -1.0, BIG, ALU.add, ALU.mult))
            tt(y.rearrange("p i (g e) -> p i g e", g=4), x, over_last(pen, 4), ALU.add)
            first_max(oh1, y, key16, r1, NE)
            linked(dve.scalar_tensor_tensor(out=y2.rearrange("p i e -> p (i e)"), in0=oh1.rearrange("p i e -> p (i e)"), scalar=-BIG,
                                            in1=y.rearrange("p i e -> p (i e)"), op0=ALU.mult, op1=ALU.add))
            first_max(oh2, y2, key16, r2, NE)
            tt(m[:, 0:NP_TILES], oh1[:, 0:NP_TILES], oh2[:, 0:NP_TILES], ALU.add)
            dve.tensor_tensor(m[0:NS, NP_TILES], oh1[0:NS, NP_TILES], oh2[0:NS, NP_TILES], ALU.add).then_inc(cnt_ready, 1)
            for w, oh in ((w1, oh1), (w2, oh2)):
                tt(tmp, s, oh, ALU.mult)
                linked(dve.tensor_reduce(w, tmp, AX.X, ALU.add))
            tt(ws, w1, w2, ALU.add)
            linked(dve.reciprocal(ws, ws))
            tt(c.xw[:, :, 0], w1, ws, ALU.mult)
            tt(c.xw[:, :, 1], w2, ws, ALU.mult)
            dve.wait_ge(cnt_ps, 1)
            linked(dve.tensor_copy(tot, c.bank(1)[:, 0:NT * NE].rearrange("p (i e) -> p i e", i=NT)))
            for i in range(NT):
                tt(pref[:, i + 1], pref[:, i], tot[:, i], ALU.add)
            tt(over, over_last(pref[:, NT], 8), limits.unsqueeze(1).to_broadcast([P, NE, 8]), ALU.is_gt)
            linked(dve.tensor_reduce(nb, over, AX.X, ALU.add))
            linked(dve.tensor_scalar(nb, nb, 1.0, None, ALU.add))
            tt(tri, before, nb.unsqueeze(1).to_broadcast([P, NE, NE]), ALU.mult)
            linked(dve.tensor_reduce(starts, tri, AX.X, ALU.add))
            tt(dest, c.bank(0)[:, 0:NT * NE].rearrange("p (i e) -> p i e", i=NT), pref[:, 0:NT], ALU.add)
            linked(dve.tensor_scalar(y[:, 0], starts, float(MB), None, ALU.mult))
            tt(dest, dest, y[:, 0].unsqueeze(1).to_broadcast([P, NT, NE]), ALU.add)
            for k, oh in enumerate((oh1, oh2)):
                tt(tmp, dest, oh, ALU.mult)
                linked(dve.tensor_reduce(dests[:, :, k], tmp, AX.X, ALU.add))
            linked(dve.tensor_copy(c.dest_i[:, :, :], dests))
            linked(dve.tensor_scalar(c.dest_y[:, :, :], c.dest_i[:, :, :], 7, None, ALU.arith_shift_right))
            linked(dve.tensor_copy(slot_f, c.dest_y[:, :, :]))
            linked(dve.scalar_tensor_tensor(out=place_f, in0=slot_f, scalar=-float(MB), in1=dests, op0=ALU.mult, op1=ALU.add))
            for i in range(NT):
                T = tile_rows(i)
                for k in range(2):
                    dve.tensor_scalar(one_place[0:T, 2 * i + k], place_n[0:T], place_f[0:T, i, k:k + 1], None, ALU.is_equal)
                    ins = dve.tensor_scalar(one_slot[0:T, 2 * i + k], slot_n[0:T], slot_f[0:T, i, k:k + 1],
                                            tok_id[0:T, i:i + 1], ALU.is_equal, ALU.mult)
            ins.then_inc(dest_ready, 1)
            linked(dve.tensor_scalar(dests, dests, float(MB), None, ALU.add))
            linked(dve.tensor_copy(c.dest_y[:, :, :], dests))
            tt(table[0:1], starts[0:1].unsqueeze(1).to_broadcast([1, MAX_SLOTS, NE]), over_last(slot_n[0:1, 0:MAX_SLOTS], NE), ALU.is_le)
            linked(dve.tensor_reduce(exps[0:1], table[0:1], AX.X, ALU.add))
            linked(dve.tensor_scalar(exps[0:1], exps[0:1], -1.0, None, ALU.add))
            linked(dve.tensor_copy(c.slot_e[:, :], exps[0:1]))
            linked(dve.tensor_copy(ends[0:1, 0:NE], starts[0:1]))
            tt(ends[0:1, NE:NE + 1], starts[0:1, NE - 1:NE], nb[0:1, NE - 1:NE], ALU.add)
            dve.tensor_copy(c.start_e[:, :], ends[0:1]).then_inc(tab_ready, 1)
            dve.wait_ge(ids_ps, 1)
            dve.tensor_copy(c.ids_i[:, :], c.bank(2)[:, 0:MAX_SLOTS + 1]).then_inc(tab_ready, 1)
            dve.wait_ge(tab_ready, 2)

        @block.tensor
        def _(pe):
            pe.wait_ge(cnt_ready, 1)
            flat = m.rearrange("p i e -> p (i e)")
            pe.matmul(c.bank(0)[:, 0:NT * NE], strict, flat, start=True, stop=True)
            pe.matmul(c.bank(1)[:, 0:NT * NE], ones, flat, start=True, stop=True).then_inc(cnt_ps, 1)
            pe.wait_ge(dest_ready, 1)
            for n in range(2 * NT):
                T = tile_rows(n // 2)
                mm = pe.matmul(c.bank(2)[:, 0:MAX_SLOTS + 1], one_place[0:T, n], one_slot[0:T, n], start=n == 0, stop=n == 2 * NT - 1)
            mm.then_inc(ids_ps, 1)


PARTS = ((0, KT, DE), (1, KT, DE), (2, DE // P, D))


def load_expert(c, sp, e):
    for (p, nk, n), name in zip(PARTS, ("moe_w_gate", "moe_w_up", "moe_w_down")):
        if not isinstance(e, int):
            sp.wait_ge(c.lo_done[p], e * 2)
            sp.sem_inc(c.reloads, 1)
        src = c.t[name][0, e].rearrange("(k p) f -> p k f", p=P) if isinstance(e, int) else \
            c.t[name][0, bass.ds(e, 1)].rearrange("a (k p) f -> p (a k) f", p=P)
        dst = c.raw[:, PART * p:PART * (p + 1)].rearrange("p (k f) -> p k f", k=nk)
        sp.dma_start(dst, src).then_inc(c.raw_in[p], 16)


def block_experts(c):
    nc, t, sem = c.nc, c.t, c.sem
    xb, y = c.work[:, 0:D], c.work[:, D:2 * D]
    sg, a = c.work[:, 2 * D:2 * D + DE], c.work[:, 2 * D + DE:]
    xT = [c.x_parts[:, D * i:D * (i + 1)] for i in range(2)]
    aT = [c.a_parts[:, DE * i:DE * (i + 1)] for i in range(2)]
    (xb_in, x_ps, x_hi, x_lo, gate_done, up_done, down_done, sil, a_ready, a_ps, a_hi, a_lo, y_act, y_dve, y_out, id_set,
     fetches, fill_out, filled) = (
        sem(n) for n in ("xb_in", "x8_ps", "x8_hi", "x8_lo", "gate8_done", "up8_done", "down8_done", "silu8", "a_ready",
                         "a_ps", "a_hi", "a_lo", "y_act", "y_dve", "y_out", "id_set", "fetches", "fill_out", "filled"))
    hi_done = [sem(f"hi_done{p}") for p in range(3)]
    used = (gate_done, up_done, down_done)

    def slots(eng):
        return eng.value_load(c.start_e[0:1, NE:NE + 1], min_val=NE, max_val=MAX_SLOTS)

    def place(p, e_odd):
        return PART * (p + (e_odd if p == 2 else 0))

    def expert_loop(eng, slot, split):
        def nothing(p):
            pass

        def section(e, odd, last):
            begin = eng.value_load(c.start_e[0:1, e:e + 1] if isinstance(e, int) else c.start_e[0:1, bass.ds(e, 1)],
                                   min_val=0, max_val=MAX_SLOTS)
            end = eng.value_load(c.start_e[0:1, e + 1:e + 2] if isinstance(e, int) else c.start_e[0:1, bass.ds(e + 1, 1)],
                                 min_val=1, max_val=MAX_SLOTS)
            if last:
                with eng.Fori(begin, end) as s:
                    slot(s, nothing)
            else:
                with eng.If(begin < end - 1):
                    with eng.Fori(begin, end - 1) as s:
                        slot(s, nothing)
                slot(end - 1, lambda p: split(p, e + 1, 1 - odd, end))

        for p in range(3):
            split(p, 0, 0, None)
            if p == 0:
                slot(None, None)
        with eng.Fori(0, NE // 2 - 1) as pair:
            section(pair * 2, 0, False)
            section(pair * 2 + 1, 1, False)
        section(NE - 2, 0, False)
        section(NE - 1, 1, True)

    with nc.Block() as block:
        @block.sync
        def _(sp):
            with sp.Fori(1, NE) as e:
                load_expert(c, sp, e)
            with sp.Fori(0, slots(sp)):
                sp.sem_inc(fill_out, 16)
            with sp.Fori(slots(sp), MAX_SLOTS + 1) as n:
                sp.dma_start(c.y_d[bass.ds(n * MB + MB, MB), :].rearrange("p (a b) -> p a b", b=P),
                             c.ident.unsqueeze(1).to_broadcast([P, KT, P])).then_inc(fill_out, 16)
                sp.wait_ge(fill_out, n * 16 + 16)
                sp.sem_inc(filled, 1)

        @block.gpsimd
        def _(pool):
            def fetch(s, first):
                ins = pool.tensor_copy(c.id_now[:, :], c.ids_i[:, 0:1] if first else c.ids_i[:, bass.ds(s, 1)])
                ins.then_inc(id_set, 1)
                pool.wait_ge(id_set, s + 1)
                pool.sem_inc(fetches, 1)
                pool.indirect_dma_start(xb, None, c.h2_d, bass.IndirectOffsetOnAxis(ap=c.id_now[:, 0:1], axis=0)).then_inc(xb_in, 16)

            fetch(0, True)
            with pool.Fori(1, slots(pool) + 1) as s:
                pool.wait_ge(x_ps, s)
                fetch(s, False)
            pool.wait_ge(xb_in, slots(pool) * 16 + 16)

        @block.tensor
        def _(pe):
            def turn_x(s):
                pe.wait_ge(xb_in, s * 16 + 16)
                for k in range(KT):
                    mm = pe.transpose(c.bank(4 + k // 4)[:, (k % 4) * P:(k % 4 + 1) * P], xb[:, k * P:(k + 1) * P], c.ident)
                mm.then_inc(x_ps, 1)

            def short_products(out, left, at, nk, step):
                steps = [(k, l, w) for k in range(nk) for l, w in ((0, c.w_hi), (0, c.w_lo), (1, c.w_hi))]
                for n, (k, l, w) in enumerate(steps):
                    mm = pe.matmul(out, left[l][:, k * P:(k + 1) * P], w[:, bass.ds(at + k * step, 512)],
                                   start=n == 0, stop=n == len(steps) - 1)
                return mm

            def product(p, e):
                pe.wait_ge(c.lo_done[p], e * 2 + 2)
                short_products(c.bank(p), xT, place(p, 0), KT, DE).then_inc(used[p], 1)

            def turn_a(n):
                pe.wait_ge(a_ready, n + 2)
                for f in range(4):
                    mm = pe.transpose(c.bank(6)[:, f * P:(f + 1) * P], a[:, f * P:(f + 1) * P], c.ident)
                mm.then_inc(a_ps, 1)

            def down(n, e):
                pe.wait_ge(a_lo, n + 3)
                pe.wait_ge(c.lo_done[2], e * 2 + 2)
                pe.wait_ge(y_act, n + 1)
                pe.wait_ge(y_dve, n + 1)
                at = e % 2 * PART + place(2, 0)
                for m in range(2):
                    mm = short_products(c.bank(2 + m), aT, at + 512 * m, 4, D)
                mm.then_inc(down_done, 1)

            turn_x(0)
            for f in range(4):
                mm = pe.transpose(c.bank(6)[:, f * P:(f + 1) * P], c.ident, c.ident)
            mm.then_inc(a_ps, 1)
            for f in range(8):
                mm = pe.transpose(c.bank(2 + f // 4)[:, f % 4 * P:(f % 4 + 1) * P], c.ident, c.ident)
            mm.then_inc(down_done, 1)
            pe.wait_ge(x_lo, 1)
            zero = pe.value_load(c.slot_e[0:1, 0:1], min_val=0, max_val=NE - 1)
            product(0, zero)
            product(1, zero)
            turn_x(1)
            with pe.Fori(1, slots(pe)) as s:
                e = pe.value_load(c.slot_e[0:1, bass.ds(s, 1)], min_val=0, max_val=NE - 1)
                e_last = pe.value_load(c.slot_e[0:1, bass.ds(s - 1, 1)], min_val=0, max_val=NE - 1)
                pe.wait_ge(x_lo, s + 1)
                pe.wait_ge(sil, s)
                product(0, e)
                turn_a(s - 1)
                product(1, e)
                turn_x(s + 1)
                down(s - 1, e_last)
            n = slots(pe)
            turn_a(n - 1)
            down(n - 1, pe.value_load(c.slot_e[0:1, bass.ds(n - 1, 1)], min_val=0, max_val=NE - 1))

        @block.scalar
        def _(act):
            def split(p, e, odd, begun):
                act.wait_ge(c.raw_in[p], e * 16 + 16)
                if begun is not None and p < 2:
                    act.wait_ge(used[p], begun)
                for h in range(2):
                    o, at = PART * p + h * PART // 2, place(p, odd) + h * PART // 2
                    act.copy(c.w_hi[:, at:at + PART // 2], c.raw[:, o:o + PART // 2]).then_inc(hi_done[p], 1)

            def x_part(s):
                act.wait_ge(x_ps, s + 1)
                for h in range(2):
                    ins = act.copy(xT[0][:, 512 * h:512 * h + 512], c.bank(4 + h))
                ins.then_inc(x_hi, 1)

            def aT_part(s):
                act.wait_ge(a_ps, s + 1)
                act.wait_ge(a_hi, s + 1)
                act.copy(aT[0], c.bank(6)).then_inc(a_hi, 1)

            def y_part(s):
                act.wait_ge(down_done, s + 1)
                act.wait_ge(y_out, s * 16 + 16)
                act.copy(y[:, 0:512], c.bank(2)).then_inc(y_act, 1)
                act.wait_ge(y_act, s + 1)
                act.wait_ge(y_dve, s + 1)
                act.dma_start(c.y_d[bass.ds(s * MB, MB), :], y).then_inc(y_out, 16)

            def slot(s, among):
                if s is None:
                    x_part(0)
                    return
                act.wait_ge(gate_done, s + 1)
                act.wait_ge(a_ready, s + 1)
                act.activation(sg, c.bank(0), ACT.Silu).then_inc(sil, 1)
                aT_part(s)
                among(0)
                act.wait_ge(up_done, s + 1)
                x_part(s + 1)
                among(1)
                y_part(s)
                among(2)

            act.sem_inc(y_out, 16)
            act.sem_inc(a_hi, 1)
            expert_loop(act, slot, split)
            n = slots(act)
            aT_part(n)
            y_part(n)
            act.wait_ge(y_out, n * 16 + 32)
            act.sem_inc(fetches, 1)

        @block.vector
        def _(dve):
            def split(p, e, odd, begun):
                for h in range(2):
                    dve.wait_ge(hi_done[p], e * 2 + 1 + h)
                    o, at = PART * p + h * PART // 2, place(p, odd) + h * PART // 2
                    dve.tensor_tensor(c.w_lo[:, at:at + PART // 2], c.raw[:, o:o + PART // 2],
                                      c.w_hi[:, at:at + PART // 2].bitcast(F32), ALU.subtract).then_inc(c.lo_done[p], 1)

            def x_part(s):
                dve.wait_ge(x_hi, s + 1)
                for h in range(2):
                    cols = slice(512 * h, 512 * h + 512)
                    ins = dve.tensor_tensor(xT[1][:, cols], c.bank(4 + h), xT[0][:, cols].bitcast(F32), ALU.subtract)
                ins.then_inc(x_lo, 1)

            def aT_part(s):
                dve.wait_ge(a_hi, s + 2)
                dve.wait_ge(a_lo, s + 1)
                dve.tensor_tensor(aT[1], c.bank(6), aT[0].bitcast(F32), ALU.subtract).then_inc(a_lo, 1)

            def y_part(s):
                dve.wait_ge(down_done, s + 1)
                dve.wait_ge(y_out, s * 16 + 16)
                dve.tensor_copy(y[:, 512:], c.bank(3)).then_inc(y_dve, 1)

            def slot(s, among):
                if s is None:
                    x_part(0)
                    return
                aT_part(s)
                among(0)
                dve.wait_ge(sil, s + 1)
                dve.wait_ge(up_done, s + 1)
                dve.tensor_tensor(a, c.bank(1), sg, ALU.mult).then_inc(a_ready, 1)
                x_part(s + 1)
                among(1)
                y_part(s)
                among(2)

            dve.sem_inc(a_ready, 1)
            dve.sem_inc(a_lo, 1)
            expert_loop(dve, slot, split)
            n = slots(dve)
            aT_part(n)
            y_part(n)


def block_combine(c):
    nc, t, sem = c.nc, c.t, c.sem
    RY = 5
    yy = [[c.view(W_ + 2 * D * s + D * k, D) for k in range(2)] for s in range(RY)]
    acc = [c.view(W_ + 2 * RY * D + D * s, D) for s in range(2)]
    nrm = [c.view(W_ + (2 * RY + 2) * D + D * s, D) for s in range(3)]
    o = W_ + (2 * RY + 5) * D
    g2, g2s, lng2, lnb2 = (c.view(o + D * n, D) for n in range(4))
    assert o + 4 * D <= X1_
    x1 = c.view(X1_, NT, D)
    v_in = sem("v9_in")
    x1_in = [sem(f"x9_in{i}") for i in range(NT)]
    st = c.view(S1_, 48)
    diag = c.view(S1_ + 48, NT, 2, P)
    y_in = [sem(f"y9_in{s}") for s in range(RY)]
    done = [sem(f"y9_out{s}") for s in range(3)]
    b_done, d_done, y_sum, g2_done, a_done, st_ready, sq, rs_done, n_done, g_done, link = (
        sem(n) for n in ("b9_done", "d9_done", "y9_sum", "g29_done", "a9_done", "s9_ready", "s9_sq", "s9_rs", "n9_done", "g9_done", "l9"))
    smp = NP_TILES

    with nc.Block() as block:
        @block.tensor
        def _(pe):
            for i in range(NT):
                T = tile_rows(i)
                pe.wait_ge(d_done, i + 1)
                pe.wait_ge(y_in[i % RY], 32 * (i // RY + 1))
                if i >= 4:
                    pe.wait_ge(g2_done, i - 3)
                for n in range(2):
                    for k in range(2):
                        mm = pe.matmul(c.bank(2 * (i % 4) + n)[0:T, :], diag[0:T, i, k, 0:T],
                                       yy[i % RY][k][0:T, 512 * n:512 * n + 512], start=(k == 0), stop=(k == 1))
                mm.then_inc(y_sum, 1)

        @block.gpsimd
        def _(pool):
            def fetch(i):
                T = tile_rows(i)
                if i >= RY:
                    pool.wait_ge(y_sum, i - RY + 1)
                for k in range(2):
                    pool.indirect_dma_start(yy[i % RY][k][0:T, :], None, c.y_d,
                                            bass.IndirectOffsetOnAxis(ap=c.dest_y[0:T, i, k:k + 1], axis=0)).then_inc(y_in[i % RY], 16)

            for i in range(RY):
                fetch(i)
            for i in range(NT):
                T = tile_rows(i)
                out = nrm[i % 3][0:T, :]
                pool.wait_ge(n_done, i + 1)
                if i == 0:
                    pool.wait_ge(v_in, 64)
                pool.tensor_tensor(out, out, lng2[0:T, :], ALU.mult).then_inc(g_done, 1)
                if i + RY < NT:
                    fetch(i + RY)

        @block.scalar
        def _(act):
            for i in range(NT):
                T = tile_rows(i)
                for k in range(2):
                    a = act.activation(diag[0:T, i, k, :], c.ident[0:T, :], ACT.Identity, scale=c.xw[0:T, i, k:k + 1])
                a.then_inc(d_done, 1)
            for i in range(NT):
                T = tile_rows(i)
                q = st[:, 24 * (i % 2):24 * (i % 2) + 24]
                act.wait_ge(st_ready, i + 1)
                act.activation(q[0:T, 16:17], q[0:T, 13:14], ACT.Sqrt).then_inc(sq, 1)
                act.wait_ge(rs_done, i + 1)
                if i >= 3:
                    act.wait_ge(done[i % 3], 16 * (i // 3))
                act.activation(nrm[i % 3][0:T, :], acc[i % 2][0:T, :], ACT.Identity, bias=q[0:T, 20:21],
                               scale=q[0:T, 16:17]).then_inc(n_done, 1)

        @block.vector
        def _(dve):
            links = [0]

            def linked(ins):
                links[0] += 1
                ins.then_inc(link, 1)
                dve.wait_ge(link, links[0])

            def residual(i):
                T = tile_rows(i)
                ac = acc[i % 2][0:T, :]
                dve.wait_ge(y_sum, i + 1)
                if i >= 2:
                    dve.wait_ge(n_done, i - 1)
                dve.tensor_tensor(ac, c.psum[0:T, D * (i % 4):D * (i % 4) + D], (g2 if i < smp else g2s)[0:T, :],
                                  ALU.mult).then_inc(g2_done, 1)
                dve.wait_ge(g2_done, i + 1)
                dve.wait_ge(x1_in[i], 16)
                linked(dve.scalar_tensor_tensor(out=ac, in0=x1[0:T, i, :], scalar=ALPHA, in1=ac, op0=ALU.mult, op1=ALU.add))

            def statistics(i):
                T = tile_rows(i)
                ac = acc[i % 2][0:T, :]
                q = st[0:T, 24 * (i % 2):24 * (i % 2) + 24]
                for n in range(2):
                    a = dve.bn_stats(q[:, 6 * n:6 * n + 6], ac[:, 512 * n:512 * n + 512])
                linked(a)
                linked(dve.bn_aggr(q[:, 12:14], q[:, 0:12]))
                dve.tensor_scalar(q[:, 13:14], q[:, 13:14], EPS, None, ALU.add).then_inc(st_ready, 1)

            def roots(i):
                T = tile_rows(i)
                q = st[0:T, 24 * (i % 2):24 * (i % 2) + 24]
                dve.wait_ge(sq, i + 1)
                linked(dve.reciprocal(q[:, 16:17], q[:, 16:17]))
                dve.scalar_tensor_tensor(out=q[:, 20:21], in0=q[:, 12:13], scalar=-1.0, in1=q[:, 16:17],
                                         op0=ALU.mult, op1=ALU.mult).then_inc(rs_done, 1)

            def bias_add(i):
                T = tile_rows(i)
                out = nrm[i % 3][0:T, :]
                dve.wait_ge(g_done, i + 1)
                dve.tensor_tensor(out, out, lnb2[0:T, :], ALU.add).then_inc(b_done, 1)

            dve.wait_ge(v_in, 64)
            for i in range(NT):
                residual(i)
                if i >= 1:
                    roots(i - 1)
                statistics(i)
                if i >= 2:
                    bias_add(i - 2)
            roots(smp)
            bias_add(smp - 1)
            bias_add(smp)

        @block.sync
        def _(sp):
            for dst, src in ((g2, row_broadcast(c.mod_d, 5 * D, D)), (g2s[0:NS, :], sample_rows(c, 5)),
                             (lng2, row_broadcast(t["ln_g"], D, D)), (lnb2, row_broadcast(t["ln_b"], D, D))):
                sp.dma_start(dst, src).then_inc(v_in, 16)
            for i in range(NT):
                T = tile_rows(i)
                sp.dma_start(x1[0:T, i, :], c.x1_d[i * P:i * P + T, :]).then_inc(x1_in[i], 16)
            for i in range(NT):
                T = tile_rows(i)
                sp.wait_ge(b_done, i + 1)
                dst = t["o_y_p"][0, i * P:(i + 1) * P, :] if i < smp else t["o_y_s"].rearrange("b j d -> (b j) d")
                sp.dma_start(dst, nrm[i % 3][0:T, :]).then_inc(done[i % 3], 16)
            sp.wait_ge(c.out_done, c.out_total)
            for s in range(3):
                sp.wait_ge(done[s], 16 * ((NT - s + 2) // 3))


BLOCKS = (block_modulation, block_projection, block_compression, block_decode_attention,
          retire_early_semaphores, block_prompt_attention, memory_output, block_output, memory_routing, block_routing,
          memory_experts, block_experts, memory_combine, block_combine)


CONST_INPUTS = ("ident", "onehot", "cph1", "cph2", "cph3", "cph4")
INPUTS = ("x_prompt", "x_sample", "cache_cmp_kv", "cache_sel_kv", "state_win_kv", "state_pool", "page_table",
          "c_prompt", "c_sample", "w_in", "w_out", "pool_w", "pool_scale", "sgu_ln_g", "sgu_ln_b", "sgu_w", "sgu_b",
          "cmp_pe", "cmp_w1", "cmp_w2", "rel_bias", "w_mod", "b_mod", "ln_g", "ln_b", "router_w", "router_b",
          "moe_w_gate", "moe_w_up", "moe_w_down")
OUTPUTS = (("o_y_p", (1, SEQ, D)), ("o_y_s", (NB, JS, D)),
           ("o_cmp_p", (1, 1, SEQ, 2, NKV, HD)), ("o_cmp_s", (1, NB, JS, 2, NKV, HD)),
           ("o_sel_p", (1, 1, SEQ, 2, NKV, HD)), ("o_sel_s", (1, NB, JS, 2, NKV, HD)),
           ("o_win_p", (1, 1, 512, 2, NKV, HD)), ("o_win_s", (1, NB, PAST, 2, NKV, HD)),
           ("o_pool_p", (1, 1, PBUF, PW)), ("o_pool_s", (1, NB, PBUF, PW)), ("o_sgu_s", (1, NB, JS, PW)))


def build_program(nc, t):
    with ExitStack() as ctx:
        c = setup(nc, ctx, t)
        for part in BLOCKS:
            part(c)
        while c.stacks:
            c.stacks.pop().close()


def kernel(**inputs):
    import concourse.bacc as bacc
    from concourse.bass_utils import run_bass_kernel_spmd

    nc = bacc.Bacc("TRN2", target_bir_lowering=False, num_devices=1)
    arrays, t = {}, {}
    made = constants()
    for name in INPUTS + CONST_INPUTS:
        a = np.ascontiguousarray(made[name] if name in made else inputs[name])
        arrays[f"in_{name}"] = a
        t[name] = nc.dram_tensor(f"in_{name}", a.shape, mybir.dt.from_np(a.dtype), kind="ExternalInput").ap()
    for name, shape in OUTPUTS:
        t[name] = nc.dram_tensor(f"out_{name}", shape, F32, kind="ExternalOutput").ap()
    build_program(nc, t)
    r = run_bass_kernel_spmd(nc, [arrays], core_ids=[0])
    return tuple(r.results[0][f"out_{name}"] for name, _ in OUTPUTS)
```
